# Optimizing a Trainium2 kernel written in Bass

```python
import jax, jax.numpy as jnp
from jax import lax
import numpy as np

D_MODEL = 1024
BATCH = 1
SEQ = 1024
DEPTH = 2
DEC_BATCH = 8
DEC_SEQ = 1
PAST_LEN = 8192
PAGE_SIZE = 128

N_META = 16
CHUNK = 64
N_MIXERS = 2
N_GLA_LAYERS = (DEPTH + 1) // 2
N_SSD_LAYERS = DEPTH // 2
NORM_EPS = 1e-6

GLA_HEADS = 4
GLA_DK = D_MODEL // 2
GLA_DV = D_MODEL
GLA_HK = GLA_DK // GLA_HEADS
GLA_HV = GLA_DV // GLA_HEADS
GLA_RANK = 16
GLA_TAU = 16.0
GLA_IN = 2 * GLA_DK + 2 * GLA_DV + GLA_RANK

SSD_EXPAND = 2
SSD_DINNER = SSD_EXPAND * D_MODEL
SSD_HEADDIM = 64
SSD_HEADS = SSD_DINNER // SSD_HEADDIM
SSD_GROUPS = 4
SSD_HPG = SSD_HEADS // SSD_GROUPS
SSD_STATE = 128
SSD_CONV = 4
SSD_CONV_DIM = SSD_DINNER + 2 * SSD_GROUPS * SSD_STATE
SSD_IN = SSD_DINNER + SSD_CONV_DIM + SSD_HEADS

kernel_name = "hybrid_gla_ssd_meta_decoder_step"

def rmsnorm(x, w):
    xf = x.astype(jnp.float32)
    y = xf * lax.rsqrt(jnp.mean(xf * xf, axis=-1, keepdims=True) + NORM_EPS)
    return (y * w.astype(jnp.float32)).astype(x.dtype)

def chunked_scan(step, state, xs, chunk):
    b, l = xs[0].shape[:2]
    n = l // chunk
    xs_c = tuple(jnp.moveaxis(a.reshape((b, n, chunk) + a.shape[2:]), 1, 0) for a in xs)
    state, ys = lax.scan(step, state, xs_c)
    ys = jnp.moveaxis(ys, 0, 1).reshape((b, l) + ys.shape[3:])
    return state, ys

def segmented_scan(step, state, xs, seg_lens):
    outs = []
    start = 0
    for seg in seg_lens:
        part = tuple(a[:, start:start + seg] for a in xs)
        chunk = CHUNK if seg % CHUNK == 0 else seg
        state, y = chunked_scan(step, state, part, chunk)
        outs.append(y)
        start += seg
    return state, jnp.concatenate(outs, axis=1)

def gla_chunk_step(S, inp):
    q, k, v, g = inp
    c = q.shape[1]
    bcum = jnp.cumsum(g, axis=1)
    causal = jnp.tril(jnp.ones((c, c), dtype=bool))[None, :, :, None, None]
    decay = jnp.exp(jnp.where(causal, bcum[:, :, None] - bcum[:, None], -jnp.inf))
    attn = jnp.einsum('bihk,bjhk,bijhk->bhij', q, k, decay)
    o = jnp.einsum('bhij,bjhv->bihv', attn, v) + jnp.einsum('bihk,bhkv->bihv', q * jnp.exp(bcum), S)
    b_last = bcum[:, -1]
    k_dec = k * jnp.exp(b_last[:, None] - bcum)
    S = jnp.exp(b_last)[..., None] * S + jnp.einsum('bjhk,bjhv->bhkv', k_dec, v)
    return S, o

def ssd_chunk_step(S, inp):
    x, dt, a, Bm, Cm = inp
    c = x.shape[1]
    acum = jnp.cumsum(a, axis=1)
    causal = jnp.tril(jnp.ones((c, c), dtype=bool))[None, :, :, None, None]
    lmat = jnp.exp(jnp.where(causal, acum[:, :, None] - acum[:, None], -jnp.inf))
    cb = jnp.einsum('bign,bjgn->bijg', Cm, Bm)
    y = jnp.einsum('bijg,bijgr,bjgrp->bigrp', cb, lmat * dt[:, None], x)
    y = y + jnp.einsum('bign,bgrpn->bigrp', Cm, S) * jnp.exp(acum)[..., None]
    a_last = acum[:, -1]
    w = jnp.exp(a_last[:, None] - acum) * dt
    S = jnp.exp(a_last)[..., None, None] * S + jnp.einsum('bjgn,bjgr,bjgrp->bgrpn', Bm, w, x)
    return S, y

def gla_mixer(h, S0, seg_lens, w_in, w_gate_up, b_gate, w_norm, w_out):
    bsz, l, _ = h.shape
    f32 = jnp.float32
    proj = (h @ w_in).astype(f32)
    q, k, v, r, g_low = jnp.split(
        proj, [GLA_DK, 2 * GLA_DK, 2 * GLA_DK + GLA_DV, 2 * GLA_DK + 2 * GLA_DV], axis=-1)
    log_alpha = jax.nn.log_sigmoid(g_low @ w_gate_up.astype(f32) + b_gate.astype(f32)) / GLA_TAU
    q = q.reshape(bsz, l, GLA_HEADS, GLA_HK) * (GLA_HK ** -0.5)
    k = k.reshape(bsz, l, GLA_HEADS, GLA_HK)
    v = v.reshape(bsz, l, GLA_HEADS, GLA_HV)
    log_alpha = log_alpha.reshape(bsz, l, GLA_HEADS, GLA_HK)
    S, o = segmented_scan(gla_chunk_step, S0.astype(f32), (q, k, v, log_alpha), seg_lens)
    o = o * lax.rsqrt(jnp.mean(o * o, axis=-1, keepdims=True) + NORM_EPS)
    o = o * w_norm.astype(f32).reshape(GLA_HEADS, GLA_HV)
    o = o.reshape(bsz, l, GLA_DV) * jax.nn.silu(r)
    y = o.astype(h.dtype) @ w_out
    return y, S.astype(h.dtype)

def ssd_mixer(h, S0, conv_buf, seg_lens, w_in, conv_w, conv_b, dt_bias, a_log, d_skip, w_norm, w_out):
    bsz, l, _ = h.shape
    f32 = jnp.float32
    proj = (h @ w_in).astype(f32)
    z, xbc, dt_raw = jnp.split(proj, [SSD_DINNER, SSD_DINNER + SSD_CONV_DIM], axis=-1)
    xpad = jnp.concatenate([conv_buf.astype(f32), xbc], axis=1)
    new_buf = xpad[:, xpad.shape[1] - (SSD_CONV - 1):]
    cw = conv_w.astype(f32)
    conv = conv_b.astype(f32) + xpad[:, 0:l] * cw[0]
    for i in range(1, SSD_CONV):
        conv = conv + xpad[:, i:i + l] * cw[i]
    xbc = jax.nn.silu(conv)
    x, Bm, Cm = jnp.split(xbc, [SSD_DINNER, SSD_DINNER + SSD_GROUPS * SSD_STATE], axis=-1)
    x = x.reshape(bsz, l, SSD_GROUPS, SSD_HPG, SSD_HEADDIM)
    Bm = Bm.reshape(bsz, l, SSD_GROUPS, SSD_STATE)
    Cm = Cm.reshape(bsz, l, SSD_GROUPS, SSD_STATE)
    dt = jax.nn.softplus(dt_raw + dt_bias.astype(f32)).reshape(bsz, l, SSD_GROUPS, SSD_HPG)
    A = -jnp.exp(a_log.astype(f32)).reshape(SSD_GROUPS, SSD_HPG)
    S0g = S0.astype(f32).reshape(bsz, SSD_GROUPS, SSD_HPG, SSD_HEADDIM, SSD_STATE)
    S, y = segmented_scan(ssd_chunk_step, S0g, (x, dt, dt * A, Bm, Cm), seg_lens)
    y = y + d_skip.astype(f32).reshape(SSD_GROUPS, SSD_HPG)[..., None] * x
    y = y.reshape(bsz, l, SSD_DINNER) * jax.nn.silu(z)
    yg = y.reshape(bsz, l, SSD_GROUPS, SSD_DINNER // SSD_GROUPS)
    yg = yg * lax.rsqrt(jnp.mean(yg * yg, axis=-1, keepdims=True) + NORM_EPS)
    y = yg.reshape(bsz, l, SSD_DINNER) * w_norm.astype(f32)
    out = y.astype(h.dtype) @ w_out
    S = S.reshape(bsz, SSD_HEADS, SSD_HEADDIM, SSD_STATE)
    return out, S.astype(h.dtype), new_buf.astype(h.dtype)

def trunk(x, gla_states, ssm_states, conv_bufs, seg_lens, pre_norm, post_norm,
          gla_w_in, gla_w_gate_up, gla_b_gate, gla_w_norm, gla_w_out,
          ssd_w_in, ssd_conv_w, ssd_conv_b, ssd_dt_bias, ssd_a_log, ssd_d_skip, ssd_w_norm, ssd_w_out):
    new_gla, new_ssm, new_conv = [], [], []
    for i in range(DEPTH):
        h = rmsnorm(x, pre_norm[i])
        j = i // N_MIXERS
        if i % N_MIXERS == 0:
            y, S = gla_mixer(h, gla_states[j], seg_lens, gla_w_in[j], gla_w_gate_up[j],
                             gla_b_gate[j], gla_w_norm[j], gla_w_out[j])
            new_gla.append(S)
        else:
            y, S, buf = ssd_mixer(h, ssm_states[j], conv_bufs[j], seg_lens, ssd_w_in[j],
                                  ssd_conv_w[j], ssd_conv_b[j], ssd_dt_bias[j], ssd_a_log[j],
                                  ssd_d_skip[j], ssd_w_norm[j], ssd_w_out[j])
            new_ssm.append(S)
            new_conv.append(buf)
        x = x + rmsnorm(y, post_norm[i]).astype(x.dtype)
    return x, jnp.stack(new_gla), jnp.stack(new_ssm), jnp.stack(new_conv)

def setup_inputs(seed: int = 0) -> dict:
    key = jax.random.key(seed)
    ks = jax.random.split(key, 24)
    f32 = jnp.float32
    nrm = lambda k, shape, s: jax.random.normal(k, shape, f32) * s
    dt0 = jnp.exp(jax.random.uniform(ks[17], (N_SSD_LAYERS, SSD_HEADS), f32,
                                     np.log(1e-3).astype(np.float32), np.log(1e-1).astype(np.float32)))
    return {
        "x_prompt": nrm(ks[0], (BATCH, SEQ, D_MODEL), 1.0),
        "x_sample": nrm(ks[1], (DEC_BATCH, DEC_SEQ, D_MODEL), 1.0),
        "state_gla": nrm(ks[2], (N_GLA_LAYERS, DEC_BATCH, GLA_HEADS, GLA_HK, GLA_HV), 0.1),
        "state_ssm": nrm(ks[3], (N_SSD_LAYERS, DEC_BATCH, SSD_HEADS, SSD_HEADDIM, SSD_STATE), 0.1),
        "state_conv": nrm(ks[4], (N_SSD_LAYERS, DEC_BATCH, SSD_CONV - 1, SSD_CONV_DIM), 1.0),
        "meta_tokens": nrm(ks[5], (N_META, D_MODEL), 1.0),
        "pre_norm": 1.0 + nrm(ks[6], (DEPTH, D_MODEL), 0.02),
        "post_norm": 1.0 + nrm(ks[7], (DEPTH, D_MODEL), 0.02),
        "gla_w_in": nrm(ks[8], (N_GLA_LAYERS, D_MODEL, GLA_IN), D_MODEL ** -0.5),
        "gla_w_gate_up": nrm(ks[9], (N_GLA_LAYERS, GLA_RANK, GLA_DK), GLA_RANK ** -0.5),
        "gla_b_gate": nrm(ks[10], (N_GLA_LAYERS, GLA_DK), 0.1),
        "gla_w_norm": 1.0 + nrm(ks[11], (N_GLA_LAYERS, GLA_DV), 0.02),
        "gla_w_out": nrm(ks[12], (N_GLA_LAYERS, GLA_DV, D_MODEL), GLA_DV ** -0.5),
        "ssd_w_in": nrm(ks[13], (N_SSD_LAYERS, D_MODEL, SSD_IN), D_MODEL ** -0.5),
        "ssd_conv_w": nrm(ks[14], (N_SSD_LAYERS, SSD_CONV, SSD_CONV_DIM), SSD_CONV ** -0.5),
        "ssd_conv_b": nrm(ks[15], (N_SSD_LAYERS, SSD_CONV_DIM), 0.02),
        "ssd_dt_bias": dt0 + jnp.log(-jnp.expm1(-dt0)),
        "ssd_a_log": jnp.log(jax.random.uniform(ks[18], (N_SSD_LAYERS, SSD_HEADS), f32, 1.0, 16.0)),
        "ssd_d_skip": 1.0 + nrm(ks[19], (N_SSD_LAYERS, SSD_HEADS), 0.1),
        "ssd_w_norm": 1.0 + nrm(ks[20], (N_SSD_LAYERS, SSD_DINNER), 0.02),
        "ssd_w_out": nrm(ks[21], (N_SSD_LAYERS, SSD_DINNER, D_MODEL), SSD_DINNER ** -0.5),
    }

def reference(x_prompt, x_sample, state_gla, state_ssm, state_conv, meta_tokens, pre_norm, post_norm,
              gla_w_in, gla_w_gate_up, gla_b_gate, gla_w_norm, gla_w_out,
              ssd_w_in, ssd_conv_w, ssd_conv_b, ssd_dt_bias, ssd_a_log, ssd_d_skip, ssd_w_norm, ssd_w_out):
    weights = (pre_norm, post_norm, gla_w_in, gla_w_gate_up, gla_b_gate, gla_w_norm, gla_w_out,
               ssd_w_in, ssd_conv_w, ssd_conv_b, ssd_dt_bias, ssd_a_log, ssd_d_skip, ssd_w_norm, ssd_w_out)
    dt = x_prompt.dtype
    meta = jnp.broadcast_to(meta_tokens.astype(dt)[None], (BATCH, N_META, D_MODEL))
    xp = jnp.concatenate([meta, x_prompt], axis=1)
    gla0 = jnp.zeros((N_GLA_LAYERS, BATCH, GLA_HEADS, GLA_HK, GLA_HV), dt)
    ssm0 = jnp.zeros((N_SSD_LAYERS, BATCH, SSD_HEADS, SSD_HEADDIM, SSD_STATE), dt)
    conv0 = jnp.zeros((N_SSD_LAYERS, BATCH, SSD_CONV - 1, SSD_CONV_DIM), dt)
    yp, gla_p, ssm_p, conv_p = trunk(xp, gla0, ssm0, conv0, (N_META, SEQ), *weights)
    y_prompt = yp[:, N_META:]
    y_sample, gla_s, ssm_s, conv_s = trunk(x_sample, state_gla, state_ssm, state_conv,
                                           (DEC_SEQ,), *weights)
    return (y_prompt, y_sample, gla_p, ssm_p, conv_p, gla_s, ssm_s, conv_s)


_drawn_inputs = setup_inputs


def setup_inputs(seed=0):
    import zlib

    import numpy as np

    out = dict(_drawn_inputs(seed))
    spreads = {}
    factors = {}
    for name, (base, spread) in spreads.items():
        noise = np.random.default_rng([zlib.crc32(name.encode()), seed]).standard_normal(out[name].shape)
        drawn = base * np.exp(spread * noise) if base else spread * noise
        out[name] = __import__('jax').numpy.asarray(drawn.astype(out[name].dtype))
    for name, factor in factors.items():
        out[name] = (out[name] * factor).astype(out[name].dtype)
    return out
```

```python
from contextlib import ExitStack

import concourse.bass as bass
from concourse import mybir

F32 = mybir.dt.float32
F32R = mybir.dt.float32r
I32 = mybir.dt.int32
ALU = mybir.AluOpType
ACT = mybir.ActivationFunctionType

P = 128
D = 1024
KT = D // P
NS = 8
NM = 16
SEQ = 1024
C0 = NS + NM
T = C0 + SEQ
STEPS = 1 + SEQ // P
EPS = 1e-6
U = 4
HK = 128
HV = 256
TAU = 16.0
GR = 16
SH = 32
HPG = 8
HD = 64
DI = 2048
CONV = 3072
CGS = [(0, 350), (350, 350), (700, 348)]
GLA_COLS = {"q": 0, "k": 512, "v": 1024, "r": 2048, "g": 3072}
SSD_COLS = {"z": 0, "x": 2048, "B": 4096, "C": 4608, "dt": 5120}


def step_cols(s):
    return (0, C0) if s == 0 else (C0 + P * (s - 1), P)


def gla_levels(s):
    return ([8, 4, 2, 1], NS) if s == 0 else ([64, 32, 16, 8, 4, 2, 1], 0)


def interleave(tiles, convs, wo_tiles, lead):
    pieces, late = [], None
    for t in range(U * tiles):
        for c in range(3):
            pieces.append((t, c))
            if c == 0 and late is not None:
                pieces.append((late, 3))
                late = None
        if t % tiles in convs:
            late = t
    if late is not None:
        pieces.append((late, 3))
    last = [max(i for i, (t, _) in enumerate(pieces) if t // tiles == u) for u in range(U)]
    order, weights = [], []
    at = 0

    def weight(w):
        weights.append(w)
        order.append(("split", len(weights) - 1))

    def piece():
        nonlocal at
        if at >= len(pieces):
            return
        t, c = pieces[at]
        order.append(("piece", at))
        if c == 0 and t + 1 < U * tiles:
            weight(("in", t + 1))
        for lag, name in enumerate(("evac", "finish", "store"), 1):
            if at >= lag:
                order.append((name, at - lag))
        at += 1
        if at == len(pieces):
            order.extend([("evac", at - 1), ("finish", at - 2), ("store", at - 3), ("finish", at - 1),
                          ("store", at - 2), ("store", at - 1)])

    weight(("in", 0))
    for _ in range(min(last[0] + 1 + lead, len(pieces))):
        piece()
    per = len(pieces) / U / STEPS
    start = at
    slot = 0

    def fill(k, n):
        goal = start + (slot * 1.0 + k / n) * per
        while at < len(pieces) and at < goal:
            piece()

    for u in range(U):
        for k in range(wo_tiles):
            weight(("out", u * wo_tiles + k))
        order.append(("load", u, 0))
        for s in range(STEPS):
            if s + 1 < STEPS:
                order.append(("load", u, s + 1))
            order.append(("A", u, s))
            fill(1, 3)
            if s:
                order.append(("D", u, s - 1))
            order.append(("B", u, s))
            fill(2, 3)
            order.append(("C", u, s))
            fill(3, 3)
            slot += 1
        order.append(("D", u, STEPS - 1))
        order.append(("E", u))
    return order, pieces, weights, last


def hybrid_kernel(nc, x_prompt, x_sample, state_gla, state_ssm, state_conv, meta_tokens, pre_norm,
                  post_norm, gla_w_in, gla_w_gate_up, gla_b_gate, gla_w_norm, gla_w_out, ssd_w_in,
                  ssd_conv_w, ssd_conv_b, ssd_dt_bias, ssd_a_log, ssd_d_skip, ssd_w_norm, ssd_w_out,
                  y_prompt, y_sample, gla_prompt, ssm_prompt, conv_prompt, gla_sample, ssm_sample,
                  conv_sample):
    gq = nc.dram_tensor("gla_rows", [U, 7 * P, T], F32, kind="Internal").ap()
    sq = nc.dram_tensor("ssd_rows", [U, 10 * P, T], F32, kind="Internal").ap()
    acd = nc.dram_tensor("ssd_decay_rows", [SH, T], F32, kind="Internal").ap()
    x1d = nc.dram_tensor("x_after_gla", [T, D], F32, kind="Internal").ap()

    with ExitStack() as top:
        def sb(name, shape, dt=F32):
            return top.enter_context(nc.sbuf_tensor(name, shape, dt))

        def ps(name):
            return top.enter_context(nc.psum_tensor(name, [P, 512], F32))

        m = {}
        m["h"] = sb("h", [P, 2, KT, T], F32R)
        m["y"] = sb("y_acc", [P, STEPS, D])
        m["w"] = sb("w", [P, 2, 2, KT, P], F32R)
        m["raw"] = sb("w_raw", [P, 2, D])
        m["wo"] = sb("w_out", [P, 4, 2, D], F32R)
        m["ident"] = sb("ident", [P, P])
        m["tri"] = sb("tri", [P, P])
        m["tri0"] = sb("tri0", [C0, C0])
        m["wn"] = sb("wn", [P, 24])
        m["bg"] = sb("bg", [P, U])
        m["cw"] = sb("cw", [P, 5, 24])
        m["banks"] = [ps(f"bank{i}") for i in range(8)]
        io = dict(xp=x_prompt, xs=x_sample, meta=meta_tokens, x1=x1d, pre=pre_norm, post=post_norm,
                  yp=y_prompt, ys=y_sample)
        for name in ("rows_out0", "rows_out1", "rows_out2", "gla_state_out", "gla_sample_out0",
                     "gla_sample_out1", "conv_old_out", "conv_out", "ssm_state_out", "ssm_sample_out0",
                     "ssm_sample_out1"):
            m[name] = nc.alloc_semaphore(name)
        with nc.cleanup_on_exit():
            constants(nc, m, gla_w_norm, ssd_w_norm, gla_b_gate, ssd_conv_w, ssd_conv_b)
        with nc.cleanup_on_exit():
            norm_phase(nc, m, io, 0)
        with nc.cleanup_on_exit():
            gla_gates(nc, m, gla_w_in, gla_w_gate_up, gq)
        with nc.cleanup_on_exit():
            gla_layer(nc, m, gq, gla_w_in, gla_w_out, state_gla, gla_prompt, gla_sample)
        with nc.cleanup_on_exit():
            norm_phase(nc, m, io, 1)
        with ExitStack() as ssd:
            t = {}
            for name, shape in (("dt", [P, STEPS, SH]), ("ac", [P, STEPS, SH]), ("ecol", [P, 16, NS]),
                                ("dskip", [P, SH]), ("sc", [P, 24, 3, NS])):
                t[name] = ssd.enter_context(nc.sbuf_tensor(name, shape, F32))
            with nc.cleanup_on_exit():
                ssd_step_sizes(nc, m, t, ssd_w_in, ssd_dt_bias, ssd_a_log, ssd_d_skip, state_conv, acd,
                               conv_sample)
            with nc.cleanup_on_exit():
                ssd_layer(nc, m, t, sq, acd, ssd_w_in, ssd_w_out, state_ssm, ssm_prompt, ssm_sample,
                          conv_prompt, conv_sample)
        with nc.cleanup_on_exit():
            norm_phase(nc, m, io, 2)


def constants(nc, m, gla_w_norm, ssd_w_norm, gla_b_gate, conv_w, conv_b):
    ident, tri, tri0 = m["ident"], m["tri"], m["tri0"]
    bank = m["banks"][0]
    with ExitStack() as ctx:
        rows = ctx.enter_context(nc.sbuf_tensor("rows", [24, 8, P], F32))
        loaded = nc.alloc_semaphore("c_loaded")
        made = nc.alloc_semaphore("c_made")
        turned = nc.alloc_semaphore("c_turned")
        kept = nc.alloc_semaphore("c_kept")
        block = ctx.enter_context(nc.Block())
        parts = [(conv_w[0, i].rearrange("(a p) -> a p", p=P), 24) for i in range(4)]
        parts.append((conv_b[0].rearrange("(a p) -> a p", p=P), 24))
        parts.append((ssd_w_norm[0].rearrange("(a p) -> a p", p=P), 16))
        parts.append((gla_w_norm[0].rearrange("(a p) -> a p", p=P), 8))
        parts.append((gla_b_gate[0].rearrange("(a p) -> a p", p=P), 4))

        @block.sync
        def _(sp):
            for i, (src, n) in enumerate(parts):
                sp.dma_start(rows[0:n, i, :], src).then_inc(loaded, 16)

        @block.gpsimd
        def _(pool):
            pool.memset(ident[:, :], 0.0).then_inc(made, 1)
            pool.memset(tri[:, :], 1.0).then_inc(made, 1)
            pool.wait_ge(made, 2)
            pool.affine_select(out=ident[:, :], in_=ident[:, :], compare_op=ALU.not_equal, fill=1.0,
                               base=0, pattern=[[-1, P]], channel_multiplier=1).then_inc(made, 1)
            pool.affine_select(out=tri[:, :], in_=tri[:, :], compare_op=ALU.is_ge, fill=0.0,
                               base=0, pattern=[[1, P]], channel_multiplier=-1).then_inc(made, 1)
            pool.wait_ge(made, 4)
            pool.tensor_copy(tri0[:, :], tri[0:C0, 0:C0]).then_inc(made, 1)
            pool.wait_ge(made, 5)
            pool.tensor_copy(tri0[0:NS, :], ident[0:NS, 0:C0]).then_inc(made, 1)

        @block.tensor
        def _(pe):
            pe.wait_ge(made, 6)
            pe.wait_ge(loaded, 16 * len(parts))
            for i, (_, n) in enumerate(parts):
                last = pe.transpose(bank[:, 24 * i:24 * i + n], rows[0:n, i, :], ident[0:n, 0:n])
            last.then_inc(turned, 1)

        @block.scalar
        def _(act):
            act.wait_ge(turned, 1)
            act.activation(m["cw"][:, :, :], bank[:, 0:120].rearrange("p (i a) -> p i a", i=5),
                           ACT.Copy, scale=0.5).then_inc(kept, 1)
            act.activation(m["wn"][:, 0:16], bank[:, 120:136], ACT.Copy).then_inc(kept, 1)
            act.activation(m["wn"][:, 16:24], bank[:, 144:152], ACT.Copy, scale=0.5).then_inc(kept, 1)
            act.activation(m["bg"][:, :], bank[:, 168:172], ACT.Copy).then_inc(kept, 1)
            act.wait_ge(kept, 4)


def norm_phase(nc, m, io, k):
    y, h, ident = m["y"], m["h"], m["ident"]
    banks = m["banks"]
    with ExitStack() as ctx:
        def sb(name, shape):
            return ctx.enter_context(nc.sbuf_tensor(f"{name}{k}", shape, F32))

        def sem(name):
            return nc.alloc_semaphore(f"n{k}_{name}")

        pre, post = sb("pre", [P, D]), sb("post", [P, D])
        xt = sb("xt", [P, 3, D])
        junk = sb("junk", [P, D])
        ssum, mean, rstd = sb("ssum", [P, 2, STEPS]), sb("mean", [P, 2, STEPS]), sb("rstd", [P, 2, STEPS])
        power = sb("power", [P, 1])
        w_in, x_in = sem("w_in"), [sem(f"x_in{i}") for i in range(3)]
        stored = [m[f"rows_out{i}"] if k == 2 else sem(f"stored{i}") for i in range(3)]
        ready, squared, meant, rooted = sem("ready"), sem("squared"), sem("meant"), sem("rooted")
        scaled, added, normed, turned, high, low = (sem(n) for n in
                                                    ("scaled", "added", "normed", "turned", "high", "low"))
        block = ctx.enter_context(nc.Block())
        norms = [0] if k == 0 else [0, 1] if k == 1 else [1]

        def copies(s):
            if k < 2:
                return [(0, io["xs"][:, 0, :]), (NS, io["meta"])] if s == 0 else \
                       [(0, io["xp"][0, P * (s - 1):P * s, :])]
            c, n = step_cols(s)
            return [(0, io["x1"][c:c + n, :])]

        def arrived_all(s):
            two = 1 if k != 2 and s % 3 == 0 else 0
            return 16 * (s // 3 + 1 + two)

        def stores(s):
            if k == 2:
                return [(NS, io["ys"][:, 0, :])] if s == 0 else [(P, io["yp"][0, P * (s - 1):P * s, :])]
            c, n = step_cols(s)
            return [(n, io["x1"][c:c + n, :])]

        @block.sync
        def _(sp):
            if 0 in norms:
                sp.dma_start(pre[:, :], io["pre"][min(k, 1):min(k, 1) + 1, :].to_broadcast([P, D])).then_inc(w_in, 16)
            if 1 in norms:
                sp.dma_start(post[:, :], io["post"][k - 1:k, :].to_broadcast([P, D])).then_inc(w_in, 16)
            for s in range(STEPS + 2):
                if s < STEPS:
                    if s >= 3:
                        if k < 2:
                            sp.wait_ge(normed, s - 2)
                        if k > 0:
                            sp.wait_ge(stored[s % 3], 16 * (s // 3))
                    for p0, src in copies(s):
                        sp.dma_start(xt[p0:p0 + src.shape[0], s % 3, :], src).then_inc(x_in[s % 3], 16)
                if k > 0 and s >= 2:
                    q = s - 2
                    sp.wait_ge(added, q + 1)
                    for n, dst in stores(q):
                        sp.dma_start(dst, xt[0:n, q % 3, :]).then_inc(stored[q % 3], 16)
            if k > 0:
                for i in range(3):
                    sp.wait_ge(stored[i], 16 * (STEPS // 3))

        @block.gpsimd
        def _(pool):
            pool.memset(power[:, :], -0.5).then_inc(ready, 1)
            pool.wait_ge(ready, 1)
            i = 0
            for s in range(STEPS):
                n = step_cols(s)[1]
                for w in reversed(norms):
                    i += 1
                    pool.wait_ge(squared, i)
                    pool.tensor_scalar(mean[0:n, w, s:s + 1], ssum[0:n, w, s:s + 1], 1.0 / D, EPS,
                                       ALU.mult, ALU.add).then_inc(meant, 1)
                    pool.wait_ge(meant, i)
                    pool.tensor_tensor(rstd[0:n, w, s:s + 1], mean[0:n, w, s:s + 1], power[0:n, :],
                                       ALU.pow).then_inc(rooted, 1)

        @block.scalar
        def _(act):
            def square(src, w, s, n):
                done = len(norms) * s + (1 if len(norms) == 2 and w == 0 else 0)
                if done:
                    act.wait_ge(squared, done)
                act.activation(junk[0:n, :], src, ACT.Square,
                               accum_out=ssum[0:n, w, s:s + 1]).then_inc(squared, 1)

            for s in range(STEPS):
                c, n = step_cols(s)
                if 1 in norms:
                    square(y[0:n, s, :], 1, s, n)
                if 0 in norms:
                    if k == 0:
                        act.wait_ge(x_in[s % 3], arrived_all(s))
                    else:
                        act.wait_ge(added, s + 1)
                    square(xt[0:n, s % 3, :], 0, s, n)
                    for j in range(2):
                        act.wait_ge(turned, 2 * s + j + 1)
                        act.activation(h[:, 0, 4 * j:4 * j + 4, c:c + n],
                                       banks[j][:, 0:4 * n].rearrange("p (a c) -> p a c", a=4),
                                       ACT.Copy).then_inc(high, 1)

        @block.vector
        def _(dve):
            dve.wait_ge(w_in, 16 * len(norms))
            i = 0
            for s in range(STEPS):
                c, n = step_cols(s)
                if 1 in norms:
                    i += 1
                    dve.wait_ge(rooted, i)
                    dve.scalar_tensor_tensor(out=y[0:n, s, :], in0=y[0:n, s, :],
                                             scalar=rstd[0:n, 1, s:s + 1], in1=post[0:n, :],
                                             op0=ALU.mult, op1=ALU.mult).then_inc(scaled, 1)
                    dve.wait_ge(scaled, s + 1)
                    dve.wait_ge(x_in[s % 3], arrived_all(s))
                    dve.tensor_tensor(xt[0:n, s % 3, :], xt[0:n, s % 3, :], y[0:n, s, :],
                                      ALU.add).then_inc(added, 1)
                if 0 in norms:
                    i += 1
                    dve.wait_ge(rooted, i)
                    if k == 1:
                        dve.wait_ge(added, s + 1)
                    dve.scalar_tensor_tensor(out=y[0:n, s, :], in0=xt[0:n, s % 3, :],
                                             scalar=rstd[0:n, 0, s:s + 1], in1=pre[0:n, :],
                                             op0=ALU.mult, op1=ALU.mult).then_inc(normed, 1)
                    for j in range(2):
                        dve.wait_ge(high, 2 * s + j + 1)
                        dve.tensor_tensor(h[:, 1, 4 * j:4 * j + 4, c:c + n],
                                          banks[j][:, 0:4 * n].rearrange("p (a c) -> p a c", a=4),
                                          h[:, 0, 4 * j:4 * j + 4, c:c + n].bitcast(F32),
                                          ALU.subtract).then_inc(low, 1)

        if 0 in norms:
            @block.tensor
            def _(pe):
                for s in range(STEPS):
                    n = step_cols(s)[1]
                    pe.wait_ge(normed, s + 1)
                    for j in range(2):
                        if s:
                            pe.wait_ge(low, 2 * s - 1 + j)
                        for a in range(4):
                            f = (4 * j + a) * P
                            last = pe.transpose(banks[j][:, a * n:a * n + n], y[0:n, s, f:f + P],
                                                ident[0:n, 0:n])
                        last.then_inc(turned, 1)


def reset_mask(pool, mask, made, at):
    pool.memset(mask, 1.0).then_inc(made, 1)
    pool.wait_ge(made, at + 1)
    n = mask.shape[0]
    pool.memset(mask[:, 0:NS + 1], 0.0).then_inc(made, 1)
    for s in range(1, STEPS):
        c = step_cols(s)[0]
        pool.memset(mask[:, c:c + 1], 0.0).then_inc(made, 1)
    return at + 1 + STEPS


def narrow_projection(pe, m, n_w, w_lo, evacuated, projected):
    h, w, banks = m["h"], m["w"], m["banks"]
    pe.wait_ge(w_lo, 1)
    for g, (c, n) in enumerate(CGS):
        i = 0
        for k in range(KT):
            for a, b in ((0, 0), (0, 1), (1, 0)):
                last = pe.matmul(banks[g][:, 0:n], w[:, 0, a, k, :], h[:, b, k, c:c + n],
                                 start=(i == 0), stop=(i == 3 * KT - 1))
                i += 1
        last.then_inc(projected, 1)


def gla_gates(nc, m, w_in, w_up, gq):
    w, raw, banks, bg = m["w"], m["raw"], m["banks"], m["bg"]
    c0 = GLA_COLS["g"]
    with ExitStack() as ctx:
        def sem(name):
            return nc.alloc_semaphore(f"gg_{name}")

        low = ctx.enter_context(nc.sbuf_tensor("g_low", [GR, T], F32))
        up = ctx.enter_context(nc.sbuf_tensor("g_up", [GR, U * HK], F32))
        mask = ctx.enter_context(nc.sbuf_tensor("g_mask", [P, T], F32))
        t1 = ctx.enter_context(nc.sbuf_tensor("g_t1", [P, 2, T], F32))
        t2 = ctx.enter_context(nc.sbuf_tensor("g_t2", [P, 2, T], F32))
        wr, up_in, made, zeroed, w_hi, w_lo, projected, lows, gated = (
            sem(x) for x in ("w_raw", "up_in", "made", "zeroed", "w_hi", "w_lo", "projected", "lows", "gated"))
        absd, capped, exped, logged, summed, scanned = (
            sem(x) for x in ("absd", "capped", "exped", "logged", "summed", "scanned"))
        stored = [sem(f"stored{i}") for i in range(2)]
        block = ctx.enter_context(nc.Block())
        r = raw[:, 0, 0:KT * GR].rearrange("p (k f) -> p k f", k=KT)

        @block.sync
        def _(sp):
            sp.dma_start(r, w_in[0, :, c0:c0 + GR].rearrange("(k p) f -> p k f", p=P)).then_inc(wr, 16)
            sp.dma_start(up[:, :], w_up[0]).then_inc(up_in, 16)
            for u in range(U):
                sp.wait_ge(scanned, u + 1)
                sp.dma_start(gq[u, 2 * P:3 * P, :], t2[:, u % 2, :]).then_inc(stored[u % 2], 16)
            for i in range(2):
                sp.wait_ge(stored[i], 16 * (U // 2))

        @block.gpsimd
        def _(pool):
            pool.memset(w[:, 0, 0, :, :].bitcast(F32), 0.0).then_inc(zeroed, 1)
            pool.memset(w[:, 0, 1, :, :].bitcast(F32), 0.0).then_inc(zeroed, 1)
            reset_mask(pool, mask[:, :], made, 0)

        @block.scalar
        def _(act):
            act.wait_ge(zeroed, 2)
            act.wait_ge(wr, 16)
            act.activation(w[:, 0, 0, :, 0:GR], r, ACT.Copy).then_inc(w_hi, 1)
            for g, (c, n) in enumerate(CGS):
                act.wait_ge(projected, g + 1)
                act.activation(low[:, c:c + n], banks[g][0:GR, 0:n], ACT.Copy).then_inc(lows, 1)
            for u in range(U):
                if u >= 2:
                    act.wait_ge(scanned, u - 1)
                for g, (c, n) in enumerate(CGS):
                    i = 3 * u + g
                    act.wait_ge(gated, i + 1)
                    act.activation(t1[:, u % 2, c:c + n], banks[i % 6][:, 0:n], ACT.Abs,
                                   bias=bg[:, u:u + 1]).then_inc(absd, 1)
                act.wait_ge(absd, 3 * u + 3)
                act.activation(t1[:, u % 2, :], t1[:, u % 2, :], ACT.Exp, scale=-1.0).then_inc(exped, 1)
                act.wait_ge(exped, u + 1)
                act.activation(t1[:, u % 2, :], t1[:, u % 2, :], ACT.Ln, bias=1.0).then_inc(logged, 1)

        @block.vector
        def _(dve):
            dve.wait_ge(w_hi, 1)
            dve.tensor_tensor(w[:, 0, 1, :, 0:GR], r, w[:, 0, 0, :, 0:GR].bitcast(F32),
                              ALU.subtract).then_inc(w_lo, 1)
            dve.wait_ge(made, 1 + STEPS)
            for u in range(U):
                if u >= 2:
                    dve.wait_ge(stored[u % 2], 16 * (u // 2))
                for g, (c, n) in enumerate(CGS):
                    i = 3 * u + g
                    dve.wait_ge(absd, i + 1)
                    dve.tensor_scalar(t2[:, u % 2, c:c + n], banks[i % 6][:, 0:n], bg[:, u:u + 1], 0.0,
                                      ALU.add, ALU.min).then_inc(capped, 1)
                dve.wait_ge(logged, u + 1)
                dve.wait_ge(capped, 3 * u + 3)
                dve.tensor_tensor(t1[:, u % 2, :], t2[:, u % 2, :], t1[:, u % 2, :],
                                  ALU.subtract).then_inc(summed, 1)
                dve.wait_ge(summed, u + 1)
                dve.tensor_tensor_scan(t2[:, u % 2, :], mask[:, :], t1[:, u % 2, :], 0.0, ALU.mult,
                                       ALU.add).then_inc(scanned, 1)

        @block.tensor
        def _(pe):
            narrow_projection(pe, m, GR, w_lo, None, projected)
            pe.wait_ge(up_in, 16)
            pe.wait_ge(lows, 3)
            for u in range(U):
                for g, (c, n) in enumerate(CGS):
                    i = 3 * u + g
                    if i >= 6:
                        pe.wait_ge(capped, i - 5)
                    pe.matmul(banks[i % 6][:, 0:n], up[:, u * HK:(u + 1) * HK], low[:, c:c + n],
                              start=True, stop=True).then_inc(gated, 1)


class Weights:

    def __init__(self, weights, pieces, w_in, w_out, columns, tiles, wo_tiles, wn0):
        self.ends = {t: i + 1 for i, (t, g) in enumerate(pieces) if g == 2}
        self.weights, self.w_in, self.w_out, self.columns = weights, w_in, w_out, columns
        self.tiles, self.wo_tiles, self.wn0 = tiles, wo_tiles, wn0
        self.index = {w: i for i, w in enumerate(weights)}

    def source(self, i):
        kind, t = self.weights[i]
        if kind == "in":
            c = self.columns(t)
            return self.w_in[:, c:c + P].rearrange("(k p) f -> p k f", p=P)
        return self.w_out[t * P:(t + 1) * P, :]

    def raw(self, m, i):
        r = m["raw"][:, i % 2, :]
        return r.rearrange("p (k f) -> p k f", k=KT) if self.weights[i][0] == "in" else r

    def part(self, m, i, part):
        kind, t = self.weights[i]
        return m["w"][:, t % 2, part, :, :] if kind == "in" else m["wo"][:, t % self.wo_tiles, part, :]

    def load(self, sp, m, i, raw_in, w_lo):
        if i >= 2:
            sp.wait_ge(w_lo, i - 1)
        sp.dma_start(self.raw(m, i), self.source(i)).then_inc(raw_in[i % 2], 16)

    def high(self, act, m, i, raw_in, w_hi, piece_done, out_used):
        kind, t = self.weights[i]
        act.wait_ge(raw_in[i % 2], 16 * (i // 2 + 1))
        if kind == "in":
            if t >= 2:
                act.wait_ge(piece_done, self.ends[t - 2])
            act.activation(self.part(m, i, 0), self.raw(m, i), ACT.Copy).then_inc(w_hi, 1)
        else:
            u = t // self.wo_tiles
            if u:
                act.wait_ge(out_used, 2 * STEPS * u)
            act.activation(self.part(m, i, 0), self.raw(m, i), ACT.Copy,
                           scale=m["wn"][:, self.wn0 + t:self.wn0 + t + 1]).then_inc(w_hi, 1)

    def low(self, dve, m, i, w_hi, w_lo):
        kind, t = self.weights[i]
        dve.wait_ge(w_hi, i + 1)
        hi = self.part(m, i, 0).bitcast(F32)
        if kind == "in":
            dve.tensor_tensor(self.part(m, i, 1), self.raw(m, i), hi, ALU.subtract).then_inc(w_lo, 1)
        else:
            dve.scalar_tensor_tensor(out=self.part(m, i, 1), in0=self.raw(m, i),
                                     scalar=m["wn"][:, self.wn0 + t:self.wn0 + t + 1], in1=hi,
                                     op0=ALU.mult, op1=ALU.subtract).then_inc(w_lo, 1)


def project_piece(pe, m, t, g, bank):
    c, n = CGS[g]
    i = 0
    for k in range(KT):
        for a, b in ((0, 0), (0, 1), (1, 0)):
            last = pe.matmul(bank[:, 0:n], m["w"][:, t % 2, a, k, :], m["h"][:, b, k, c:c + n],
                             start=(i == 0), stop=(i == 3 * KT - 1))
            i += 1
    return last


def out_products(pe, m, yt, wo_tiles, half, bank):
    i = 0
    for k in range(wo_tiles):
        for a, b in ((0, 0), (0, 1), (1, 0)):
            last = pe.matmul(bank[:, :], yt[a][:, k, :], m["wo"][:, k, b, 512 * half:512 * half + 512],
                             start=(i == 0), stop=(i == 3 * wo_tiles - 1))
            i += 1
    return last


def gla_layer(nc, m, gq, w_in, w_out, state, state_prompt, state_sample):
    NT, WT = 6, 2
    order, pieces, weights, last_piece = interleave(NT, set(), WT, 4)
    kinds = ["q", "k", "v", "v", "r", "r"]
    rows = [0, 1, 3, 4, 5, 6]

    def column(t):
        u, j = divmod(t, NT)
        kind = kinds[j]
        width = HK if kind in "qk" else HV
        return GLA_COLS[kind] + u * width + (P if j in (3, 5) else 0)

    W = Weights(weights, pieces, w_in[0], w_out[0], column, NT, WT, 16)
    PA, PB, TA, TB, L0, L1, O, X = m["banks"]
    PR, L, ident, y = (PA, PB), (L0, L1), m["ident"], m["y"]
    with ExitStack() as ctx:
        def sb(name, shape, dt=F32):
            return ctx.enter_context(nc.sbuf_tensor("g_" + name, shape, dt))

        def sem(name):
            return nc.alloc_semaphore("g_" + name)

        mask = sb("lmask", [P, 7, P])
        mask0 = sb("lmask0", [C0, 4, C0])
        rowsel = sb("rowsel", [C0, NS + 1])
        st = sb("stage", [P, 2, 350])
        th = sb("th", [P, 350])
        ck = sb("chunk", [P, 2, 7, P])
        E = sb("decays", [P, 8, P])
        Eq = sb("q_decayed", [P, 7, P])
        eb = sb("ebcum", [P, P])
        qe = sb("q_inter", [P, P])
        kd0 = sb("k_first", [P, C0])
        kt = sb("k_turned", [P, P])
        km = sb("k_masked", [C0, NS + 1, P])
        vt = sb("v_turned", [P, HV])
        G, G0 = sb("attn", [P, P]), sb("attn0", [C0, C0])
        on, og = sb("o_normed", [P, HV]), sb("o_gated", [P, HV])
        othi, otlo = sb("ot_hi", [P, 2, P], F32R), sb("ot_lo", [P, 2, P], F32R)
        S = sb("state", [P, HV])
        qm = sb("q_masked", [P, NS * C0])
        ss = sb("sample_state", [P, 2, 2, HV])
        osum, omean, orstd, power = (sb(x, [P, 1]) for x in ("osum", "omean", "orstd", "power"))

        raw_in = [sem(f"raw_in{i}") for i in range(2)]
        w_hi, w_lo = sem("w_hi"), sem("w_lo")
        piece_done = sem("piece_done")
        bank_free = [sem(f"bank_free{i}") for i in range(2)]
        tanhed = sem("tanhed")
        staged = [sem(f"staged{i}") for i in range(2)]
        stored = [sem(f"stored{i}") for i in range(2)]
        ck_in = [sem(f"ck_in{i}") for i in range(2)]
        consts, zeros, dsub, dabs, decays, eb_done = (sem(x) for x in
                                                      ("consts", "zeros", "dsub", "dabs", "decays", "eb_done"))
        k_ready, q_ready, qi_ready, ta_done, tb_done = (sem(x) for x in
                                                        ("k_ready", "q_ready", "qi_ready", "ta_done", "tb_done"))
        v_turned, k_turned, levels, attn_part, attn = (sem(x) for x in
                                                       ("v_turned", "k_turned", "levels", "attn_part", "attn"))
        s_prod, s_new, o_done, squared = (sem(x) for x in ("s_prod", "s_new", "o_done", "squared"))
        meant, rooted, o_scaled, o_gated, o_turned = (sem(x) for x in
                                                      ("meant", "rooted", "o_scaled", "o_gated", "o_turned"))
        ot_hi, ot_lo, out_done, added = (sem(x) for x in ("ot_hi", "ot_lo", "out_done", "added"))
        s_saved = m["gla_state_out"]
        ss_in = [sem(f"ss_in{i}") for i in range(2)]
        ss_out = [m[f"gla_sample_out{i}"] for i in range(2)]
        qm_ready, km_ready, ss_inter, ss_prod, ss_new = (sem(x) for x in
                                                         ("qm_ready", "km_ready", "ss_inter", "ss_prod", "ss_new"))
        k_ready0 = sem("k_ready0")
        CONSTS = 10 + 3 * 11 + 2
        block = ctx.enter_context(nc.Block())

        def ev(u, s):
            return u * STEPS + s

        def tokens(u, s):
            return ck[:, ev(u, s) % 2, :, 0:step_cols(s)[1]]

        @block.sync
        def _(sp):
            def store(i):
                t, g = pieces[i]
                u, j = divmod(t, NT)
                c, n = CGS[g]
                sp.wait_ge(staged[i % 2], i // 2 + 1)
                sp.dma_start(gq[u, rows[j] * P:(rows[j] + 1) * P, c:c + n],
                             st[:, i % 2, 0:n]).then_inc(stored[i % 2], 16)

            def load(u, s):
                e = ev(u, s)
                c, n = step_cols(s)
                if s == 0:
                    for i in range(2):
                        sp.wait_ge(stored[i], 16 * ((last_piece[u] - i) // 2 + 1))
                if e >= 2:
                    sp.wait_ge(ta_done, e - 1)
                    sp.wait_ge(levels, 2 * (e - 1))
                    sp.wait_ge(qi_ready, e - 1)
                    sp.wait_ge(eb_done, e - 1)
                sp.dma_start(tokens(u, s), gq[u, :, c:c + n].rearrange("(t p) c -> p t c", p=P)).then_inc(
                    ck_in[e % 2], 16)

            def sample_state(i, out):
                u, b = divmod(i, 4)
                if out:
                    sp.wait_ge(ss_new, 2 * (i + 1))
                    sp.dma_start(state_sample[0, 2 * b:2 * b + 2, u].rearrange("b k v -> k b v"),
                                 ss[:, i % 2, :, :]).then_inc(ss_out[i % 2], 16)
                else:
                    if i >= 2:
                        sp.wait_ge(ss_out[i % 2], 16 * (i // 2))
                    sp.dma_start(ss[:, i % 2, :, :],
                                 state[0, 2 * b:2 * b + 2, u].rearrange("b k v -> k b v")).then_inc(
                                     ss_in[i % 2], 16)

            W.load(sp, m, 0, raw_in, w_lo)
            W.load(sp, m, 1, raw_in, w_lo)
            for task in order:
                if task[0] == "split" and task[1] + 2 < len(weights):
                    W.load(sp, m, task[1] + 2, raw_in, w_lo)
                elif task[0] == "store":
                    store(task[1])
                elif task[0] == "load":
                    load(*task[1:])
                elif task[0] == "B" and task[2] == 0:
                    for i in range(4 * task[1], 4 * task[1] + 4):
                        sample_state(i, False)
                        if i > 4 * task[1]:
                            sample_state(i - 1, True)
                    sample_state(i, True)
                elif task[0] == "C" and task[2] == STEPS - 1:
                    u = task[1]
                    sp.wait_ge(s_new, STEPS * (u + 1))
                    sp.dma_start(state_prompt[0, 0, u], S[:, :]).then_inc(s_saved, 16)
            sp.wait_ge(s_saved, 16 * U)
            for i in range(2):
                sp.wait_ge(ss_out[i], 16 * 2 * U)
                sp.wait_ge(stored[i], 16 * ((len(pieces) - 1 - i) // 2 + 1))

        @block.gpsimd
        def _(pool):
            n = 0
            for li, h in enumerate(gla_levels(1)[0]):
                pool.memset(mask[:, li, :], 0.0).then_inc(consts, 1)
            pool.memset(mask0[:, :, :], 0.0).then_inc(consts, 1)
            pool.memset(rowsel[:, :], 1.0).then_inc(consts, 1)
            pool.memset(power[:, :], -0.5).then_inc(consts, 1)
            n = 10
            pool.wait_ge(consts, n)
            sets = [(mask[:, li, :], h, 0) for li, h in enumerate(gla_levels(1)[0])]
            sets += [(mask0[:, li, NS:C0], h, NS) for li, h in enumerate(gla_levels(0)[0])]
            views = [(v.rearrange("p (b w) -> p b w", w=2 * h)[:, :, h:2 * h], h, off) for v, h, off in sets]
            for v, h, off in views:
                pool.memset(v, 1.0).then_inc(consts, 1)
            n += len(views)
            pool.wait_ge(consts, n)
            for v, h, off in views:
                pool.affine_select(out=v, in_=v, compare_op=ALU.is_ge, fill=0.0, base=-off,
                                   pattern=[[-2 * h, v.shape[1]], [0, h]],
                                   channel_multiplier=1).then_inc(consts, 1)
            n += len(views)
            pool.wait_ge(consts, n)
            for v, h, off in views:
                pool.affine_select(out=v, in_=v, compare_op=ALU.is_ge, fill=0.0, base=off + h - 1,
                                   pattern=[[2 * h, v.shape[1]], [0, h]],
                                   channel_multiplier=-1).then_inc(consts, 1)
            n += len(views)
            pool.affine_select(out=rowsel[:, NS:NS + 1], in_=rowsel[:, NS:NS + 1], compare_op=ALU.is_ge,
                               fill=0.0, base=-NS, pattern=[[0, 1]], channel_multiplier=1).then_inc(consts, 1)
            pool.tensor_copy(rowsel[:, 0:NS], ident[0:C0, 0:NS]).then_inc(consts, 1)
            assert n + 2 == CONSTS
            for e in range(U * STEPS):
                n = step_cols(e % STEPS)[1]
                pool.wait_ge(squared, e + 1)
                pool.tensor_scalar(omean[0:n, :], osum[0:n, :], 1.0 / HV, EPS, ALU.mult,
                                   ALU.add).then_inc(meant, 1)
                pool.wait_ge(meant, e + 1)
                if e:
                    pool.wait_ge(o_scaled, e)
                pool.tensor_tensor(orstd[0:n, :], omean[0:n, :], power[0:n, :], ALU.pow).then_inc(rooted, 1)

        @block.scalar
        def _(act):
            def evac(i):
                t, g = pieces[i]
                j, n = t % NT, CGS[g][1]
                act.wait_ge(piece_done, i + 1)
                if j >= 4:
                    q = (t // NT) * 6 + (j - 4) * 3 + g
                    if q:
                        act.wait_ge(staged[(prev_gate[i]) % 2], prev_gate[i] // 2 + 1)
                    act.activation(th[:, 0:n], PR[i % 2][:, 0:n], ACT.Tanh, scale=0.5).then_inc(tanhed, 1)
                    return
                if i >= 2:
                    act.wait_ge(stored[i % 2], 16 * (i // 2))
                act.activation(st[:, i % 2, 0:n], PR[i % 2][:, 0:n], ACT.Copy,
                               scale=HK ** -0.5 if j == 0 else 1.0).then_inc(staged[i % 2], 1)

            def stage_a(u, s):
                e, n = ev(u, s), step_cols(s)[1]
                x = tokens(u, s)
                act.wait_ge(ck_in[e % 2], 16 * (e // 2 + 1))
                if e:
                    act.wait_ge(qi_ready, e)
                    act.wait_ge(s_new, e)
                    if s == 1:
                        act.wait_ge(ss_new, 2 * 4 * (u + 1))
                act.activation(eb[:, 0:n], x[:, 2, :], ACT.Exp, scale=1.0 / TAU).then_inc(eb_done, 1)
                act.wait_ge(dsub, e + 1)
                act.activation(E[:, :, 0:n], E[:, :, 0:n], ACT.Abs).then_inc(dabs, 1)
                act.wait_ge(dabs, e + 1)
                act.activation(E[:, :, 0:n], E[:, :, 0:n], ACT.Exp, scale=-1.0 / TAU).then_inc(decays, 1)
                act.wait_ge(ta_done, e + 1)
                if e:
                    act.wait_ge(o_done, e)
                    act.wait_ge(s_prod, e)
                    if s == 1:
                        act.wait_ge(ss_prod, 4 * (u + 1))
                act.activation(vt[0:n, :], TA[0:n, 0:HV], ACT.Copy).then_inc(v_turned, 1)
                if s:
                    act.wait_ge(tb_done, e + 1)
                    act.activation(kt[:, :], TB[:, 0:P], ACT.Copy).then_inc(k_turned, 1)

            def stage_c(u, s):
                e, n = ev(u, s), step_cols(s)[1]
                act.wait_ge(o_done, e + 1)
                if e:
                    act.wait_ge(rooted, e)
                    act.wait_ge(o_gated, e)
                act.activation(on[0:n, :], O[0:n, 0:HV], ACT.Square, accum_out=osum[0:n, :]).then_inc(squared, 1)
                act.wait_ge(rooted, e + 1)
                act.activation(on[0:n, :], O[0:n, 0:HV], ACT.Copy, scale=orstd[0:n, :]).then_inc(o_scaled, 1)
                act.wait_ge(o_turned, e + 1)
                if e:
                    act.wait_ge(out_done, 2 * e)
                act.activation(othi[:, :, 0:n], O[:, 0:2 * n].rearrange("p (a c) -> p a c", a=2),
                               ACT.Copy).then_inc(ot_hi, 1)

            prev_gate, seen = {}, None
            for i, (t, g) in enumerate(pieces):
                if t % NT >= 4:
                    prev_gate[i] = seen
                    seen = i
            for task in order:
                if task[0] == "split":
                    W.high(act, m, task[1], raw_in, w_hi, piece_done, out_done)
                elif task[0] == "evac":
                    evac(task[1])
                elif task[0] == "A":
                    stage_a(*task[1:])
                elif task[0] == "C":
                    stage_c(*task[1:])

        @block.vector
        def _(dve):
            dve.memset(E[:, :, :], 0.0).then_inc(zeros, 1)
            dve.memset(G[:, :], 0.0).then_inc(zeros, 1)
            dve.memset(G0[:, :], 0.0).then_inc(zeros, 1)
            dve.memset(othi[:, :, :].bitcast(F32), 0.0).then_inc(zeros, 1)
            dve.memset(otlo[:, :, :].bitcast(F32), 0.0).then_inc(zeros, 1)
            dve.memset(qm[:, :], 0.0).then_inc(zeros, 1)
            dve.wait_ge(zeros, 6)
            dve.wait_ge(consts, CONSTS)

            def evac(i):
                t, g = pieces[i]
                n = CGS[g][1]
                if t % NT < 4:
                    return
                q = (t // NT) * 6 + (t % NT - 4) * 3 + g
                dve.wait_ge(tanhed, q + 1)
                if i >= 2:
                    dve.wait_ge(stored[i % 2], 16 * (i // 2))
                dve.scalar_tensor_tensor(out=st[:, i % 2, 0:n], in0=th[:, 0:n], scalar=1.0,
                                         in1=PR[i % 2][:, 0:n], op0=ALU.add,
                                         op1=ALU.mult).then_inc(staged[i % 2], 1)

            def stage_a(u, s):
                e, n = ev(u, s), step_cols(s)[1]
                x = tokens(u, s)
                sizes, off = gla_levels(s)
                dve.wait_ge(ck_in[e % 2], 16 * (e // 2 + 1))
                if e:
                    dve.wait_ge(levels, 2 * e)
                    dve.wait_ge(tb_done, e)
                b = x[:, 2, off:n]
                if s == 0:
                    dve.memset(E[:, :, 0:NS], 0.0).then_inc(zeros, 1)
                for li, h in enumerate(sizes):
                    v = b.rearrange("p (b w) -> p b w", w=2 * h)
                    nb = v.shape[1]
                    dve.tensor_tensor(E[:, li, off:n].rearrange("p (b w) -> p b w", w=2 * h), v,
                                      v[:, :, h - 1:h].to_broadcast([P, nb, 2 * h]), ALU.subtract)
                dve.tensor_tensor(E[:, 7, off:n], b, x[:, 2, n - 1:n].to_broadcast([P, n - off]),
                                  ALU.subtract).then_inc(dsub, 1)
                dve.wait_ge(decays, e + 1)
                nl = len(sizes)
                dve.tensor_tensor(Eq[:, 0:nl, 0:n], E[:, 0:nl, 0:n],
                                  x[:, 0:1, :].to_broadcast([P, nl, n]), ALU.mult).then_inc(q_ready, 1)
                dve.wait_ge(q_ready, e + 1)
                dve.tensor_tensor(E[:, :, 0:n], E[:, :, 0:n],
                                  x[:, 1:2, :].to_broadcast([P, 8, n]), ALU.mult).then_inc(k_ready, 1)
                dve.wait_ge(eb_done, e + 1)
                if e:
                    dve.wait_ge(o_done, e)
                dve.tensor_tensor(qe[:, 0:n], x[:, 0, :], eb[:, 0:n], ALU.mult).then_inc(qi_ready, 1)
                if s == 0:
                    dve.wait_ge(k_ready, e + 1)
                    dve.tensor_copy(kd0[:, 0:NS], x[:, 1, 0:NS]).then_inc(k_ready0, 1)
                    dve.tensor_copy(kd0[:, NS:C0], E[:, 7, NS:C0]).then_inc(k_ready0, 1)
                    dve.wait_ge(qi_ready, e + 1)
                    dve.tensor_copy(qm[:, 0:(NS - 1) * (C0 + 1) + 1:C0 + 1], qe[:, 0:NS]).then_inc(qm_ready, 1)
                    dve.wait_ge(tb_done, e + 1)
                    dve.tensor_tensor(km[:, :, :], TB[0:C0, 0:P].unsqueeze(1).to_broadcast([C0, NS + 1, P]),
                                      rowsel[:, :].unsqueeze(2).to_broadcast([C0, NS + 1, P]),
                                      ALU.mult).then_inc(km_ready, 1)

            def stage_b(u, s):
                e, n = ev(u, s), step_cols(s)[1]
                sizes, off = gla_levels(s)
                nl = len(sizes)
                g, mk = (G0, mask0) if s == 0 else (G, mask)
                if e:
                    dve.wait_ge(o_done, e)
                part = 60 * u + (7 * s - 3 if s else 0)
                for li in range(nl):
                    if li % 4 == 0:
                        dve.wait_ge(levels, 2 * e + li // 4 + 1)
                    if li:
                        dve.wait_ge(attn_part, part + li)
                    dve.copy_predicated(g[:, :], mk[:, li, :].bitcast(I32),
                                        L[li // 4][0:n, (li % 4) * P:(li % 4) * P + n]).then_inc(attn_part, 1)
                dve.wait_ge(attn_part, part + nl)
                dve.wait_ge(levels, 2 * e + 2)
                dve.copy_predicated(g[:, :], ident[0:n, 0:n].bitcast(I32),
                                    L1[0:n, 3 * P:3 * P + n]).then_inc(attn, 1)
                if s == 0:
                    for i in range(4 * u, 4 * u + 4):
                        dve.wait_ge(ss_prod, i + 1)
                        for b in range(2):
                            c = 2 * (i % 4) + b
                            dve.scalar_tensor_tensor(out=ss[:, i % 2, b, :], in0=ss[:, i % 2, b, :],
                                                     scalar=eb[:, c:c + 1], in1=X[:, b * HV:(b + 1) * HV],
                                                     op0=ALU.mult, op1=ALU.add).then_inc(ss_new, 1)
                    if e:
                        dve.wait_ge(s_saved, 16 * u)
                    dve.wait_ge(s_prod, e + 1)
                    dve.tensor_copy(S[:, :], TB[:, P:P + HV]).then_inc(s_new, 1)
                else:
                    dve.wait_ge(s_prod, e + 1)
                    dve.scalar_tensor_tensor(out=S[:, :], in0=S[:, :], scalar=eb[:, n - 1:n],
                                             in1=TB[:, P:P + HV], op0=ALU.mult, op1=ALU.add).then_inc(s_new, 1)

            def stage_c(u, s):
                e, n = ev(u, s), step_cols(s)[1]
                dve.wait_ge(o_scaled, e + 1)
                if e:
                    dve.wait_ge(o_turned, e)
                dve.tensor_tensor(og[0:n, :], on[0:n, :], TA[0:n, HV:2 * HV], ALU.mult).then_inc(o_gated, 1)
                dve.wait_ge(ot_hi, e + 1)
                if e:
                    dve.wait_ge(out_done, 2 * e)
                dve.tensor_tensor(otlo[:, :, 0:n], O[:, 0:2 * n].rearrange("p (a c) -> p a c", a=2),
                                  othi[:, :, 0:n].bitcast(F32), ALU.subtract).then_inc(ot_lo, 1)

            def stage_d(u, s):
                e, n = ev(u, s), step_cols(s)[1]
                for half in range(2):
                    dve.wait_ge(out_done, 2 * e + half + 1)
                    dst = y[0:n, s, 512 * half:512 * half + 512]
                    if u == 0:
                        dve.tensor_copy(dst, L[half][0:n, :]).then_inc(added, 1)
                    else:
                        dve.tensor_tensor(dst, dst, L[half][0:n, :], ALU.add).then_inc(added, 1)

            for task in order:
                if task[0] == "split":
                    W.low(dve, m, task[1], w_hi, w_lo)
                elif task[0] == "evac":
                    evac(task[1])
                elif task[0] in ("A", "B", "C", "D"):
                    {"A": stage_a, "B": stage_b, "C": stage_c, "D": stage_d}[task[0]](*task[1:])

        @block.tensor
        def _(pe):
            def piece(i):
                t, g = pieces[i]
                if g == 0:
                    pe.wait_ge(w_lo, W.index[("in", t)] + 1)
                if i >= 2:
                    pe.wait_ge(staged[i % 2], i // 2)
                last = project_piece(pe, m, t, g, PR[i % 2])
                last.then_inc(piece_done, 1)

            def stage_a(u, s):
                e, n = ev(u, s), step_cols(s)[1]
                x = tokens(u, s)
                pe.wait_ge(ck_in[e % 2], 16 * (e // 2 + 1))
                if e:
                    pe.wait_ge(o_gated, e)
                for j in range(4):
                    last = pe.transpose(TA[0:n, j * P:(j + 1) * P], x[:, 3 + j, :], ident[:, :])
                last.then_inc(ta_done, 1)
                if e:
                    pe.wait_ge(s_new, e)
                if s == 0:
                    pe.wait_ge(k_ready0, 2 * (u + 1))
                    pe.transpose(TB[0:n, 0:P], kd0[:, :], ident[:, :]).then_inc(tb_done, 1)
                else:
                    pe.wait_ge(k_ready, e + 1)
                    pe.transpose(TB[0:n, 0:P], E[:, 7, :], ident[:, :]).then_inc(tb_done, 1)

            def stage_b(u, s):
                e, n = ev(u, s), step_cols(s)[1]
                x = tokens(u, s)
                nl = len(gla_levels(s)[0])
                pe.wait_ge(q_ready, e + 1)
                pe.wait_ge(k_ready, e + 1)
                if e:
                    pe.wait_ge(added, 2 * e)
                for half in range(2):
                    for li in range(4 * half, min(4 * half + 4, nl)):
                        last = pe.matmul(L[half][0:n, (li % 4) * P:(li % 4) * P + n], E[:, li, 0:n],
                                         Eq[:, li, 0:n], start=True, stop=True)
                    if half:
                        last = pe.matmul(L1[0:n, 3 * P:3 * P + n], x[:, 1, :], x[:, 0, :],
                                         start=True, stop=True)
                    last.then_inc(levels, 1)
                if e:
                    pe.wait_ge(ot_lo, e)
                pe.wait_ge(qi_ready, e + 1)
                pe.wait_ge(v_turned, e + 1)
                if s == 0:
                    pe.wait_ge(qm_ready, u + 1)
                    pe.wait_ge(km_ready, u + 1)
                    for i in range(4 * u, 4 * u + 4):
                        pe.wait_ge(ss_in[i % 2], 16 * (i // 2 + 1))
                        for b in range(2):
                            c = 2 * (i % 4) + b
                            last = pe.matmul(O[0:n, 0:HV], qm[:, c * C0:(c + 1) * C0], ss[:, i % 2, b, :],
                                             start=(c == 0), stop=False)
                        last.then_inc(ss_inter, 1)
                        if i:
                            pe.wait_ge(ss_new, 2 * i)
                        for b in range(2):
                            c = 2 * (i % 4) + b
                            last = pe.matmul(X[:, b * HV:(b + 1) * HV], km[:, c, :], vt[0:n, :],
                                             start=True, stop=True)
                        last.then_inc(ss_prod, 1)
                    pe.matmul(TB[:, P:P + HV], km[:, NS, :], vt[0:n, :], start=True, stop=True).then_inc(s_prod, 1)
                else:
                    pe.wait_ge(k_turned, e + 1 - (u + 1))
                    pe.wait_ge(s_new, e)
                    pe.matmul(O[0:n, 0:HV], qe[:, :], S[:, :], start=True, stop=False)
                    pe.matmul(TB[:, P:P + HV], kt[:, :], vt[:, :], start=True, stop=True).then_inc(s_prod, 1)
                pe.wait_ge(attn, e + 1)
                g = G0 if s == 0 else G
                last = pe.matmul(O[0:n, 0:HV], g[:, :], vt[0:n, :], start=False, stop=True)
                last.then_inc(o_done, 1)

            def stage_c(u, s):
                e, n = ev(u, s), step_cols(s)[1]
                pe.wait_ge(o_gated, e + 1)
                for j in range(2):
                    last = pe.transpose(O[:, j * n:(j + 1) * n], og[0:n, j * P:(j + 1) * P], ident[0:n, 0:n])
                last.then_inc(o_turned, 1)

            def stage_d(u, s):
                e = ev(u, s)
                pe.wait_ge(ot_lo, e + 1)
                pe.wait_ge(w_lo, W.index[("out", u * WT + WT - 1)] + 1)
                pe.wait_ge(attn, e + 1)
                for half in range(2):
                    out_products(pe, m, (othi, otlo), WT, half, L[half]).then_inc(out_done, 1)

            for task in order:
                if task[0] == "piece":
                    piece(task[1])
                elif task[0] in ("A", "B", "C", "D"):
                    {"A": stage_a, "B": stage_b, "C": stage_c, "D": stage_d}[task[0]](*task[1:])


def ssd_step_sizes(nc, m, t, w_in, dt_bias, a_log, d_skip, state_conv, acd, conv_sample):
    w, raw, banks, ident = m["w"], m["raw"], m["banks"], m["ident"]
    c0 = SSD_COLS["dt"]
    with ExitStack() as ctx:
        def sb(name, shape):
            return ctx.enter_context(nc.sbuf_tensor("d_" + name, shape, F32))

        def sem(name):
            return nc.alloc_semaphore("d_" + name)

        bias, alog, aexp = sb("bias", [SH, 1]), sb("alog", [SH, 1]), sb("aexp", [SH, 1])
        mask = sb("mask", [SH, T])
        t1, t2, ac = sb("t1", [SH, T]), sb("t2", [SH, T]), sb("ac", [SH, T])
        sel = sb("sel", [SH, DI])
        ea = sb("ea", [SH, NS])
        cs = sb("conv_rows", [3 * NS, CONV])
        (w_raw, small_in, made, zeroed, w_hi, w_lo, projected, aexped, absd, capped, exped, logged,
         dt_done, a_done, scanned, ea_done, turned, kept, conv_in, d_in, stored) = (
            sem(x) for x in ("w_raw", "small_in", "made", "zeroed", "w_hi", "w_lo", "projected", "aexped",
                             "absd", "capped", "exped", "logged", "dt_done", "a_done", "scanned",
                             "ea_done", "turned", "kept", "conv_in", "d_in", "stored"))
        moved = m["conv_old_out"]
        block = ctx.enter_context(nc.Block())
        r = raw[:, 0, 0:KT * SH].rearrange("p (k f) -> p k f", k=KT)
        DTB, ACB, EB, C1, C2 = banks[3], banks[4], banks[5], banks[6], banks[7]

        @block.sync
        def _(sp):
            sp.dma_start(r, w_in[0, :, c0:c0 + SH].rearrange("(k p) f -> p k f", p=P)).then_inc(w_raw, 16)
            sp.dma_start(bias[:, :], dt_bias.rearrange("a h -> h a")).then_inc(small_in, 16)
            sp.dma_start(alog[:, :], a_log.rearrange("a h -> h a")).then_inc(small_in, 16)
            for i in range(3):
                sp.dma_start(cs[NS * i:NS * i + NS, :], state_conv[0, :, i, :]).then_inc(conv_in, 16)
            sp.dma_start(t["dskip"][:, :], d_skip.to_broadcast([P, SH])).then_inc(d_in, 16)
            sp.dma_start(conv_sample[0, :, 0:2, :], state_conv[0, :, 1:3, :]).then_inc(moved, 16)
            sp.wait_ge(scanned, 1)
            sp.dma_start(acd, ac[:, :]).then_inc(stored, 16)
            sp.wait_ge(stored, 16)
            sp.wait_ge(moved, 16)
            sp.wait_ge(d_in, 16)

        @block.gpsimd
        def _(pool):
            pool.memset(w[:, 0, 0, :, :].bitcast(F32), 0.0).then_inc(zeroed, 1)
            pool.memset(w[:, 0, 1, :, :].bitcast(F32), 0.0).then_inc(zeroed, 1)
            n = reset_mask(pool, mask[:, :], made, 0)
            pool.memset(sel[:, :], 1.0).then_inc(made, 1)
            pool.wait_ge(made, n + 1)
            pool.affine_select(out=sel[:, :], in_=sel[:, :], compare_op=ALU.is_ge, fill=0.0, base=0,
                               pattern=[[1, DI]], channel_multiplier=-HD).then_inc(made, 1)
            pool.wait_ge(made, n + 2)
            pool.affine_select(out=sel[:, :], in_=sel[:, :], compare_op=ALU.is_ge, fill=0.0, base=HD - 1,
                               pattern=[[-1, DI]], channel_multiplier=HD).then_inc(made, 1)

        @block.scalar
        def _(act):
            act.wait_ge(zeroed, 2)
            act.wait_ge(w_raw, 16)
            act.activation(w[:, 0, 0, :, 0:SH], r, ACT.Copy).then_inc(w_hi, 1)
            act.wait_ge(small_in, 32)
            act.activation(aexp[:, :], alog[:, :], ACT.Exp).then_inc(aexped, 1)
            for g, (c, n) in enumerate(CGS):
                act.wait_ge(projected, g + 1)
                act.activation(t1[:, c:c + n], banks[g][0:SH, 0:n], ACT.Abs, bias=bias[:, :]).then_inc(absd, 1)
            act.wait_ge(absd, 3)
            act.activation(t1[:, :], t1[:, :], ACT.Exp, scale=-1.0).then_inc(exped, 1)
            act.wait_ge(exped, 1)
            act.activation(t1[:, :], t1[:, :], ACT.Ln, bias=1.0).then_inc(logged, 1)
            act.wait_ge(scanned, 1)
            act.activation(ea[:, :], ac[:, 0:NS], ACT.Exp).then_inc(ea_done, 1)
            act.wait_ge(turned, 1)
            for c, bank in enumerate((C1, C2)):
                act.activation(t["sc"][:, 12 * c:12 * c + 12, :, :],
                               bank[:, 0:12 * 24].rearrange("p (a i b) -> p a i b", a=12, i=3),
                               ACT.Copy).then_inc(kept, 1)
            act.wait_ge(turned, 2)
            for q, n in ((slice(0, 1), C0), (slice(1, STEPS), P)):
                def view(bank):
                    return bank[0:n, 0:STEPS * SH].rearrange("p (s h) -> p s h", h=SH)[:, q, :]
                act.activation(t["dt"][0:n, q, :], view(DTB), ACT.Copy).then_inc(kept, 1)
                act.activation(t["ac"][0:n, q, :], view(ACB), ACT.Copy).then_inc(kept, 1)
            act.activation(t["ecol"][:, :, :], EB[:, 0:P].rearrange("p (a b) -> p a b", a=16),
                           ACT.Copy).then_inc(kept, 1)
            act.wait_ge(kept, 7)

        @block.vector
        def _(dve):
            dve.wait_ge(w_hi, 1)
            dve.tensor_tensor(w[:, 0, 1, :, 0:SH], r, w[:, 0, 0, :, 0:SH].bitcast(F32),
                              ALU.subtract).then_inc(w_lo, 1)
            dve.wait_ge(small_in, 32)
            for g, (c, n) in enumerate(CGS):
                dve.wait_ge(absd, g + 1)
                dve.tensor_scalar(t2[:, c:c + n], banks[g][0:SH, 0:n], bias[:, :], 0.0, ALU.add,
                                  ALU.max).then_inc(capped, 1)
            dve.wait_ge(capped, 3)
            dve.wait_ge(logged, 1)
            dve.tensor_tensor(t2[:, :], t2[:, :], t1[:, :], ALU.add).then_inc(dt_done, 1)
            dve.wait_ge(dt_done, 1)
            dve.wait_ge(aexped, 1)
            dve.tensor_scalar(t1[:, :], t2[:, :], aexp[:, :], -1.0, ALU.mult, ALU.mult).then_inc(a_done, 1)
            dve.wait_ge(a_done, 1)
            dve.wait_ge(made, 1 + STEPS)
            dve.tensor_tensor_scan(ac[:, :], mask[:, :], t1[:, :], 0.0, ALU.mult, ALU.add).then_inc(scanned, 1)

        @block.tensor
        def _(pe):
            narrow_projection(pe, m, SH, w_lo, None, projected)
            pe.wait_ge(conv_in, 48)
            for a in range(24):
                bank = (C1, C2)[a // 12]
                last = pe.transpose(bank[:, (a % 12) * 24:(a % 12) * 24 + 24], cs[:, a * P:(a + 1) * P],
                                    ident[0:24, 0:24])
            last.then_inc(turned, 1)
            pe.wait_ge(dt_done, 1)
            pe.wait_ge(scanned, 1)
            pe.wait_ge(ea_done, 1)
            pe.wait_ge(made, 1 + STEPS + 3)
            for s in range(STEPS):
                c, n = step_cols(s)
                pe.transpose(DTB[0:n, s * SH:(s + 1) * SH], t2[:, c:c + n], ident[0:SH, 0:SH])
                pe.transpose(ACB[0:n, s * SH:(s + 1) * SH], ac[:, c:c + n], ident[0:SH, 0:SH])
            for a in range(16):
                last = pe.matmul(EB[:, a * NS:(a + 1) * NS], sel[:, a * P:(a + 1) * P], ea[:, :],
                                 start=True, stop=True)
            last.then_inc(turned, 1)


def ssd_layer(nc, m, tab, sq, acd, w_in, w_out, state, state_prompt, state_sample, conv_prompt,
              conv_sample):
    NT, WT = 10, 4
    convs = set(range(6))
    order, pieces, weights, last_piece = interleave(NT, convs, WT, 5)

    def column(t):
        g, j = divmod(t, NT)
        if j < 4:
            return SSD_COLS["x"] + g * 512 + j * P
        if j < 6:
            return SSD_COLS["B" if j == 4 else "C"] + g * P
        return SSD_COLS["z"] + g * 512 + (j - 6) * P

    def channel(t):
        g, j = divmod(t, NT)
        return 4 * g + j if j < 4 else 16 + 4 * (j - 4) + g

    W = Weights(weights, pieces, w_in[0], w_out[0], column, NT, WT, 0)
    PA, PB, X, Z, M, Y1, Y2, SU = m["banks"]
    PR, Y, ident, y_acc = (PA, PB), (Y1, Y2), m["ident"], m["y"]
    conv_index = {p: i for i, p in enumerate(p for p in pieces if p[0] % NT in convs and p[1] < 3)}
    where = {p: i for i, p in enumerate(pieces)}
    rows_before = [[], []]
    for i, (t, g) in enumerate(pieces):
        for par in range(2):
            rows_before[par].append((rows_before[par][-1] if i else 0) +
                                    (1 if i and (i - 1) % 2 == par and pieces[i - 1][1] < 3 else 0))

    def tile_index(t):
        return 6 * (t // NT) + t % NT

    with ExitStack() as ctx:
        def sb(name, shape, dt=F32):
            return ctx.enter_context(nc.sbuf_tensor("s_" + name, shape, dt))

        def sem(name):
            return nc.alloc_semaphore("s_" + name)

        pre = sb("pre", [P, 2, 353])
        cu = sb("conv", [P, 2, 350])
        th = sb("tanh", [P, 2, 350])
        cvp, cvo = sb("cv_cols", [P, 2, 11]), sb("cv_rows", [11, P])
        ck = sb("chunk", [P, 2, 6, P])
        zc = sb("z", [P, 4, P])
        acb = sb("decay", [P, 2, HPG, P])
        el, wl, ea = sb("e_last", [P, HPG]), sb("w_last", [P, HPG]), sb("e_sum", [P, HPG])
        bt, cbm = sb("b_turned", [P, P]), sb("cb", [P, P])
        xdt, xw, y = sb("xdt", [P, 512]), sb("xw", [P, 512]), sb("ys", [P, 512])
        ythi, ytlo = sb("yt_hi", [P, 4, P], F32R), sb("yt_lo", [P, 4, P], F32R)
        S = sb("state", [P, 512])
        cm = sb("c_masked", [P, NS * C0])
        bm = sb("b_masked", [C0, P])
        meta_row = sb("meta_row", [C0, 1])
        ss = sb("sample_state", [P, 2, 4, P])
        ysum, ymean, yrstd, power = (sb(x, [P, 1]) for x in ("ysum", "ymean", "yrstd", "power"))

        raw_in = [sem(f"raw_in{i}") for i in range(2)]
        bank_free = [sem(f"bank_free{i}") for i in range(2)]
        stored = [sem(f"stored{i}") for i in range(2)]
        cv_stored, s_saved = m["conv_out"], m["ssm_state_out"]
        ck_in = [sem(f"ck_in{i}") for i in range(2)]
        acb_in = [sem(f"acb_in{i}") for i in range(2)]
        ss_in = [sem(f"ss_in{i}") for i in range(2)]
        ss_out = [m[f"ssm_sample_out{i}"] for i in range(2)]
        (w_hi, w_lo, piece_done, z_in, convolved, tanhed, silued, cv_packed, consts, zeros, chain) = (
            sem(x) for x in ("w_hi", "w_lo", "piece_done", "z_in", "convolved", "tanhed", "silued",
                             "cv_packed", "consts", "zeros", "chain"))
        gaps = sem("gaps")
        (turned, b_turned, el_done, decays, cb_masked, xdt_ready, xw_ready, attn, intra, inter, s_prod,
         s_new, y_summed, z_turned, gated, squared, meant, rooted, y_normed, y_turned, yt_hi, yt_lo,
         out_done, added) = (sem(x) for x in (
             "turned", "b_turned", "el_done", "decays", "cb_masked", "xdt_ready", "xw_ready", "attn",
             "intra", "inter", "s_prod", "s_new", "y_summed", "z_turned", "gated", "squared", "meant",
             "rooted", "y_normed", "y_turned", "yt_hi", "yt_lo", "out_done", "added"))
        (cm_ready, bm_ready, ss_turned, ss_copied, ss_inter, ss_prod, ss_new, s_turned, s_kept) = (sem(x) for x in ("cm_ready", "bm_ready", "ss_turned", "ss_copied", "ss_inter",
                                      "ss_prod", "ss_new", "s_turned", "s_kept"))
        block = ctx.enter_context(nc.Block())

        def ev(u, s):
            return u * STEPS + s

        def tokens(u, s):
            return ck[:, ev(u, s) % 2, :, 0:step_cols(s)[1]]

        def decay(u, s):
            return acb[:, ev(u, s) % 2, :, 0:step_cols(s)[1]]

        def tanh_count(i):
            return tanh_order[i] + 1

        tanh_order = {}
        for task in order:
            if task[0] in ("evac", "finish"):
                j, g = pieces[task[1]][0] % NT, pieces[task[1]][1]
                if g < 3 and (j in convs) == (task[0] == "finish"):
                    tanh_order[task[1]] = len(tanh_order)

        @block.sync
        def _(sp):
            def store(i):
                t, g = pieces[i]
                u, j = divmod(t, NT)
                if g == 3:
                    q, a = tile_index(t), channel(t)
                    sp.wait_ge(bank_free[i % 2], i // 2 + 1)
                    sp.dma_start(conv_prompt[0, 0, :, a * P:(a + 1) * P],
                                 cvo[0:3, :]).then_inc(cv_stored, 16)
                    sp.dma_start(conv_sample[0, :, 2, a * P:(a + 1) * P],
                                 cvo[3:11, :]).then_inc(cv_stored, 16)
                    return
                c, n = CGS[g]
                if j in convs:
                    sp.wait_ge(silued, conv_index[(t, g)] + 1)
                else:
                    sp.wait_ge(bank_free[i % 2], i // 2 + 1)
                sp.dma_start(sq[u, j * P:(j + 1) * P, c:c + n], th[:, i % 2, 0:n]).then_inc(stored[i % 2], 16)

            def load(u, s):
                e = ev(u, s)
                c, n = step_cols(s)
                if s == 0:
                    for par in range(2):
                        n_rows = rows_before[par][last_piece[u]] + (1 if last_piece[u] % 2 == par and
                                                                    pieces[last_piece[u]][1] < 3 else 0)
                        sp.wait_ge(stored[par], 16 * n_rows)
                if e >= 2:
                    sp.wait_ge(intra, e - 1)
                    sp.wait_ge(s_prod, e - 1)
                    if s in (1, 2):
                        sp.wait_ge(cm_ready, u + 1 if s == 2 else max(u, 0))
                sp.dma_start(tokens(u, s), sq[u, 0:6 * P, c:c + n].rearrange("(t p) c -> p t c", p=P)).then_inc(
                    ck_in[e % 2], 16)
                sp.dma_start(decay(u, s), acd[HPG * u:HPG * u + HPG, c:c + n].unsqueeze(0).to_broadcast(
                    [P, HPG, n])).then_inc(acb_in[e % 2], 16)

            def load_z(u, s):
                e = ev(u, s)
                c, n = step_cols(s)
                if e:
                    sp.wait_ge(z_turned, e)
                sp.dma_start(zc[:, :, 0:n], sq[u, 6 * P:10 * P, c:c + n].rearrange("(t p) c -> p t c", p=P)).then_inc(
                    z_in, 16)

            def sample_state(i, out):
                u, b = divmod(i, NS)
                view = (state_sample if out else state)[0, b, HPG * u:HPG * u + HPG].rearrange(
                    "(t two) p n -> (two p) t n", two=2)
                if out:
                    sp.wait_ge(ss_new, i + 1)
                    sp.dma_start(view, ss[:, i % 2, :, :]).then_inc(ss_out[i % 2], 16)
                else:
                    if i >= 2:
                        sp.wait_ge(ss_out[i % 2], 16 * (i // 2))
                    if i and i % NS < 1:
                        sp.wait_ge(s_saved, 16 * u)
                    sp.dma_start(ss[:, i % 2, :, :], view).then_inc(ss_in[i % 2], 16)

            W.load(sp, m, 0, raw_in, w_lo)
            W.load(sp, m, 1, raw_in, w_lo)
            for task in order:
                if task[0] == "split" and task[1] + 2 < len(weights):
                    W.load(sp, m, task[1] + 2, raw_in, w_lo)
                elif task[0] == "store":
                    store(task[1])
                elif task[0] == "load":
                    load(*task[1:])
                elif task[0] == "A":
                    load_z(*task[1:])
                elif task[0] == "B" and task[2] == 0:
                    first = NS * task[1]
                    for i in range(first, first + NS):
                        sample_state(i, False)
                        if i > first:
                            sample_state(i - 1, True)
                    sample_state(first + NS - 1, True)
                elif task[0] == "E":
                    u = task[1]
                    sp.wait_ge(s_kept, u + 1)
                    sp.dma_start(state_prompt[0, 0, HPG * u:HPG * u + HPG].rearrange(
                        "(t two) p n -> (two p) t n", two=2), ss[:, 0, :, :]).then_inc(s_saved, 16)
            sp.wait_ge(s_saved, 16 * U)
            sp.wait_ge(cv_stored, 32 * 6 * U)
            for i in range(2):
                sp.wait_ge(ss_out[i], 16 * U * NS // 2)
                sp.wait_ge(stored[i], 16 * (rows_before[i][-1] + (1 if (len(pieces) - 1) % 2 == i and
                                                                  pieces[-1][1] < 3 else 0)))

        @block.gpsimd
        def _(pool):
            pool.memset(meta_row[:, :], 1.0).then_inc(consts, 1)
            pool.memset(power[:, :], -0.5).then_inc(consts, 1)
            pool.wait_ge(consts, 2)
            pool.affine_select(out=meta_row[:, :], in_=meta_row[:, :], compare_op=ALU.is_ge,
                               fill=0.0, base=-NS, pattern=[[0, 1]], channel_multiplier=1).then_inc(consts, 1)
            for e in range(U * STEPS):
                n = step_cols(e % STEPS)[1]
                pool.wait_ge(squared, e + 1)
                pool.tensor_scalar(ymean[0:n, :], ysum[0:n, :], 1.0 / 512, 4 * EPS, ALU.mult,
                                   ALU.add).then_inc(meant, 1)
                pool.wait_ge(meant, e + 1)
                if e:
                    pool.wait_ge(y_normed, e)
                pool.tensor_tensor(yrstd[0:n, :], ymean[0:n, :], power[0:n, :], ALU.pow).then_inc(rooted, 1)

        @block.scalar
        def _(act):
            def evac(i):
                t, g = pieces[i]
                j = t % NT
                act.wait_ge(piece_done, i + 1)
                bank = PR[i % 2]
                if g == 3:
                    q = tile_index(t)
                    if q:
                        act.wait_ge(cv_stored, 32 * q)
                    act.activation(cvo[:, :], bank[0:11, 0:P], ACT.Copy).then_inc(bank_free[i % 2], 1)
                elif j in convs:
                    c, n = CGS[g]
                    ci, q = conv_index[(t, g)], tile_index(t)
                    if ci >= 2:
                        act.wait_ge(convolved, ci - 1)
                    if ci >= 1 and g == 0:
                        act.wait_ge(cv_packed, q)
                    if g == 0:
                        if q >= 2:
                            act.wait_ge(piece_done, where[(prev_tile[prev_tile[t]], 3)] + 1)
                        act.activation(cvp[:, q % 2, 3:11], bank[:, 0:NS], ACT.Copy)
                        act.activation(pre[:, ci % 2, 3:3 + n - NS], bank[:, NS:n],
                                       ACT.Copy).then_inc(bank_free[i % 2], 1)
                    else:
                        if g == 2:
                            act.wait_ge(convolved, ci)
                        act.activation(pre[:, ci % 2, 3:3 + n], bank[:, 0:n],
                                       ACT.Copy).then_inc(bank_free[i % 2], 1)
                else:
                    n = CGS[g][1]
                    act.wait_ge(stored[i % 2], 16 * rows_before[i % 2][i])
                    act.activation(th[:, i % 2, 0:n], bank[:, 0:n], ACT.Tanh, scale=0.5).then_inc(tanhed, 1)

            prev_tile, last = {}, None
            for t in range(U * NT):
                if t % NT in convs:
                    prev_tile[t] = last
                    last = t

            def finish(i):
                t, g = pieces[i]
                if t % NT not in convs or g == 3:
                    return
                n = CGS[g][1]
                act.wait_ge(convolved, conv_index[(t, g)] + 1)
                act.wait_ge(stored[i % 2], 16 * rows_before[i % 2][i])
                act.activation(th[:, i % 2, 0:n], cu[:, i % 2, 0:n], ACT.Tanh).then_inc(tanhed, 1)

            def stage_a(u, s):
                e, n = ev(u, s), step_cols(s)[1]
                L = decay(u, s)
                act.wait_ge(acb_in[e % 2], 16 * (e // 2 + 1))
                if e:
                    act.wait_ge(s_new, e)
                    act.wait_ge(y_summed, e)
                act.activation(ea[0:n, :], tab["ac"][0:n, s, HPG * u:HPG * u + HPG], ACT.Exp)
                act.activation(el[:, :].unsqueeze(2), L[:, :, n - 1:n], ACT.Exp).then_inc(el_done, 1)
                act.wait_ge(el_done, e + 1)
                for r in range(HPG):
                    h = HPG * u + r
                    last = act.activation(L[0:n, r, :], L[0:n, r, :], ACT.Relu, scale=-1.0,
                                          bias=tab["ac"][0:n, s, h:h + 1])
                last.then_inc(gaps, 1)
                act.wait_ge(gaps, e + 1)
                act.activation(L[0:n], L[0:n], ACT.Exp, scale=-1.0).then_inc(decays, 1)
                act.wait_ge(turned, e + 1)
                if e:
                    act.wait_ge(s_prod, e)
                act.activation(bt[0:n, :], M[0:n, 0:P], ACT.Copy).then_inc(b_turned, 1)

            def stage_b(u, s):
                if s:
                    return
                e = ev(u, s)
                if e:
                    act.wait_ge(y_turned, e)
                for i in range(NS * u, NS * u + NS):
                    act.wait_ge(ss_turned, i + 1)
                    if i % NS:
                        act.wait_ge(ss_inter, i - u)
                    act.activation(y[:, :], SU[:, :], ACT.Copy).then_inc(ss_copied, 1)

            def stage_c(u, s):
                e, n = ev(u, s), step_cols(s)[1]
                act.wait_ge(gated, e + 1)
                if e:
                    act.wait_ge(rooted, e)
                    act.wait_ge(yt_lo, e)
                    act.wait_ge(out_done, 2 * e)
                act.activation(ythi[0:n, :, :], y[0:n, :].rearrange("p (a b) -> p a b", a=4),
                               ACT.Square, accum_out=ysum[0:n, :]).then_inc(squared, 1)
                act.wait_ge(rooted, e + 1)
                act.activation(y[0:n, :], y[0:n, :], ACT.Copy, scale=yrstd[0:n, :]).then_inc(y_normed, 1)
                act.wait_ge(y_turned, e + 1)
                act.activation(ythi[:, :, 0:n], X[:, 0:4 * n].rearrange("p (a c) -> p a c", a=4),
                               ACT.Copy).then_inc(yt_hi, 1)

            def stage_e(u):
                act.wait_ge(s_turned, u + 1)
                act.wait_ge(ss_out[0], 16 * (u + 1) * NS // 2)
                act.activation(ss[:, 0, :, :], Z[:, :].rearrange("p (a n) -> p a n", a=4),
                               ACT.Copy).then_inc(s_kept, 1)

            act.wait_ge(zeros, 3)
            for task in order:
                if task[0] == "split":
                    W.high(act, m, task[1], raw_in, w_hi, piece_done, out_done)
                elif task[0] in stages_of(act, evac, finish, stage_a, stage_b, stage_c, None, stage_e):
                    stages_of(act, evac, finish, stage_a, stage_b, stage_c, None, stage_e)[task[0]](*task[1:])

        @block.vector
        def _(dve):
            links = [0]

            def link(ins):
                links[0] += 1
                ins.then_inc(chain, 1)
                dve.wait_ge(chain, links[0])

            dve.memset(ythi[:, :, :].bitcast(F32), 0.0).then_inc(zeros, 1)
            dve.memset(ytlo[:, :, :].bitcast(F32), 0.0).then_inc(zeros, 1)
            dve.memset(cm[:, :], 0.0).then_inc(zeros, 1)
            dve.wait_ge(zeros, 3)
            dve.wait_ge(consts, 3)
            cw = m["cw"]

            def evac(i):
                t, g = pieces[i]
                j, n = t % NT, CGS[min(g, 2)][1]
                if g == 3:
                    return
                if j not in convs:
                    dve.wait_ge(tanhed, tanh_count(i))
                    dve.scalar_tensor_tensor(out=th[:, i % 2, 0:n], in0=th[:, i % 2, 0:n], scalar=1.0,
                                             in1=PR[i % 2][:, 0:n], op0=ALU.add,
                                             op1=ALU.mult).then_inc(bank_free[i % 2], 1)
                    return
                ci, q, a = conv_index[(t, g)], tile_index(t), channel(t)
                p, u = pre[:, ci % 2, :], cu[:, i % 2, :]
                dve.wait_ge(bank_free[i % 2], i // 2 + 1)
                if ci >= 1:
                    dve.wait_ge(silued, done_before(i))
                off = NS if g == 0 else 0
                if g == 0:
                    link(dve.memset(p[:, 0:3], 0.0))
                else:
                    w = CGS[g - 1][1] - (NS if g == 1 else 0)
                    link(dve.tensor_copy(p[:, 0:3], pre[:, (ci + 1) % 2, w:w + 3]))
                if g == 2:
                    dve.tensor_copy(cvp[:, q % 2, 0:3], p[:, n:n + 3]).then_inc(cv_packed, 1)
                if g == 0:
                    old, new = tab["sc"][:, a, :, :], cvp[:, q % 2, 3:11]
                    taps = [old[:, 0, :], old[:, 1, :], old[:, 2, :], new]
                    link(dve.tensor_scalar(u[:, 0:NS], taps[0], cw[:, 0, a:a + 1], cw[:, 4, a:a + 1],
                                           ALU.mult, ALU.add))
                    for k in range(1, 4):
                        link(dve.scalar_tensor_tensor(out=u[:, 0:NS], in0=taps[k], scalar=cw[:, k, a:a + 1],
                                                      in1=u[:, 0:NS], op0=ALU.mult, op1=ALU.add))
                w = n - off
                link(dve.tensor_scalar(u[:, off:n], p[:, 0:w], cw[:, 0, a:a + 1], cw[:, 4, a:a + 1],
                                       ALU.mult, ALU.add))
                for k in range(1, 4):
                    ins = dve.scalar_tensor_tensor(out=u[:, off:n], in0=p[:, k:k + w],
                                                   scalar=cw[:, k, a:a + 1], in1=u[:, off:n],
                                                   op0=ALU.mult, op1=ALU.add)
                    if k < 3:
                        link(ins)
                    else:
                        ins.then_inc(convolved, 1)

            silu_order = []

            def done_before(i):
                return len([x for x in silu_order if x <= i - 2])

            def finish(i):
                t, g = pieces[i]
                if t % NT not in convs or g == 3:
                    return
                n = CGS[g][1]
                silu_order.append(i)
                dve.wait_ge(tanhed, tanh_count(i))
                dve.scalar_tensor_tensor(out=th[:, i % 2, 0:n], in0=th[:, i % 2, 0:n], scalar=1.0,
                                         in1=cu[:, i % 2, 0:n], op0=ALU.add, op1=ALU.mult).then_inc(silued, 1)

            def heads(x, n, w=HD):
                return x.unsqueeze(2).to_broadcast([n, HPG, w])

            def split_heads(x):
                return x.rearrange("p (r c) -> p r c", r=HPG)

            def stage_a(u, s):
                e, n = ev(u, s), step_cols(s)[1]
                L, x = decay(u, s), tokens(u, s)
                hs = slice(HPG * u, HPG * u + HPG)
                dve.wait_ge(b_turned, e + 1)
                tri = m["tri0"] if s == 0 else m["tri"]
                dve.tensor_tensor(cbm[0:n, 0:n], M[0:n, P:P + n], tri[:, :], ALU.mult).then_inc(cb_masked, 1)
                if e:
                    dve.wait_ge(intra, e)
                    dve.wait_ge(s_prod, e)
                    if s == 1:
                        dve.wait_ge(ss_prod, NS * (u + 1))
                    dve.wait_ge(y_summed, e)
                dve.tensor_tensor(split_heads(xdt[0:n, :]), split_heads(X[0:n, :]),
                                  heads(tab["dt"][0:n, s, hs], n), ALU.mult).then_inc(xdt_ready, 1)
                dve.wait_ge(decays, e + 1)
                dve.wait_ge(acb_in[e % 2], 16 * (e // 2 + 1))
                last = L[0:n, :, n - 1:n].rearrange("p r o -> p (r o)")
                if s:
                    link(dve.tensor_copy(wl[0:n, :], last))
                else:
                    link(dve.tensor_scalar(wl[0:n, :], last, meta_row[:, :], None, ALU.mult))
                dve.wait_ge(xdt_ready, e + 1)
                dve.tensor_tensor(split_heads(xw[0:n, :]), split_heads(xdt[0:n, :]), heads(wl[0:n, :], n),
                                  ALU.mult).then_inc(xw_ready, 1)
                dve.wait_ge(cb_masked, e + 1)
                dve.tensor_tensor(L[0:n], L[0:n], cbm[0:n, 0:n].unsqueeze(1).to_broadcast([n, HPG, n]),
                                  ALU.mult).then_inc(attn, 1)
                if s == 0:
                    dve.wait_ge(ck_in[e % 2], 16 * (e // 2 + 1))
                    dve.tensor_copy(cm[:, 0:(NS - 1) * (C0 + 1) + 1:C0 + 1], x[:, 5, 0:NS]).then_inc(cm_ready, 1)
                    mask_b(NS * u)

            def mask_b(i):
                if i:
                    dve.wait_ge(ss_prod, i)
                dve.tensor_scalar(bm[:, :], bt[0:C0, :], ident[0:C0, i % NS:i % NS + 1], None,
                                  ALU.mult).then_inc(bm_ready, 1)

            def stage_b(u, s):
                e, n = ev(u, s), step_cols(s)[1]
                hs = slice(HPG * u, HPG * u + HPG)
                if s == 0:
                    for i in range(NS * u, NS * u + NS):
                        b = i % NS
                        st = ss[:, i % 2, :, :]
                        dve.wait_ge(ss_turned, i + 1)
                        dve.wait_ge(ss_in[i % 2], 16 * (i // 2 + 1))
                        link(dve.tensor_tensor(st, st, tab["ecol"][:, 4 * u:4 * u + 4, b:b + 1].to_broadcast(
                            [P, 4, P]), ALU.mult))
                        dve.wait_ge(ss_prod, i + 1)
                        dve.tensor_tensor(st, st, Z[:, :].rearrange("p (a n) -> p a n", a=4),
                                          ALU.add).then_inc(ss_new, 1)
                        if b + 1 < NS:
                            mask_b(i + 1)
                    if u:
                        dve.wait_ge(s_turned, u)
                    dve.wait_ge(s_prod, e + 1)
                    dve.tensor_copy(S[:, :], SU[:, :]).then_inc(s_new, 1)
                else:
                    dve.wait_ge(s_prod, e + 1)
                    dve.wait_ge(el_done, e + 1)
                    link(dve.tensor_tensor(split_heads(S[:, :]), split_heads(S[:, :]), heads(el[:, :], P),
                                           ALU.mult))
                    dve.tensor_tensor(S[:, :], S[:, :], SU[:, :], ALU.add).then_inc(s_new, 1)
                dve.wait_ge(inter, e + 1)
                dve.wait_ge(el_done, e + 1)
                if e:
                    dve.wait_ge(y_turned, e)
                link(dve.tensor_tensor(split_heads(y[0:n, :]), split_heads(Y2[0:n, :]),
                                       heads(ea[0:n, :], n), ALU.mult))
                dve.wait_ge(intra, e + 1)
                link(dve.tensor_tensor(y[0:n, :], y[0:n, :], Y1[0:n, :], ALU.add))
                link(dve.tensor_tensor(split_heads(xw[0:n, :]), split_heads(X[0:n, :]),
                                       heads(tab["dskip"][0:n, hs], n), ALU.mult))
                dve.tensor_tensor(y[0:n, :], y[0:n, :], xw[0:n, :], ALU.add).then_inc(y_summed, 1)

            def stage_c(u, s):
                e, n = ev(u, s), step_cols(s)[1]
                dve.wait_ge(z_turned, e + 1)
                dve.wait_ge(y_summed, e + 1)
                dve.tensor_tensor(y[0:n, :], y[0:n, :], Z[0:n, :], ALU.mult).then_inc(gated, 1)
                dve.wait_ge(yt_hi, e + 1)
                dve.tensor_tensor(ytlo[:, :, 0:n], X[:, 0:4 * n].rearrange("p (a c) -> p a c", a=4),
                                  ythi[:, :, 0:n].bitcast(F32), ALU.subtract).then_inc(yt_lo, 1)

            def stage_d(u, s):
                e, n = ev(u, s), step_cols(s)[1]
                for half in range(2):
                    dve.wait_ge(out_done, 2 * e + half + 1)
                    dst = y_acc[0:n, s, 512 * half:512 * half + 512]
                    if u == 0:
                        dve.tensor_copy(dst, Y[half][0:n, :]).then_inc(added, 1)
                    else:
                        dve.tensor_tensor(dst, dst, Y[half][0:n, :], ALU.add).then_inc(added, 1)

            for task in order:
                if task[0] == "split":
                    W.low(dve, m, task[1], w_hi, w_lo)
                elif task[0] in stages_of(dve, evac, finish, stage_a, stage_b, stage_c, stage_d, None):
                    stages_of(dve, evac, finish, stage_a, stage_b, stage_c, stage_d, None)[task[0]](*task[1:])

        @block.tensor
        def _(pe):
            def piece(i):
                t, g = pieces[i]
                if g == 0:
                    pe.wait_ge(w_lo, W.index[("in", t)] + 1)
                if i >= 2:
                    pe.wait_ge(bank_free[i % 2], i // 2)
                if g == 3:
                    q = tile_index(t)
                    pe.wait_ge(cv_packed, q + 1)
                    pe.transpose(PR[i % 2][0:11, 0:P], cvp[:, q % 2, :], ident[:, :]).then_inc(piece_done, 1)
                else:
                    project_piece(pe, m, t, g, PR[i % 2]).then_inc(piece_done, 1)

            def stage_a(u, s):
                e, n = ev(u, s), step_cols(s)[1]
                x = tokens(u, s)
                pe.wait_ge(ck_in[e % 2], 16 * (e // 2 + 1))
                if e:
                    pe.wait_ge(yt_lo, e)
                    pe.wait_ge(cb_masked, e)
                for j in range(4):
                    pe.transpose(X[0:n, j * P:(j + 1) * P], x[:, j, :], ident[:, :])
                pe.transpose(M[0:n, 0:P], x[:, 4, :], ident[:, :])
                pe.matmul(M[0:n, P:P + n], x[:, 4, :], x[:, 5, :], start=True, stop=True).then_inc(turned, 1)

            def stage_b(u, s):
                e, n = ev(u, s), step_cols(s)[1]
                x, G = tokens(u, s), decay(u, s)
                if e:
                    pe.wait_ge(added, 2 * e)
                    pe.wait_ge(s_new, e)
                if s == 0:
                    pe.wait_ge(cm_ready, u + 1)
                    pe.wait_ge(xdt_ready, e + 1)
                    if u:
                        pe.wait_ge(s_kept, u)
                    for i in range(NS * u, NS * u + NS):
                        pe.wait_ge(ss_in[i % 2], 16 * (i // 2 + 1))
                        if i % NS:
                            pe.wait_ge(ss_copied, i)
                        for j in range(4):
                            last = pe.transpose(SU[:, j * P:(j + 1) * P], ss[:, i % 2, j, :], ident[:, :])
                        last.then_inc(ss_turned, 1)
                        pe.wait_ge(bm_ready, i + 1)
                        if i % NS:
                            pe.wait_ge(ss_new, i)
                        for j in range(4):
                            last = pe.matmul(Z[:, j * P:(j + 1) * P], xdt[0:n, j * P:(j + 1) * P],
                                             bm[:, :], start=True, stop=True)
                        last.then_inc(ss_prod, 1)
                        pe.wait_ge(ss_copied, i + 1)
                        pe.matmul(Y2[0:n, :], cm[:, (i % NS) * C0:(i % NS + 1) * C0], y[:, :], start=(i % NS == 0),
                                  stop=(i % NS == NS - 1)).then_inc(inter if i % NS == NS - 1 else ss_inter, 1)
                else:
                    pe.matmul(Y2[0:n, :], x[:, 5, :], S[:, :], start=True, stop=True).then_inc(inter, 1)
                pe.wait_ge(xw_ready, e + 1)
                pe.wait_ge(b_turned, e + 1)
                pe.matmul(SU[:, :], bt[0:n, :], xw[0:n, :], start=True, stop=True).then_inc(s_prod, 1)
                pe.wait_ge(attn, e + 1)
                for r in range(HPG):
                    last = pe.matmul(Y1[0:n, r * HD:(r + 1) * HD], G[0:n, r, :],
                                     xdt[0:n, r * HD:(r + 1) * HD], start=True, stop=True)
                last.then_inc(intra, 1)

            def stage_c(u, s):
                e, n = ev(u, s), step_cols(s)[1]
                pe.wait_ge(z_in, 16 * (e + 1))
                if e:
                    pe.wait_ge(gated, e)
                if s == 0:
                    pe.wait_ge(ss_new, NS * (u + 1))
                for j in range(4):
                    last = pe.transpose(Z[0:n, j * P:(j + 1) * P], zc[:, j, 0:n], ident[:, :])
                last.then_inc(z_turned, 1)
                pe.wait_ge(y_normed, e + 1)
                for j in range(4):
                    last = pe.transpose(X[:, j * n:(j + 1) * n], y[0:n, j * P:(j + 1) * P], ident[0:n, 0:n])
                last.then_inc(y_turned, 1)

            def stage_d(u, s):
                e = ev(u, s)
                pe.wait_ge(yt_lo, e + 1)
                pe.wait_ge(w_lo, W.index[("out", u * WT + WT - 1)] + 1)
                for half in range(2):
                    out_products(pe, m, (ythi, ytlo), WT, half, Y[half]).then_inc(out_done, 1)

            def stage_e(u):
                pe.wait_ge(s_new, STEPS * (u + 1))
                pe.wait_ge(gated, STEPS * (u + 1))
                for j in range(4):
                    last = pe.transpose(Z[:, j * P:(j + 1) * P], S[:, j * P:(j + 1) * P], ident[:, :])
                last.then_inc(s_turned, 1)

            for task in order:
                if task[0] == "piece":
                    piece(task[1])
                elif task[0] in stages_of(pe, None, None, stage_a, stage_b, stage_c, stage_d, stage_e):
                    stages_of(pe, None, None, stage_a, stage_b, stage_c, stage_d, stage_e)[task[0]](*task[1:])


def stages_of(engine, evac, finish, a, b, c, d, e):
    parts = {"evac": evac, "finish": finish, "A": a, "B": b, "C": c, "D": d, "E": e}
    return {name: part for name, part in parts.items() if part is not None}


_INS = ["x_prompt", "x_sample", "state_gla", "state_ssm", "state_conv", "meta_tokens", "pre_norm",
        "post_norm", "gla_w_in", "gla_w_gate_up", "gla_b_gate", "gla_w_norm", "gla_w_out", "ssd_w_in",
        "ssd_conv_w", "ssd_conv_b", "ssd_dt_bias", "ssd_a_log", "ssd_d_skip", "ssd_w_norm", "ssd_w_out"]
_OUTS = [(1, SEQ, D), (NS, 1, D), (1, 1, U, HK, HV), (1, 1, SH, HD, P), (1, 1, 3, CONV),
         (1, NS, U, HK, HV), (1, NS, SH, HD, P), (1, NS, 3, CONV)]


def kernel(**inputs):
    import numpy as _np
    import concourse.bacc as _bacc
    from concourse import mybir as _mybir
    from concourse.bass_utils import run_bass_kernel_spmd as _run

    nc = _bacc.Bacc("TRN2", target_bir_lowering=False, num_devices=1)
    arrays, args = {}, []
    for name in _INS:
        a = _np.ascontiguousarray(inputs[name])
        arrays[f"in_{name}_dram"] = a
        args.append(nc.dram_tensor(f"in_{name}_dram", a.shape, _mybir.dt.from_np(a.dtype), kind="ExternalInput").ap())
    for i, shape in enumerate(_OUTS):
        args.append(nc.dram_tensor(f"out_{i}_dram", shape, _mybir.dt.float32, kind="ExternalOutput").ap())
    hybrid_kernel(nc, *args)
    r = _run(nc, [arrays], core_ids=[0])
    return tuple(r.results[0][f"out_{i}_dram"] for i in range(len(_OUTS)))
```

```python
from contextlib import ExitStack

import concourse.bass as bass
from concourse import mybir

F32 = mybir.dt.float32
F32R = mybir.dt.float32r
I32 = mybir.dt.int32
ALU = mybir.AluOpType
ACT = mybir.ActivationFunctionType

P = 128
D = 1024
KT = D // P
NS = 8
NM = 16
SEQ = 1024
C0 = NS + NM
T = C0 + SEQ
STEPS = 1 + SEQ // P
EPS = 1e-6
U = 4
HK = 128
HV = 256
TAU = 16.0
GR = 16
SH = 32
HPG = 8
HD = 64
DI = 2048
CONV = 3072
CGS = [(0, 350), (350, 350), (700, 348)]
GLA_COLS = {"q": 0, "k": 512, "v": 1024, "r": 2048, "g": 3072}
SSD_COLS = {"z": 0, "x": 2048, "B": 4096, "C": 4608, "dt": 5120}


def step_cols(s):
    return (0, C0) if s == 0 else (C0 + P * (s - 1), P)


def gla_levels(s):
    return ([8, 4, 2, 1], NS) if s == 0 else ([64, 32, 16, 8, 4, 2, 1], 0)


PARTS = 4


def interleave(tiles, convs, wo_tiles, lead, first, later, between, after_last):
    pieces, late = [], None
    for t in range(U * tiles):
        for c in range(3):
            pieces.append((t, c))
            if c == 0 and late is not None:
                pieces.append((late, 3))
                late = None
        if t % tiles in convs:
            late = t
    if late is not None:
        pieces.append((late, 3))
    last = [max(i for i, (t, _) in enumerate(pieces) if t // tiles == u) for u in range(U)]
    order, weights = [], []
    at = 0

    def weight(w):
        weights.append(w)
        order.append(("split", len(weights) - 1))

    def part():
        nonlocal at
        i, p = divmod(at, PARTS)
        t, c = pieces[i]
        at += 1
        order.append(("piece", i, p))
        if p:
            return
        if c == 0 and t + 1 < U * tiles:
            weight(("in", t + 1))
        for lag, name in enumerate(("evac", "finish", "store"), 1):
            if i >= lag:
                order.append((name, i - lag))
        if c == 3:
            at += PARTS - 1
        if i + 1 == len(pieces):
            for p in range(p + 1, PARTS if c < 3 else 1):
                order.append(("piece", i, p))
            at = PARTS * len(pieces)
            order.extend([("evac", i), ("finish", i - 1), ("store", i - 2), ("finish", i),
                          ("store", i - 1), ("store", i)])

    def pieces_to(goal):
        while at < min(goal, PARTS * len(pieces)):
            part()

    weight(("in", 0))
    start = PARTS * min(last[0] + 1 + lead, len(pieces))
    pieces_to(start)
    shares = sum(n for name, n in first if name == "fill")
    shares += (STEPS - 1) * sum(n for name, n in later if name == "fill")
    per = PARTS * len(pieces) / U / shares
    filled = 0.0

    def stage(name, e):
        if 0 <= e < U * STEPS:
            u, s = divmod(e, STEPS)
            if name == "load" and s == 0:
                pieces_to(PARTS * (last[u] + 4))
            order.append((name, u, s))

    for name, shift in later:
        if name not in ("fill", "sample", "weights"):
            for e in range(shift):
                stage(name, e)
    for e in range(U * STEPS):
        u, s = divmod(e, STEPS)
        for name, n in (later if s else first):
            if name == "fill":
                filled += n
                pieces_to(start + filled * per)
            elif name == "sample":
                order.append(("sample", u, n))
            elif name == "weights":
                for k in range(wo_tiles):
                    weight(("out", u * wo_tiles + k))
            else:
                stage(name, e + n)
        if s == STEPS - 1:
            for name in between:
                order.append((name, u))
    for name in after_last:
        stage(name, U * STEPS - 1)
    return order, pieces, weights, last


def hybrid_kernel(nc, x_prompt, x_sample, state_gla, state_ssm, state_conv, meta_tokens, pre_norm,
                  post_norm, gla_w_in, gla_w_gate_up, gla_b_gate, gla_w_norm, gla_w_out, ssd_w_in,
                  ssd_conv_w, ssd_conv_b, ssd_dt_bias, ssd_a_log, ssd_d_skip, ssd_w_norm, ssd_w_out,
                  y_prompt, y_sample, gla_prompt, ssm_prompt, conv_prompt, gla_sample, ssm_sample,
                  conv_sample):
    gq = nc.dram_tensor("gla_rows", [U, 7 * P, T], F32, kind="Internal").ap()
    sq = nc.dram_tensor("ssd_rows", [U, 10 * P, T], F32, kind="Internal").ap()
    acd = nc.dram_tensor("ssd_decay_rows", [SH, T], F32, kind="Internal").ap()
    x1d = nc.dram_tensor("x_after_gla", [T, D], F32, kind="Internal").ap()

    with ExitStack() as top:
        def sb(name, shape, dt=F32):
            return top.enter_context(nc.sbuf_tensor(name, shape, dt))

        def ps(name):
            return top.enter_context(nc.psum_tensor(name, [P, 512], F32))

        m = {}
        m["h"] = sb("h", [P, 2, KT, T], F32R)
        m["y"] = sb("y_acc", [P, STEPS, D])
        m["w"] = sb("w", [P, 2, 2, KT, P], F32R)
        m["raw"] = sb("w_raw", [P, 2, D])
        m["wo"] = sb("w_out", [P, 4, 2, D], F32R)
        m["ident"] = sb("ident", [P, P])
        m["tri"] = sb("tri", [P, P])
        m["tri0"] = sb("tri0", [C0, C0])
        m["wn"] = sb("wn", [P, 24])
        m["bg"] = sb("bg", [P, U])
        m["cw"] = sb("cw", [P, 5, 24])
        m["banks"] = [ps(f"bank{i}") for i in range(8)]
        io = dict(xp=x_prompt, xs=x_sample, meta=meta_tokens, x1=x1d, pre=pre_norm, post=post_norm,
                  yp=y_prompt, ys=y_sample)
        for name in ("rows_out0", "rows_out1", "rows_out2", "gla_state_out", "gla_sample_out0",
                     "gla_sample_out1", "conv_old_out", "conv_out", "ssm_state_out", "ssm_sample_out0",
                     "ssm_sample_out1"):
            m[name] = nc.alloc_semaphore(name)
        with nc.cleanup_on_exit():
            constants(nc, m, gla_w_norm, ssd_w_norm, gla_b_gate, ssd_conv_w, ssd_conv_b)
        with nc.cleanup_on_exit():
            norm_phase(nc, m, io, 0)
        with nc.cleanup_on_exit():
            gla_gates(nc, m, gla_w_in, gla_w_gate_up, gq)
        with nc.cleanup_on_exit():
            gla_layer(nc, m, gq, gla_w_in, gla_w_out, state_gla, gla_prompt, gla_sample)
        with nc.cleanup_on_exit():
            norm_phase(nc, m, io, 1)
        with ExitStack() as ssd:
            t = {}
            for name, shape in (("dt", [P, STEPS, SH]), ("ac", [P, STEPS, SH]), ("ecol", [P, 16, NS]),
                                ("dskip", [P, SH]), ("sc", [P, 24, 3, NS])):
                t[name] = ssd.enter_context(nc.sbuf_tensor(name, shape, F32))
            with nc.cleanup_on_exit():
                ssd_step_sizes(nc, m, t, ssd_w_in, ssd_dt_bias, ssd_a_log, ssd_d_skip, state_conv, acd,
                               conv_sample)
            with nc.cleanup_on_exit():
                ssd_layer(nc, m, t, sq, acd, ssd_w_in, ssd_w_out, state_ssm, ssm_prompt, ssm_sample,
                          conv_prompt, conv_sample)
        with nc.cleanup_on_exit():
            norm_phase(nc, m, io, 2)


def constants(nc, m, gla_w_norm, ssd_w_norm, gla_b_gate, conv_w, conv_b):
    ident, tri, tri0 = m["ident"], m["tri"], m["tri0"]
    bank = m["banks"][0]
    with ExitStack() as ctx:
        rows = ctx.enter_context(nc.sbuf_tensor("rows", [24, 8, P], F32))
        loaded = nc.alloc_semaphore("c_loaded")
        made = nc.alloc_semaphore("c_made")
        turned = nc.alloc_semaphore("c_turned")
        kept = nc.alloc_semaphore("c_kept")
        block = ctx.enter_context(nc.Block())
        parts = [(conv_w[0, i].rearrange("(a p) -> a p", p=P), 24) for i in range(4)]
        parts.append((conv_b[0].rearrange("(a p) -> a p", p=P), 24))
        parts.append((ssd_w_norm[0].rearrange("(a p) -> a p", p=P), 16))
        parts.append((gla_w_norm[0].rearrange("(a p) -> a p", p=P), 8))
        parts.append((gla_b_gate[0].rearrange("(a p) -> a p", p=P), 4))

        @block.sync
        def _(sp):
            for i, (src, n) in enumerate(parts):
                sp.dma_start(rows[0:n, i, :], src).then_inc(loaded, 16)

        @block.gpsimd
        def _(pool):
            pool.memset(ident[:, :], 0.0).then_inc(made, 1)
            pool.memset(tri[:, :], 1.0).then_inc(made, 1)
            pool.wait_ge(made, 2)
            pool.affine_select(out=ident[:, :], in_=ident[:, :], compare_op=ALU.not_equal, fill=1.0,
                               base=0, pattern=[[-1, P]], channel_multiplier=1).then_inc(made, 1)
            pool.affine_select(out=tri[:, :], in_=tri[:, :], compare_op=ALU.is_ge, fill=0.0,
                               base=0, pattern=[[1, P]], channel_multiplier=-1).then_inc(made, 1)
            pool.wait_ge(made, 4)
            pool.tensor_copy(tri0[:, :], tri[0:C0, 0:C0]).then_inc(made, 1)
            pool.wait_ge(made, 5)
            pool.tensor_copy(tri0[0:NS, :], ident[0:NS, 0:C0]).then_inc(made, 1)

        @block.tensor
        def _(pe):
            pe.wait_ge(made, 6)
            pe.wait_ge(loaded, 16 * len(parts))
            for i, (_, n) in enumerate(parts):
                last = pe.transpose(bank[:, 24 * i:24 * i + n], rows[0:n, i, :], ident[0:n, 0:n])
            last.then_inc(turned, 1)

        @block.scalar
        def _(act):
            act.wait_ge(turned, 1)
            act.activation(m["cw"][:, :, :], bank[:, 0:120].rearrange("p (i a) -> p i a", i=5),
                           ACT.Copy, scale=0.5).then_inc(kept, 1)
            act.activation(m["wn"][:, 0:16], bank[:, 120:136], ACT.Copy).then_inc(kept, 1)
            act.activation(m["wn"][:, 16:24], bank[:, 144:152], ACT.Copy, scale=0.5).then_inc(kept, 1)
            act.activation(m["bg"][:, :], bank[:, 168:172], ACT.Copy).then_inc(kept, 1)
            act.wait_ge(kept, 4)


def norm_phase(nc, m, io, k):
    y, h, ident = m["y"], m["h"], m["ident"]
    banks = m["banks"]
    with ExitStack() as ctx:
        def sb(name, shape):
            return ctx.enter_context(nc.sbuf_tensor(f"{name}{k}", shape, F32))

        def sem(name):
            return nc.alloc_semaphore(f"n{k}_{name}")

        pre, post = sb("pre", [P, D]), sb("post", [P, D])
        xt = sb("xt", [P, 3, D])
        junk = sb("junk", [P, D])
        ssum, mean, rstd = sb("ssum", [P, 2, STEPS]), sb("mean", [P, 2, STEPS]), sb("rstd", [P, 2, STEPS])
        power = sb("power", [P, 1])
        w_in, x_in = sem("w_in"), [sem(f"x_in{i}") for i in range(3)]
        stored = [m[f"rows_out{i}"] if k == 2 else sem(f"stored{i}") for i in range(3)]
        ready, squared, meant, rooted = sem("ready"), sem("squared"), sem("meant"), sem("rooted")
        scaled, added, normed, turned, high, low = (sem(n) for n in
                                                    ("scaled", "added", "normed", "turned", "high", "low"))
        block = ctx.enter_context(nc.Block())
        norms = [0] if k == 0 else [0, 1] if k == 1 else [1]

        def copies(s):
            if k < 2:
                return [(0, io["xs"][:, 0, :]), (NS, io["meta"])] if s == 0 else \
                       [(0, io["xp"][0, P * (s - 1):P * s, :])]
            c, n = step_cols(s)
            return [(0, io["x1"][c:c + n, :])]

        def arrived_all(s):
            two = 1 if k != 2 and s % 3 == 0 else 0
            return 16 * (s // 3 + 1 + two)

        def stores(s):
            if k == 2:
                return [(NS, io["ys"][:, 0, :])] if s == 0 else [(P, io["yp"][0, P * (s - 1):P * s, :])]
            c, n = step_cols(s)
            return [(n, io["x1"][c:c + n, :])]

        @block.sync
        def _(sp):
            if 0 in norms:
                sp.dma_start(pre[:, :], io["pre"][min(k, 1):min(k, 1) + 1, :].to_broadcast([P, D])).then_inc(w_in, 16)
            if 1 in norms:
                sp.dma_start(post[:, :], io["post"][k - 1:k, :].to_broadcast([P, D])).then_inc(w_in, 16)
            for s in range(STEPS + 2):
                if s < STEPS:
                    if s >= 3:
                        if k < 2:
                            sp.wait_ge(normed, s - 2)
                        if k > 0:
                            sp.wait_ge(stored[s % 3], 16 * (s // 3))
                    for p0, src in copies(s):
                        sp.dma_start(xt[p0:p0 + src.shape[0], s % 3, :], src).then_inc(x_in[s % 3], 16)
                if k > 0 and s >= 2:
                    q = s - 2
                    sp.wait_ge(added, q + 1)
                    for n, dst in stores(q):
                        sp.dma_start(dst, xt[0:n, q % 3, :]).then_inc(stored[q % 3], 16)
            if k > 0:
                for i in range(3):
                    sp.wait_ge(stored[i], 16 * (STEPS // 3))

        @block.gpsimd
        def _(pool):
            pool.memset(power[:, :], -0.5).then_inc(ready, 1)
            pool.wait_ge(ready, 1)
            i = 0
            for s in range(STEPS):
                n = step_cols(s)[1]
                for w in reversed(norms):
                    i += 1
                    pool.wait_ge(squared, i)
                    pool.tensor_scalar(mean[0:n, w, s:s + 1], ssum[0:n, w, s:s + 1], 1.0 / D, EPS,
                                       ALU.mult, ALU.add).then_inc(meant, 1)
                    pool.wait_ge(meant, i)
                    pool.tensor_tensor(rstd[0:n, w, s:s + 1], mean[0:n, w, s:s + 1], power[0:n, :],
                                       ALU.pow).then_inc(rooted, 1)

        @block.scalar
        def _(act):
            def square(src, w, s, n):
                done = len(norms) * s + (1 if len(norms) == 2 and w == 0 else 0)
                if done:
                    act.wait_ge(squared, done)
                act.activation(junk[0:n, :], src, ACT.Square,
                               accum_out=ssum[0:n, w, s:s + 1]).then_inc(squared, 1)

            for s in range(STEPS):
                c, n = step_cols(s)
                if 1 in norms:
                    square(y[0:n, s, :], 1, s, n)
                if 0 in norms:
                    if k == 0:
                        act.wait_ge(x_in[s % 3], arrived_all(s))
                    else:
                        act.wait_ge(added, s + 1)
                    square(xt[0:n, s % 3, :], 0, s, n)
                    for j in range(2):
                        act.wait_ge(turned, 2 * s + j + 1)
                        act.activation(h[:, 0, 4 * j:4 * j + 4, c:c + n],
                                       banks[j][:, 0:4 * n].rearrange("p (a c) -> p a c", a=4),
                                       ACT.Copy).then_inc(high, 1)

        @block.vector
        def _(dve):
            dve.wait_ge(w_in, 16 * len(norms))
            i = 0
            for s in range(STEPS):
                c, n = step_cols(s)
                if 1 in norms:
                    i += 1
                    dve.wait_ge(rooted, i)
                    dve.scalar_tensor_tensor(out=y[0:n, s, :], in0=y[0:n, s, :],
                                             scalar=rstd[0:n, 1, s:s + 1], in1=post[0:n, :],
                                             op0=ALU.mult, op1=ALU.mult).then_inc(scaled, 1)
                    dve.wait_ge(scaled, s + 1)
                    dve.wait_ge(x_in[s % 3], arrived_all(s))
                    dve.tensor_tensor(xt[0:n, s % 3, :], xt[0:n, s % 3, :], y[0:n, s, :],
                                      ALU.add).then_inc(added, 1)
                if 0 in norms:
                    i += 1
                    dve.wait_ge(rooted, i)
                    if k == 1:
                        dve.wait_ge(added, s + 1)
                    dve.scalar_tensor_tensor(out=y[0:n, s, :], in0=xt[0:n, s % 3, :],
                                             scalar=rstd[0:n, 0, s:s + 1], in1=pre[0:n, :],
                                             op0=ALU.mult, op1=ALU.mult).then_inc(normed, 1)
                    for j in range(2):
                        dve.wait_ge(high, 2 * s + j + 1)
                        dve.tensor_tensor(h[:, 1, 4 * j:4 * j + 4, c:c + n],
                                          banks[j][:, 0:4 * n].rearrange("p (a c) -> p a c", a=4),
                                          h[:, 0, 4 * j:4 * j + 4, c:c + n].bitcast(F32),
                                          ALU.subtract).then_inc(low, 1)

        if 0 in norms:
            @block.tensor
            def _(pe):
                for s in range(STEPS):
                    n = step_cols(s)[1]
                    pe.wait_ge(normed, s + 1)
                    for j in range(2):
                        if s:
                            pe.wait_ge(low, 2 * s - 1 + j)
                        for a in range(4):
                            f = (4 * j + a) * P
                            last = pe.transpose(banks[j][:, a * n:a * n + n], y[0:n, s, f:f + P],
                                                ident[0:n, 0:n])
                        last.then_inc(turned, 1)


def reset_mask(pool, mask, made, at):
    pool.memset(mask, 1.0).then_inc(made, 1)
    pool.wait_ge(made, at + 1)
    n = mask.shape[0]
    pool.memset(mask[:, 0:NS + 1], 0.0).then_inc(made, 1)
    for s in range(1, STEPS):
        c = step_cols(s)[0]
        pool.memset(mask[:, c:c + 1], 0.0).then_inc(made, 1)
    return at + 1 + STEPS


def narrow_projection(pe, m, n_w, w_lo, evacuated, projected):
    h, w, banks = m["h"], m["w"], m["banks"]
    pe.wait_ge(w_lo, 1)
    for g, (c, n) in enumerate(CGS):
        i = 0
        for k in range(KT):
            for a, b in ((0, 0), (0, 1), (1, 0)):
                last = pe.matmul(banks[g][:, 0:n], w[:, 0, a, k, :], h[:, b, k, c:c + n],
                                 start=(i == 0), stop=(i == 3 * KT - 1))
                i += 1
        last.then_inc(projected, 1)


def gla_gates(nc, m, w_in, w_up, gq):
    w, raw, banks, bg = m["w"], m["raw"], m["banks"], m["bg"]
    c0 = GLA_COLS["g"]
    with ExitStack() as ctx:
        def sem(name):
            return nc.alloc_semaphore(f"gg_{name}")

        low = ctx.enter_context(nc.sbuf_tensor("g_low", [GR, T], F32))
        up = ctx.enter_context(nc.sbuf_tensor("g_up", [GR, U * HK], F32))
        mask = ctx.enter_context(nc.sbuf_tensor("g_mask", [P, T], F32))
        t1 = ctx.enter_context(nc.sbuf_tensor("g_t1", [P, 2, T], F32))
        t2 = ctx.enter_context(nc.sbuf_tensor("g_t2", [P, 2, T], F32))
        wr, up_in, made, zeroed, w_hi, w_lo, projected, lows, gated = (
            sem(x) for x in ("w_raw", "up_in", "made", "zeroed", "w_hi", "w_lo", "projected", "lows", "gated"))
        absd, capped, exped, logged, summed, scanned = (
            sem(x) for x in ("absd", "capped", "exped", "logged", "summed", "scanned"))
        stored = [sem(f"stored{i}") for i in range(2)]
        block = ctx.enter_context(nc.Block())
        r = raw[:, 0, 0:KT * GR].rearrange("p (k f) -> p k f", k=KT)

        @block.sync
        def _(sp):
            sp.dma_start(r, w_in[0, :, c0:c0 + GR].rearrange("(k p) f -> p k f", p=P)).then_inc(wr, 16)
            sp.dma_start(up[:, :], w_up[0]).then_inc(up_in, 16)
            for u in range(U):
                sp.wait_ge(scanned, u + 1)
                sp.dma_start(gq[u, 2 * P:3 * P, :], t2[:, u % 2, :]).then_inc(stored[u % 2], 16)
            for i in range(2):
                sp.wait_ge(stored[i], 16 * (U // 2))

        @block.gpsimd
        def _(pool):
            pool.memset(w[:, 0, 0, :, :].bitcast(F32), 0.0).then_inc(zeroed, 1)
            pool.memset(w[:, 0, 1, :, :].bitcast(F32), 0.0).then_inc(zeroed, 1)
            reset_mask(pool, mask[:, :], made, 0)

        @block.scalar
        def _(act):
            act.wait_ge(zeroed, 2)
            act.wait_ge(wr, 16)
            act.activation(w[:, 0, 0, :, 0:GR], r, ACT.Copy).then_inc(w_hi, 1)
            for g, (c, n) in enumerate(CGS):
                act.wait_ge(projected, g + 1)
                act.activation(low[:, c:c + n], banks[g][0:GR, 0:n], ACT.Copy).then_inc(lows, 1)
            for u in range(U):
                if u >= 2:
                    act.wait_ge(scanned, u - 1)
                for g, (c, n) in enumerate(CGS):
                    i = 3 * u + g
                    act.wait_ge(gated, i + 1)
                    act.activation(t1[:, u % 2, c:c + n], banks[i % 6][:, 0:n], ACT.Abs,
                                   bias=bg[:, u:u + 1]).then_inc(absd, 1)
                act.wait_ge(absd, 3 * u + 3)
                act.activation(t1[:, u % 2, :], t1[:, u % 2, :], ACT.Exp, scale=-1.0).then_inc(exped, 1)
                act.wait_ge(exped, u + 1)
                act.activation(t1[:, u % 2, :], t1[:, u % 2, :], ACT.Ln, bias=1.0).then_inc(logged, 1)

        @block.vector
        def _(dve):
            dve.wait_ge(w_hi, 1)
            dve.tensor_tensor(w[:, 0, 1, :, 0:GR], r, w[:, 0, 0, :, 0:GR].bitcast(F32),
                              ALU.subtract).then_inc(w_lo, 1)
            dve.wait_ge(made, 1 + STEPS)
            for u in range(U):
                if u >= 2:
                    dve.wait_ge(stored[u % 2], 16 * (u // 2))
                for g, (c, n) in enumerate(CGS):
                    i = 3 * u + g
                    dve.wait_ge(absd, i + 1)
                    dve.tensor_scalar(t2[:, u % 2, c:c + n], banks[i % 6][:, 0:n], bg[:, u:u + 1], 0.0,
                                      ALU.add, ALU.min).then_inc(capped, 1)
                dve.wait_ge(logged, u + 1)
                dve.wait_ge(capped, 3 * u + 3)
                dve.tensor_tensor(t1[:, u % 2, :], t2[:, u % 2, :], t1[:, u % 2, :],
                                  ALU.subtract).then_inc(summed, 1)
                dve.wait_ge(summed, u + 1)
                dve.tensor_tensor_scan(t2[:, u % 2, :], mask[:, :], t1[:, u % 2, :], 0.0, ALU.mult,
                                       ALU.add).then_inc(scanned, 1)

        @block.tensor
        def _(pe):
            narrow_projection(pe, m, GR, w_lo, None, projected)
            pe.wait_ge(up_in, 16)
            pe.wait_ge(lows, 3)
            for u in range(U):
                for g, (c, n) in enumerate(CGS):
                    i = 3 * u + g
                    if i >= 6:
                        pe.wait_ge(capped, i - 5)
                    pe.matmul(banks[i % 6][:, 0:n], up[:, u * HK:(u + 1) * HK], low[:, c:c + n],
                              start=True, stop=True).then_inc(gated, 1)


class Weights:

    def __init__(self, weights, pieces, w_in, w_out, columns, tiles, wo_tiles, wn0):
        self.ends = {t: i + 1 for i, (t, g) in enumerate(pieces) if g == 2}
        self.weights, self.w_in, self.w_out, self.columns = weights, w_in, w_out, columns
        self.tiles, self.wo_tiles, self.wn0 = tiles, wo_tiles, wn0
        self.index = {w: i for i, w in enumerate(weights)}

    def source(self, i):
        kind, t = self.weights[i]
        if kind == "in":
            c = self.columns(t)
            return self.w_in[:, c:c + P].rearrange("(k p) f -> p k f", p=P)
        return self.w_out[t * P:(t + 1) * P, :]

    def raw(self, m, i):
        r = m["raw"][:, i % 2, :]
        return r.rearrange("p (k f) -> p k f", k=KT) if self.weights[i][0] == "in" else r

    def part(self, m, i, part):
        kind, t = self.weights[i]
        return m["w"][:, t % 2, part, :, :] if kind == "in" else m["wo"][:, t % self.wo_tiles, part, :]

    def load(self, sp, m, i, raw_in, w_lo):
        if i >= 2:
            sp.wait_ge(w_lo, i - 1)
        sp.dma_start(self.raw(m, i), self.source(i)).then_inc(raw_in[i % 2], 16)

    def high(self, act, m, i, raw_in, w_hi, piece_done, out_used):
        kind, t = self.weights[i]
        act.wait_ge(raw_in[i % 2], 16 * (i // 2 + 1))
        if kind == "in":
            if t >= 2:
                act.wait_ge(piece_done, self.ends[t - 2])
            act.activation(self.part(m, i, 0), self.raw(m, i), ACT.Copy).then_inc(w_hi, 1)
        else:
            u = t // self.wo_tiles
            if u:
                act.wait_ge(out_used, 2 * STEPS * u)
            act.activation(self.part(m, i, 0), self.raw(m, i), ACT.Copy,
                           scale=m["wn"][:, self.wn0 + t:self.wn0 + t + 1]).then_inc(w_hi, 1)

    def low(self, dve, m, i, w_hi, w_lo):
        kind, t = self.weights[i]
        dve.wait_ge(w_hi, i + 1)
        hi = self.part(m, i, 0).bitcast(F32)
        if kind == "in":
            dve.tensor_tensor(self.part(m, i, 1), self.raw(m, i), hi, ALU.subtract).then_inc(w_lo, 1)
        else:
            dve.scalar_tensor_tensor(out=self.part(m, i, 1), in0=self.raw(m, i),
                                     scalar=m["wn"][:, self.wn0 + t:self.wn0 + t + 1], in1=hi,
                                     op0=ALU.mult, op1=ALU.subtract).then_inc(w_lo, 1)


def project_part(pe, m, t, g, p, bank):
    c, n = CGS[g]
    for k in range(p * KT // PARTS, (p + 1) * KT // PARTS):
        for i, (a, b) in enumerate(((0, 0), (0, 1), (1, 0))):
            last = pe.matmul(bank[:, 0:n], m["w"][:, t % 2, a, k, :], m["h"][:, b, k, c:c + n],
                             start=(k == 0 and i == 0), stop=(k == KT - 1 and i == 2))
    return last


def out_products(pe, m, yt, wo_tiles, half, bank):
    i = 0
    for k in range(wo_tiles):
        for a, b in ((0, 0), (0, 1), (1, 0)):
            last = pe.matmul(bank[:, :], yt[a][:, k, :], m["wo"][:, k, b, 512 * half:512 * half + 512],
                             start=(i == 0), stop=(i == 3 * wo_tiles - 1))
            i += 1
    return last


def gla_layer(nc, m, gq, w_in, w_out, state, state_prompt, state_sample):
    NT, WT = 6, 2
    step = [("load", 1), ("keys", 0), ("levels", 0), ("fill", 1), ("state", 0), ("decay", 1), ("fill", 1),
            ("attend", 0), ("norm", 0), ("products", -1), ("scale", 1), ("fill", 1), ("turn", 0),
            ("values", 1), ("fill", 0.5)]
    first = step[:4]
    for i in range(4):
        first += [("sample", i), ("fill", 0.5)]
    first += step[4:10] + [("weights", 0)] + step[10:]
    order, pieces, weights, last_piece = interleave(NT, set(), WT, 4, first, step, [], ["products"])
    kinds = ["q", "k", "v", "v", "r", "r"]
    rows = [0, 1, 3, 4, 5, 6]

    def column(t):
        u, j = divmod(t, NT)
        kind = kinds[j]
        width = HK if kind in "qk" else HV
        return GLA_COLS[kind] + u * width + (P if j in (3, 5) else 0)

    W = Weights(weights, pieces, w_in[0], w_out[0], column, NT, WT, 16)
    PA, PB, TA, TB, L0, L1, O, X = m["banks"]
    PR, L, ident, y = (PA, PB), (L0, L1), m["ident"], m["y"]
    with ExitStack() as ctx:
        def sb(name, shape, dt=F32):
            return ctx.enter_context(nc.sbuf_tensor("g_" + name, shape, dt))

        def sem(name):
            return nc.alloc_semaphore("g_" + name)

        mask = sb("lmask", [P, 7, P])
        mask0 = sb("lmask0", [C0, 4, C0])
        rowsel = sb("rowsel", [C0, NS + 1])
        st = sb("stage", [P, 2, 350])
        th = sb("th", [P, 350])
        ck = sb("chunk", [P, 2, 7, P])
        E = sb("decays", [P, 8, P])
        Eq = sb("q_decayed", [P, 7, P])
        eb = sb("ebcum", [P, P])
        qe = sb("q_inter", [P, P])
        kd0 = sb("k_first", [P, C0])
        kt = sb("k_turned", [P, P])
        km = sb("k_masked", [C0, NS + 1, P])
        vt = sb("v_turned", [P, HV])
        G, G0 = sb("attn", [P, P]), sb("attn0", [C0, C0])
        on, og = sb("o_normed", [P, HV]), sb("o_gated", [P, HV])
        othi, otlo = sb("ot_hi", [P, 2, P], F32R), sb("ot_lo", [P, 2, P], F32R)
        S = sb("state", [P, HV])
        qm = sb("q_masked", [P, NS * C0])
        ss = sb("sample_state", [P, 2, 2, HV])
        osum, omean, orstd, power = (sb(x, [P, 1]) for x in ("osum", "omean", "orstd", "power"))

        raw_in = [sem(f"raw_in{i}") for i in range(2)]
        w_hi, w_lo = sem("w_hi"), sem("w_lo")
        piece_done = sem("piece_done")
        bank_free = [sem(f"bank_free{i}") for i in range(2)]
        tanhed = sem("tanhed")
        staged = [sem(f"staged{i}") for i in range(2)]
        stored = [sem(f"stored{i}") for i in range(2)]
        ck_in = [sem(f"ck_in{i}") for i in range(2)]
        consts, zeros, dsub, dabs, decays, eb_done = (sem(x) for x in
                                                      ("consts", "zeros", "dsub", "dabs", "decays", "eb_done"))
        k_ready, q_ready, qi_ready, ta_done, tb_done = (sem(x) for x in
                                                        ("k_ready", "q_ready", "qi_ready", "ta_done", "tb_done"))
        v_turned, k_turned, levels, attn_part, attn = (sem(x) for x in
                                                       ("v_turned", "k_turned", "levels", "attn_part", "attn"))
        s_prod, s_new, o_done, squared = (sem(x) for x in ("s_prod", "s_new", "o_done", "squared"))
        meant, rooted, o_scaled, o_gated, o_turned = (sem(x) for x in
                                                      ("meant", "rooted", "o_scaled", "o_gated", "o_turned"))
        ot_hi, ot_lo, out_done, added = (sem(x) for x in ("ot_hi", "ot_lo", "out_done", "added"))
        s_saved = m["gla_state_out"]
        ss_in = [sem(f"ss_in{i}") for i in range(2)]
        ss_out = [m[f"gla_sample_out{i}"] for i in range(2)]
        qm_ready, km_ready, ss_inter, ss_prod, ss_new = (sem(x) for x in
                                                         ("qm_ready", "km_ready", "ss_inter", "ss_prod", "ss_new"))
        k_ready0 = sem("k_ready0")
        CONSTS = 10 + 3 * 11 + 2
        block = ctx.enter_context(nc.Block())

        def ev(u, s):
            return u * STEPS + s

        def tokens(u, s):
            return ck[:, ev(u, s) % 2, :, 0:step_cols(s)[1]]

        @block.sync
        def _(sp):
            def store(i):
                t, g = pieces[i]
                u, j = divmod(t, NT)
                c, n = CGS[g]
                sp.wait_ge(staged[i % 2], i // 2 + 1)
                sp.dma_start(gq[u, rows[j] * P:(rows[j] + 1) * P, c:c + n],
                             st[:, i % 2, 0:n]).then_inc(stored[i % 2], 16)

            def load(u, s):
                e = ev(u, s)
                c, n = step_cols(s)
                if s == 0:
                    for i in range(2):
                        sp.wait_ge(stored[i], 16 * ((last_piece[u] - i) // 2 + 1))
                if e >= 2:
                    sp.wait_ge(ta_done, e - 1)
                    sp.wait_ge(levels, 2 * (e - 1))
                    sp.wait_ge(qi_ready, e - 1)
                    sp.wait_ge(eb_done, e - 1)
                sp.dma_start(tokens(u, s), gq[u, :, c:c + n].rearrange("(t p) c -> p t c", p=P)).then_inc(
                    ck_in[e % 2], 16)

            W.load(sp, m, 0, raw_in, w_lo)
            W.load(sp, m, 1, raw_in, w_lo)
            for task in order:
                if task[0] == "split" and task[1] + 2 < len(weights):
                    W.load(sp, m, task[1] + 2, raw_in, w_lo)
                elif task[0] == "store":
                    store(task[1])
                elif task[0] == "load":
                    load(*task[1:])
                elif task[0] == "norm" and task[2] == STEPS - 1:
                    u = task[1]
                    sp.wait_ge(s_new, STEPS * (u + 1))
                    sp.dma_start(state_prompt[0, 0, u], S[:, :]).then_inc(s_saved, 16)
            sp.wait_ge(s_saved, 16 * U)
            for i in range(2):
                sp.wait_ge(stored[i], 16 * ((len(pieces) - 1 - i) // 2 + 1))

        @block.gpsimd
        def _(pool):
            n = 0
            for li, h in enumerate(gla_levels(1)[0]):
                pool.memset(mask[:, li, :], 0.0).then_inc(consts, 1)
            pool.memset(mask0[:, :, :], 0.0).then_inc(consts, 1)
            pool.memset(rowsel[:, :], 1.0).then_inc(consts, 1)
            pool.memset(power[:, :], -0.5).then_inc(consts, 1)
            n = 10
            pool.wait_ge(consts, n)
            sets = [(mask[:, li, :], h, 0) for li, h in enumerate(gla_levels(1)[0])]
            sets += [(mask0[:, li, NS:C0], h, NS) for li, h in enumerate(gla_levels(0)[0])]
            views = [(v.rearrange("p (b w) -> p b w", w=2 * h)[:, :, h:2 * h], h, off) for v, h, off in sets]
            for v, h, off in views:
                pool.memset(v, 1.0).then_inc(consts, 1)
            n += len(views)
            pool.wait_ge(consts, n)
            for v, h, off in views:
                pool.affine_select(out=v, in_=v, compare_op=ALU.is_ge, fill=0.0, base=-off,
                                   pattern=[[-2 * h, v.shape[1]], [0, h]],
                                   channel_multiplier=1).then_inc(consts, 1)
            n += len(views)
            pool.wait_ge(consts, n)
            for v, h, off in views:
                pool.affine_select(out=v, in_=v, compare_op=ALU.is_ge, fill=0.0, base=off + h - 1,
                                   pattern=[[2 * h, v.shape[1]], [0, h]],
                                   channel_multiplier=-1).then_inc(consts, 1)
            n += len(views)
            pool.affine_select(out=rowsel[:, NS:NS + 1], in_=rowsel[:, NS:NS + 1], compare_op=ALU.is_ge,
                               fill=0.0, base=-NS, pattern=[[0, 1]], channel_multiplier=1).then_inc(consts, 1)
            pool.tensor_copy(rowsel[:, 0:NS], ident[0:C0, 0:NS]).then_inc(consts, 1)
            assert n + 2 == CONSTS
            def sample_state(i, out):
                u, b = divmod(i, 4)
                if out:
                    pool.wait_ge(ss_new, 2 * (i + 1))
                    pool.dma_start(state_sample[0, 2 * b:2 * b + 2, u].rearrange("b k v -> k b v"),
                                 ss[:, i % 2, :, :]).then_inc(ss_out[i % 2], 16)
                else:
                    if i >= 2:
                        pool.wait_ge(ss_out[i % 2], 16 * (i // 2))
                    pool.dma_start(ss[:, i % 2, :, :],
                                 state[0, 2 * b:2 * b + 2, u].rearrange("b k v -> k b v")).then_inc(
                                     ss_in[i % 2], 16)

            sample_state(0, False)
            sample_state(1, False)
            for task in order:
                if task[0] == "sample":
                    i = 4 * task[1] + task[2]
                    sample_state(i, True)
                    if i + 2 < 4 * U:
                        sample_state(i + 2, False)
                elif task[0] == "norm":
                    e, n = ev(*task[1:]), step_cols(task[2])[1]
                    pool.wait_ge(squared, e + 1)
                    pool.tensor_scalar(omean[0:n, :], osum[0:n, :], 1.0 / HV, EPS, ALU.mult,
                                       ALU.add).then_inc(meant, 1)
                    pool.wait_ge(meant, e + 1)
                    if e:
                        pool.wait_ge(o_scaled, e)
                    pool.tensor_tensor(orstd[0:n, :], omean[0:n, :], power[0:n, :],
                                       ALU.pow).then_inc(rooted, 1)
            for i in range(2):
                pool.wait_ge(ss_out[i], 16 * 2 * U)

        @block.scalar
        def _(act):
            def evac(i):
                t, g = pieces[i]
                j, n = t % NT, CGS[g][1]
                act.wait_ge(piece_done, i + 1)
                if j >= 4:
                    q = (t // NT) * 6 + (j - 4) * 3 + g
                    if q:
                        act.wait_ge(staged[(prev_gate[i]) % 2], prev_gate[i] // 2 + 1)
                    act.activation(th[:, 0:n], PR[i % 2][:, 0:n], ACT.Tanh, scale=0.5).then_inc(tanhed, 1)
                    return
                if i >= 2:
                    act.wait_ge(stored[i % 2], 16 * (i // 2))
                act.activation(st[:, i % 2, 0:n], PR[i % 2][:, 0:n], ACT.Copy,
                               scale=HK ** -0.5 if j == 0 else 1.0).then_inc(staged[i % 2], 1)

            def decay(u, s):
                e, n = ev(u, s), step_cols(s)[1]
                x = tokens(u, s)
                act.wait_ge(ck_in[e % 2], 16 * (e // 2 + 1))
                if e:
                    act.wait_ge(qi_ready, e)
                    act.wait_ge(s_new, e)
                    if s == 1:
                        act.wait_ge(ss_new, 2 * 4 * (u + 1))
                act.activation(eb[:, 0:n], x[:, 2, :], ACT.Exp, scale=1.0 / TAU).then_inc(eb_done, 1)
                act.wait_ge(dsub, e + 1)
                act.activation(E[:, :, 0:n], E[:, :, 0:n], ACT.Abs).then_inc(dabs, 1)
                act.wait_ge(dabs, e + 1)
                act.activation(E[:, :, 0:n], E[:, :, 0:n], ACT.Exp, scale=-1.0 / TAU).then_inc(decays, 1)

            def values(u, s):
                e, n = ev(u, s), step_cols(s)[1]
                act.wait_ge(ta_done, e + 1)
                if e:
                    act.wait_ge(o_done, e)
                    act.wait_ge(s_prod, e)
                    if s == 1:
                        act.wait_ge(ss_prod, 4 * (u + 1))
                act.activation(vt[0:n, :], TA[0:n, 0:HV], ACT.Copy).then_inc(v_turned, 1)

            def keys(u, s):
                e = ev(u, s)
                if s:
                    act.wait_ge(tb_done, e + 1)
                    act.activation(kt[:, :], TB[:, 0:P], ACT.Copy).then_inc(k_turned, 1)

            def norm(u, s):
                e, n = ev(u, s), step_cols(s)[1]
                act.wait_ge(o_done, e + 1)
                if e:
                    act.wait_ge(rooted, e)
                    act.wait_ge(o_gated, e)
                act.activation(on[0:n, :], O[0:n, 0:HV], ACT.Square, accum_out=osum[0:n, :]).then_inc(squared, 1)
                act.wait_ge(rooted, e + 1)
                act.activation(on[0:n, :], O[0:n, 0:HV], ACT.Copy, scale=orstd[0:n, :]).then_inc(o_scaled, 1)

            def turn(u, s):
                e, n = ev(u, s), step_cols(s)[1]
                act.wait_ge(o_turned, e + 1)
                if e:
                    act.wait_ge(out_done, 2 * e)
                act.activation(othi[:, :, 0:n], O[:, 0:2 * n].rearrange("p (a c) -> p a c", a=2),
                               ACT.Copy).then_inc(ot_hi, 1)

            prev_gate, seen = {}, None
            for i, (t, g) in enumerate(pieces):
                if t % NT >= 4:
                    prev_gate[i] = seen
                    seen = i
            for task in order:
                if task[0] == "split":
                    W.high(act, m, task[1], raw_in, w_hi, piece_done, out_done)
                elif task[0] == "evac":
                    evac(task[1])
                elif task[0] in ("decay", "values", "keys", "norm", "turn"):
                    {"decay": decay, "values": values, "keys": keys, "norm": norm,
                     "turn": turn}[task[0]](*task[1:])

        @block.vector
        def _(dve):
            dve.memset(E[:, :, :], 0.0).then_inc(zeros, 1)
            dve.memset(G[:, :], 0.0).then_inc(zeros, 1)
            dve.memset(G0[:, :], 0.0).then_inc(zeros, 1)
            dve.memset(othi[:, :, :].bitcast(F32), 0.0).then_inc(zeros, 1)
            dve.memset(otlo[:, :, :].bitcast(F32), 0.0).then_inc(zeros, 1)
            dve.memset(qm[:, :], 0.0).then_inc(zeros, 1)
            dve.wait_ge(zeros, 6)
            dve.wait_ge(consts, CONSTS)

            def evac(i):
                t, g = pieces[i]
                n = CGS[g][1]
                if t % NT < 4:
                    return
                q = (t // NT) * 6 + (t % NT - 4) * 3 + g
                dve.wait_ge(tanhed, q + 1)
                if i >= 2:
                    dve.wait_ge(stored[i % 2], 16 * (i // 2))
                dve.scalar_tensor_tensor(out=st[:, i % 2, 0:n], in0=th[:, 0:n], scalar=1.0,
                                         in1=PR[i % 2][:, 0:n], op0=ALU.add,
                                         op1=ALU.mult).then_inc(staged[i % 2], 1)

            def decay(u, s):
                e, n = ev(u, s), step_cols(s)[1]
                x = tokens(u, s)
                sizes, off = gla_levels(s)
                dve.wait_ge(ck_in[e % 2], 16 * (e // 2 + 1))
                if e:
                    dve.wait_ge(levels, 2 * e)
                    dve.wait_ge(tb_done, e)
                b = x[:, 2, off:n]
                if s == 0:
                    dve.memset(E[:, :, 0:NS], 0.0).then_inc(zeros, 1)
                for li, h in enumerate(sizes):
                    v = b.rearrange("p (b w) -> p b w", w=2 * h)
                    nb = v.shape[1]
                    dve.tensor_tensor(E[:, li, off:n].rearrange("p (b w) -> p b w", w=2 * h), v,
                                      v[:, :, h - 1:h].to_broadcast([P, nb, 2 * h]), ALU.subtract)
                dve.tensor_tensor(E[:, 7, off:n], b, x[:, 2, n - 1:n].to_broadcast([P, n - off]),
                                  ALU.subtract).then_inc(dsub, 1)

            def scale(u, s):
                e, n = ev(u, s), step_cols(s)[1]
                x = tokens(u, s)
                sizes = gla_levels(s)[0]
                dve.wait_ge(decays, e + 1)
                nl = len(sizes)
                dve.tensor_tensor(Eq[:, 0:nl, 0:n], E[:, 0:nl, 0:n],
                                  x[:, 0:1, :].to_broadcast([P, nl, n]), ALU.mult).then_inc(q_ready, 1)
                dve.wait_ge(q_ready, e + 1)
                dve.tensor_tensor(E[:, :, 0:n], E[:, :, 0:n],
                                  x[:, 1:2, :].to_broadcast([P, 8, n]), ALU.mult).then_inc(k_ready, 1)
                dve.wait_ge(eb_done, e + 1)
                if e:
                    dve.wait_ge(o_done, e)
                dve.tensor_tensor(qe[:, 0:n], x[:, 0, :], eb[:, 0:n], ALU.mult).then_inc(qi_ready, 1)
                if s == 0:
                    dve.wait_ge(k_ready, e + 1)
                    dve.tensor_copy(kd0[:, 0:NS], x[:, 1, 0:NS]).then_inc(k_ready0, 1)
                    dve.tensor_copy(kd0[:, NS:C0], E[:, 7, NS:C0]).then_inc(k_ready0, 1)
                    dve.wait_ge(qi_ready, e + 1)
                    dve.tensor_copy(qm[:, 0:(NS - 1) * (C0 + 1) + 1:C0 + 1], qe[:, 0:NS]).then_inc(qm_ready, 1)

            def keys(u, s):
                e = ev(u, s)
                if s == 0:
                    dve.wait_ge(tb_done, e + 1)
                    dve.tensor_tensor(km[:, :, :], TB[0:C0, 0:P].unsqueeze(1).to_broadcast([C0, NS + 1, P]),
                                      rowsel[:, :].unsqueeze(2).to_broadcast([C0, NS + 1, P]),
                                      ALU.mult).then_inc(km_ready, 1)

            def levels_of(u, s):
                e, n = ev(u, s), step_cols(s)[1]
                sizes, off = gla_levels(s)
                nl = len(sizes)
                g, mk = (G0, mask0) if s == 0 else (G, mask)
                if e:
                    dve.wait_ge(o_done, e)
                part = 60 * u + (7 * s - 3 if s else 0)
                for li in range(nl):
                    if li % 4 == 0:
                        dve.wait_ge(levels, 2 * e + li // 4 + 1)
                    if li:
                        dve.wait_ge(attn_part, part + li)
                    dve.copy_predicated(g[:, :], mk[:, li, :].bitcast(I32),
                                        L[li // 4][0:n, (li % 4) * P:(li % 4) * P + n]).then_inc(attn_part, 1)
                dve.wait_ge(attn_part, part + nl)
                dve.wait_ge(levels, 2 * e + 2)
                dve.copy_predicated(g[:, :], ident[0:n, 0:n].bitcast(I32),
                                    L1[0:n, 3 * P:3 * P + n]).then_inc(attn, 1)

            def sample(u, i):
                i += 4 * u
                dve.wait_ge(ss_prod, i + 1)
                for b in range(2):
                    c = 2 * (i % 4) + b
                    dve.scalar_tensor_tensor(out=ss[:, i % 2, b, :], in0=ss[:, i % 2, b, :],
                                             scalar=eb[:, c:c + 1], in1=X[:, b * HV:(b + 1) * HV],
                                             op0=ALU.mult, op1=ALU.add).then_inc(ss_new, 1)

            def state_of(u, s):
                e, n = ev(u, s), step_cols(s)[1]
                if s == 0:
                    if e:
                        dve.wait_ge(s_saved, 16 * u)
                    dve.wait_ge(s_prod, e + 1)
                    dve.tensor_copy(S[:, :], TB[:, P:P + HV]).then_inc(s_new, 1)
                else:
                    dve.wait_ge(s_prod, e + 1)
                    dve.scalar_tensor_tensor(out=S[:, :], in0=S[:, :], scalar=eb[:, n - 1:n],
                                             in1=TB[:, P:P + HV], op0=ALU.mult, op1=ALU.add).then_inc(s_new, 1)

            def norm(u, s):
                e, n = ev(u, s), step_cols(s)[1]
                dve.wait_ge(o_scaled, e + 1)
                if e:
                    dve.wait_ge(o_turned, e)
                dve.tensor_tensor(og[0:n, :], on[0:n, :], TA[0:n, HV:2 * HV], ALU.mult).then_inc(o_gated, 1)

            def turn(u, s):
                e, n = ev(u, s), step_cols(s)[1]
                dve.wait_ge(ot_hi, e + 1)
                if e:
                    dve.wait_ge(out_done, 2 * e)
                dve.tensor_tensor(otlo[:, :, 0:n], O[:, 0:2 * n].rearrange("p (a c) -> p a c", a=2),
                                  othi[:, :, 0:n].bitcast(F32), ALU.subtract).then_inc(ot_lo, 1)

            def products(u, s):
                e, n = ev(u, s), step_cols(s)[1]
                for half in range(2):
                    dve.wait_ge(out_done, 2 * e + half + 1)
                    dst = y[0:n, s, 512 * half:512 * half + 512]
                    if u == 0:
                        dve.tensor_copy(dst, L[half][0:n, :]).then_inc(added, 1)
                    else:
                        dve.tensor_tensor(dst, dst, L[half][0:n, :], ALU.add).then_inc(added, 1)

            stages = {"decay": decay, "scale": scale, "keys": keys, "levels": levels_of, "sample": sample,
                      "state": state_of, "norm": norm, "turn": turn, "products": products}
            for task in order:
                if task[0] == "split":
                    W.low(dve, m, task[1], w_hi, w_lo)
                elif task[0] == "evac":
                    evac(task[1])
                elif task[0] in stages:
                    stages[task[0]](*task[1:])

        @block.tensor
        def _(pe):
            def piece(i, p):
                t, g = pieces[i]
                if g == 0 and p == 0:
                    pe.wait_ge(w_lo, W.index[("in", t)] + 1)
                if i >= 2 and p == 0:
                    pe.wait_ge(staged[i % 2], i // 2)
                last = project_part(pe, m, t, g, p, PR[i % 2])
                if p == PARTS - 1:
                    last.then_inc(piece_done, 1)

            def values(u, s):
                e, n = ev(u, s), step_cols(s)[1]
                x = tokens(u, s)
                pe.wait_ge(ck_in[e % 2], 16 * (e // 2 + 1))
                if e:
                    pe.wait_ge(o_gated, e)
                for j in range(4):
                    last = pe.transpose(TA[0:n, j * P:(j + 1) * P], x[:, 3 + j, :], ident[:, :])
                last.then_inc(ta_done, 1)

            def keys(u, s):
                e, n = ev(u, s), step_cols(s)[1]
                if e:
                    pe.wait_ge(s_new, e)
                if s == 0:
                    pe.wait_ge(k_ready0, 2 * (u + 1))
                    pe.transpose(TB[0:n, 0:P], kd0[:, :], ident[:, :]).then_inc(tb_done, 1)
                else:
                    pe.wait_ge(k_ready, e + 1)
                    pe.transpose(TB[0:n, 0:P], E[:, 7, :], ident[:, :]).then_inc(tb_done, 1)

            def levels_of(u, s):
                e, n = ev(u, s), step_cols(s)[1]
                x = tokens(u, s)
                nl = len(gla_levels(s)[0])
                pe.wait_ge(q_ready, e + 1)
                pe.wait_ge(k_ready, e + 1)
                if e >= 2:
                    pe.wait_ge(added, 2 * (e - 1))
                for half in range(2):
                    for li in range(4 * half, min(4 * half + 4, nl)):
                        last = pe.matmul(L[half][0:n, (li % 4) * P:(li % 4) * P + n], E[:, li, 0:n],
                                         Eq[:, li, 0:n], start=True, stop=True)
                    if half:
                        last = pe.matmul(L1[0:n, 3 * P:3 * P + n], x[:, 1, :], x[:, 0, :],
                                         start=True, stop=True)
                    last.then_inc(levels, 1)

            def output_free(e):
                if e:
                    pe.wait_ge(ot_lo, e)
                pe.wait_ge(qi_ready, e + 1)
                pe.wait_ge(v_turned, e + 1)

            def sample(u, i):
                n = C0
                if i == 0:
                    output_free(ev(u, 0))
                    pe.wait_ge(qm_ready, u + 1)
                    pe.wait_ge(km_ready, u + 1)
                i += 4 * u
                pe.wait_ge(ss_in[i % 2], 16 * (i // 2 + 1))
                for b in range(2):
                    c = 2 * (i % 4) + b
                    pe.matmul(O[0:n, 0:HV], qm[:, c * C0:(c + 1) * C0], ss[:, i % 2, b, :],
                              start=(c == 0), stop=False)
                if i:
                    pe.wait_ge(ss_new, 2 * i)
                for b in range(2):
                    c = 2 * (i % 4) + b
                    last = pe.matmul(X[:, b * HV:(b + 1) * HV], km[:, c, :], vt[0:n, :],
                                     start=True, stop=True)
                last.then_inc(ss_prod, 1)

            def state_of(u, s):
                e, n = ev(u, s), step_cols(s)[1]
                if s == 0:
                    pe.matmul(TB[:, P:P + HV], km[:, NS, :], vt[0:n, :], start=True, stop=True).then_inc(s_prod, 1)
                else:
                    output_free(e)
                    pe.wait_ge(k_turned, e - u)
                    pe.wait_ge(s_new, e)
                    pe.matmul(O[0:n, 0:HV], qe[:, :], S[:, :], start=True, stop=False)
                    pe.matmul(TB[:, P:P + HV], kt[:, :], vt[:, :], start=True, stop=True).then_inc(s_prod, 1)

            def attend(u, s):
                e, n = ev(u, s), step_cols(s)[1]
                pe.wait_ge(attn, e + 1)
                g = G0 if s == 0 else G
                pe.matmul(O[0:n, 0:HV], g[:, :], vt[0:n, :], start=False, stop=True).then_inc(o_done, 1)

            def turn(u, s):
                e, n = ev(u, s), step_cols(s)[1]
                pe.wait_ge(o_gated, e + 1)
                for j in range(2):
                    last = pe.transpose(O[:, j * n:(j + 1) * n], og[0:n, j * P:(j + 1) * P], ident[0:n, 0:n])
                last.then_inc(o_turned, 1)

            def products(u, s):
                e = ev(u, s)
                pe.wait_ge(ot_lo, e + 1)
                pe.wait_ge(w_lo, W.index[("out", u * WT + WT - 1)] + 1)
                for half in range(2):
                    out_products(pe, m, (othi, otlo), WT, half, L[half]).then_inc(out_done, 1)

            stages = {"piece": piece, "values": values, "keys": keys, "levels": levels_of, "sample": sample,
                      "state": state_of, "attend": attend, "turn": turn, "products": products}
            for task in order:
                if task[0] in stages:
                    stages[task[0]](*task[1:])


def ssd_step_sizes(nc, m, t, w_in, dt_bias, a_log, d_skip, state_conv, acd, conv_sample):
    w, raw, banks, ident = m["w"], m["raw"], m["banks"], m["ident"]
    c0 = SSD_COLS["dt"]
    with ExitStack() as ctx:
        def sb(name, shape):
            return ctx.enter_context(nc.sbuf_tensor("d_" + name, shape, F32))

        def sem(name):
            return nc.alloc_semaphore("d_" + name)

        bias, alog, aexp = sb("bias", [SH, 1]), sb("alog", [SH, 1]), sb("aexp", [SH, 1])
        mask = sb("mask", [SH, T])
        t1, t2, ac = sb("t1", [SH, T]), sb("t2", [SH, T]), sb("ac", [SH, T])
        sel = sb("sel", [SH, DI])
        ea = sb("ea", [SH, NS])
        cs = sb("conv_rows", [3 * NS, CONV])
        (w_raw, small_in, made, zeroed, w_hi, w_lo, projected, aexped, absd, capped, exped, logged,
         dt_done, a_done, scanned, ea_done, turned, kept, conv_in, d_in, stored) = (
            sem(x) for x in ("w_raw", "small_in", "made", "zeroed", "w_hi", "w_lo", "projected", "aexped",
                             "absd", "capped", "exped", "logged", "dt_done", "a_done", "scanned",
                             "ea_done", "turned", "kept", "conv_in", "d_in", "stored"))
        moved = m["conv_old_out"]
        block = ctx.enter_context(nc.Block())
        r = raw[:, 0, 0:KT * SH].rearrange("p (k f) -> p k f", k=KT)
        DTB, ACB, EB, C1, C2 = banks[3], banks[4], banks[5], banks[6], banks[7]

        @block.sync
        def _(sp):
            sp.dma_start(r, w_in[0, :, c0:c0 + SH].rearrange("(k p) f -> p k f", p=P)).then_inc(w_raw, 16)
            sp.dma_start(bias[:, :], dt_bias.rearrange("a h -> h a")).then_inc(small_in, 16)
            sp.dma_start(alog[:, :], a_log.rearrange("a h -> h a")).then_inc(small_in, 16)
            for i in range(3):
                sp.dma_start(cs[NS * i:NS * i + NS, :], state_conv[0, :, i, :]).then_inc(conv_in, 16)
            sp.dma_start(t["dskip"][:, :], d_skip.to_broadcast([P, SH])).then_inc(d_in, 16)
            sp.dma_start(conv_sample[0, :, 0:2, :], state_conv[0, :, 1:3, :]).then_inc(moved, 16)
            sp.wait_ge(scanned, 1)
            sp.dma_start(acd, ac[:, :]).then_inc(stored, 16)
            sp.wait_ge(stored, 16)
            sp.wait_ge(moved, 16)
            sp.wait_ge(d_in, 16)

        @block.gpsimd
        def _(pool):
            pool.memset(w[:, 0, 0, :, :].bitcast(F32), 0.0).then_inc(zeroed, 1)
            pool.memset(w[:, 0, 1, :, :].bitcast(F32), 0.0).then_inc(zeroed, 1)
            n = reset_mask(pool, mask[:, :], made, 0)
            pool.memset(sel[:, :], 1.0).then_inc(made, 1)
            pool.wait_ge(made, n + 1)
            pool.affine_select(out=sel[:, :], in_=sel[:, :], compare_op=ALU.is_ge, fill=0.0, base=0,
                               pattern=[[1, DI]], channel_multiplier=-HD).then_inc(made, 1)
            pool.wait_ge(made, n + 2)
            pool.affine_select(out=sel[:, :], in_=sel[:, :], compare_op=ALU.is_ge, fill=0.0, base=HD - 1,
                               pattern=[[-1, DI]], channel_multiplier=HD).then_inc(made, 1)

        @block.scalar
        def _(act):
            act.wait_ge(zeroed, 2)
            act.wait_ge(w_raw, 16)
            act.activation(w[:, 0, 0, :, 0:SH], r, ACT.Copy).then_inc(w_hi, 1)
            act.wait_ge(small_in, 32)
            act.activation(aexp[:, :], alog[:, :], ACT.Exp).then_inc(aexped, 1)
            for g, (c, n) in enumerate(CGS):
                act.wait_ge(projected, g + 1)
                act.activation(t1[:, c:c + n], banks[g][0:SH, 0:n], ACT.Abs, bias=bias[:, :]).then_inc(absd, 1)
            act.wait_ge(absd, 3)
            act.activation(t1[:, :], t1[:, :], ACT.Exp, scale=-1.0).then_inc(exped, 1)
            act.wait_ge(exped, 1)
            act.activation(t1[:, :], t1[:, :], ACT.Ln, bias=1.0).then_inc(logged, 1)
            act.wait_ge(scanned, 1)
            act.activation(ea[:, :], ac[:, 0:NS], ACT.Exp).then_inc(ea_done, 1)
            act.wait_ge(turned, 1)
            for c, bank in enumerate((C1, C2)):
                act.activation(t["sc"][:, 12 * c:12 * c + 12, :, :],
                               bank[:, 0:12 * 24].rearrange("p (a i b) -> p a i b", a=12, i=3),
                               ACT.Copy).then_inc(kept, 1)
            act.wait_ge(turned, 2)
            for q, n in ((slice(0, 1), C0), (slice(1, STEPS), P)):
                def view(bank):
                    return bank[0:n, 0:STEPS * SH].rearrange("p (s h) -> p s h", h=SH)[:, q, :]
                act.activation(t["dt"][0:n, q, :], view(DTB), ACT.Copy).then_inc(kept, 1)
                act.activation(t["ac"][0:n, q, :], view(ACB), ACT.Copy).then_inc(kept, 1)
            act.activation(t["ecol"][:, :, :], EB[:, 0:P].rearrange("p (a b) -> p a b", a=16),
                           ACT.Copy).then_inc(kept, 1)
            act.wait_ge(kept, 7)

        @block.vector
        def _(dve):
            dve.wait_ge(w_hi, 1)
            dve.tensor_tensor(w[:, 0, 1, :, 0:SH], r, w[:, 0, 0, :, 0:SH].bitcast(F32),
                              ALU.subtract).then_inc(w_lo, 1)
            dve.wait_ge(small_in, 32)
            for g, (c, n) in enumerate(CGS):
                dve.wait_ge(absd, g + 1)
                dve.tensor_scalar(t2[:, c:c + n], banks[g][0:SH, 0:n], bias[:, :], 0.0, ALU.add,
                                  ALU.max).then_inc(capped, 1)
            dve.wait_ge(capped, 3)
            dve.wait_ge(logged, 1)
            dve.tensor_tensor(t2[:, :], t2[:, :], t1[:, :], ALU.add).then_inc(dt_done, 1)
            dve.wait_ge(dt_done, 1)
            dve.wait_ge(aexped, 1)
            dve.tensor_scalar(t1[:, :], t2[:, :], aexp[:, :], -1.0, ALU.mult, ALU.mult).then_inc(a_done, 1)
            dve.wait_ge(a_done, 1)
            dve.wait_ge(made, 1 + STEPS)
            dve.tensor_tensor_scan(ac[:, :], mask[:, :], t1[:, :], 0.0, ALU.mult, ALU.add).then_inc(scanned, 1)

        @block.tensor
        def _(pe):
            narrow_projection(pe, m, SH, w_lo, None, projected)
            pe.wait_ge(conv_in, 48)
            for a in range(24):
                bank = (C1, C2)[a // 12]
                last = pe.transpose(bank[:, (a % 12) * 24:(a % 12) * 24 + 24], cs[:, a * P:(a + 1) * P],
                                    ident[0:24, 0:24])
            last.then_inc(turned, 1)
            pe.wait_ge(dt_done, 1)
            pe.wait_ge(scanned, 1)
            pe.wait_ge(ea_done, 1)
            pe.wait_ge(made, 1 + STEPS + 3)
            for s in range(STEPS):
                c, n = step_cols(s)
                pe.transpose(DTB[0:n, s * SH:(s + 1) * SH], t2[:, c:c + n], ident[0:SH, 0:SH])
                pe.transpose(ACB[0:n, s * SH:(s + 1) * SH], ac[:, c:c + n], ident[0:SH, 0:SH])
            for a in range(16):
                last = pe.matmul(EB[:, a * NS:(a + 1) * NS], sel[:, a * P:(a + 1) * P], ea[:, :],
                                 start=True, stop=True)
            last.then_inc(turned, 1)


def ssd_layer(nc, m, tab, sq, acd, w_in, w_out, state, state_prompt, state_sample, conv_prompt,
              conv_sample):
    NT, WT = 10, 4
    convs = set(range(6))
    step = [("load", 1), ("inputs", 0), ("fill", 1), ("scan", 0), ("gates", 0), ("fill", 1), ("norm", 0),
            ("products", -1), ("fill", 1), ("turn", 0), ("decay", 1), ("fill", 0.7)]
    first = step[:3]
    for i in range(NS):
        first += [("sample", i), ("fill", 0.4)]
    first += step[3:8] + [("weights", 0)] + step[8:]
    order, pieces, weights, last_piece = interleave(NT, convs, WT, 7, first, step, ["keep"], ["products"])

    def column(t):
        g, j = divmod(t, NT)
        if j < 4:
            return SSD_COLS["x"] + g * 512 + j * P
        if j < 6:
            return SSD_COLS["B" if j == 4 else "C"] + g * P
        return SSD_COLS["z"] + g * 512 + (j - 6) * P

    def channel(t):
        g, j = divmod(t, NT)
        return 4 * g + j if j < 4 else 16 + 4 * (j - 4) + g

    W = Weights(weights, pieces, w_in[0], w_out[0], column, NT, WT, 0)
    PA, PB, X, Z, M, Y1, Y2, SU = m["banks"]
    PR, Y, ident, y_acc = (PA, PB), (Y1, Y2), m["ident"], m["y"]
    conv_index = {p: i for i, p in enumerate(p for p in pieces if p[0] % NT in convs and p[1] < 3)}
    where = {p: i for i, p in enumerate(pieces)}
    rows_before = [[], []]
    for i, (t, g) in enumerate(pieces):
        for par in range(2):
            rows_before[par].append((rows_before[par][-1] if i else 0) +
                                    (1 if i and (i - 1) % 2 == par and pieces[i - 1][1] < 3 else 0))

    def tile_index(t):
        return 6 * (t // NT) + t % NT

    with ExitStack() as ctx:
        def sb(name, shape, dt=F32):
            return ctx.enter_context(nc.sbuf_tensor("s_" + name, shape, dt))

        def sem(name):
            return nc.alloc_semaphore("s_" + name)

        pre = sb("pre", [P, 2, 353])
        cu = sb("conv", [P, 2, 350])
        th = sb("tanh", [P, 2, 350])
        cvp, cvo = sb("cv_cols", [P, 2, 11]), sb("cv_rows", [11, P])
        ck = sb("chunk", [P, 2, 6, P])
        zc = sb("z", [P, 4, P])
        acb = sb("decay", [P, 2, HPG, P])
        el, wl, ea = sb("e_last", [P, HPG]), sb("w_last", [P, HPG]), sb("e_sum", [P, HPG])
        bt, cbm = sb("b_turned", [P, P]), sb("cb", [P, P])
        xdt, xw, y = sb("xdt", [P, 512]), sb("xw", [P, 512]), sb("ys", [P, 512])
        ythi, ytlo = sb("yt_hi", [P, 4, P], F32R), sb("yt_lo", [P, 4, P], F32R)
        S = sb("state", [P, 512])
        cm = sb("c_masked", [P, NS * C0])
        bm = sb("b_masked", [C0, P])
        meta_row = sb("meta_row", [C0, 1])
        ss = sb("sample_state", [P, 2, 4, P])
        ysum, ymean, yrstd, power = (sb(x, [P, 1]) for x in ("ysum", "ymean", "yrstd", "power"))

        raw_in = [sem(f"raw_in{i}") for i in range(2)]
        bank_free = [sem(f"bank_free{i}") for i in range(2)]
        stored = [sem(f"stored{i}") for i in range(2)]
        cv_stored, s_saved = m["conv_out"], m["ssm_state_out"]
        ck_in = [sem(f"ck_in{i}") for i in range(2)]
        acb_in = [sem(f"acb_in{i}") for i in range(2)]
        ss_in = [sem(f"ss_in{i}") for i in range(2)]
        ss_out = [m[f"ssm_sample_out{i}"] for i in range(2)]
        (w_hi, w_lo, piece_done, z_in, convolved, tanhed, silued, cv_packed, consts, zeros, chain) = (
            sem(x) for x in ("w_hi", "w_lo", "piece_done", "z_in", "convolved", "tanhed", "silued",
                             "cv_packed", "consts", "zeros", "chain"))
        gaps = sem("gaps")
        (turned, b_turned, el_done, decays, cb_masked, xdt_ready, xw_ready, attn, intra, inter, s_prod,
         s_new, y_summed, z_turned, gated, squared, meant, rooted, y_normed, y_turned, yt_hi, yt_lo,
         out_done, added) = (sem(x) for x in (
             "turned", "b_turned", "el_done", "decays", "cb_masked", "xdt_ready", "xw_ready", "attn",
             "intra", "inter", "s_prod", "s_new", "y_summed", "z_turned", "gated", "squared", "meant",
             "rooted", "y_normed", "y_turned", "yt_hi", "yt_lo", "out_done", "added"))
        (cm_ready, bm_ready, ss_turned, ss_copied, ss_inter, ss_prod, ss_new, s_turned, s_kept) = (sem(x) for x in ("cm_ready", "bm_ready", "ss_turned", "ss_copied", "ss_inter",
                                      "ss_prod", "ss_new", "s_turned", "s_kept"))
        block = ctx.enter_context(nc.Block())

        def ev(u, s):
            return u * STEPS + s

        def tokens(u, s):
            return ck[:, ev(u, s) % 2, :, 0:step_cols(s)[1]]

        def decay(u, s):
            return acb[:, ev(u, s) % 2, :, 0:step_cols(s)[1]]

        def tanh_count(i):
            return tanh_order[i] + 1

        tanh_order = {}
        for task in order:
            if task[0] in ("evac", "finish"):
                j, g = pieces[task[1]][0] % NT, pieces[task[1]][1]
                if g < 3 and (j in convs) == (task[0] == "finish"):
                    tanh_order[task[1]] = len(tanh_order)

        @block.sync
        def _(sp):
            def store(i):
                t, g = pieces[i]
                u, j = divmod(t, NT)
                if g == 3:
                    q, a = tile_index(t), channel(t)
                    sp.wait_ge(bank_free[i % 2], i // 2 + 1)
                    sp.dma_start(conv_prompt[0, 0, :, a * P:(a + 1) * P],
                                 cvo[0:3, :]).then_inc(cv_stored, 16)
                    sp.dma_start(conv_sample[0, :, 2, a * P:(a + 1) * P],
                                 cvo[3:11, :]).then_inc(cv_stored, 16)
                    return
                c, n = CGS[g]
                if j in convs:
                    sp.wait_ge(silued, conv_index[(t, g)] + 1)
                else:
                    sp.wait_ge(bank_free[i % 2], i // 2 + 1)
                sp.dma_start(sq[u, j * P:(j + 1) * P, c:c + n], th[:, i % 2, 0:n]).then_inc(stored[i % 2], 16)

            def load(u, s):
                e = ev(u, s)
                c, n = step_cols(s)
                if s == 0:
                    for par in range(2):
                        n_rows = rows_before[par][last_piece[u]] + (1 if last_piece[u] % 2 == par and
                                                                    pieces[last_piece[u]][1] < 3 else 0)
                        sp.wait_ge(stored[par], 16 * n_rows)
                if e >= 2:
                    sp.wait_ge(intra, e - 1)
                    sp.wait_ge(s_prod, e - 1)
                    if s in (1, 2):
                        sp.wait_ge(cm_ready, u + 1 if s == 2 else max(u, 0))
                sp.dma_start(tokens(u, s), sq[u, 0:6 * P, c:c + n].rearrange("(t p) c -> p t c", p=P)).then_inc(
                    ck_in[e % 2], 16)
                sp.dma_start(decay(u, s), acd[HPG * u:HPG * u + HPG, c:c + n].unsqueeze(0).to_broadcast(
                    [P, HPG, n])).then_inc(acb_in[e % 2], 16)

            def load_z(u, s):
                e = ev(u, s)
                c, n = step_cols(s)
                if e:
                    sp.wait_ge(z_turned, e)
                sp.dma_start(zc[:, :, 0:n], sq[u, 6 * P:10 * P, c:c + n].rearrange("(t p) c -> p t c", p=P)).then_inc(
                    z_in, 16)

            W.load(sp, m, 0, raw_in, w_lo)
            W.load(sp, m, 1, raw_in, w_lo)
            for task in order:
                if task[0] == "split" and task[1] + 2 < len(weights):
                    W.load(sp, m, task[1] + 2, raw_in, w_lo)
                elif task[0] == "store":
                    store(task[1])
                elif task[0] == "load":
                    load(*task[1:])
                elif task[0] == "inputs":
                    load_z(*task[1:])
            sp.wait_ge(cv_stored, 32 * 6 * U)
            for i in range(2):
                sp.wait_ge(stored[i], 16 * (rows_before[i][-1] + (1 if (len(pieces) - 1) % 2 == i and
                                                                  pieces[-1][1] < 3 else 0)))

        @block.gpsimd
        def _(pool):
            pool.memset(meta_row[:, :], 1.0).then_inc(consts, 1)
            pool.memset(power[:, :], -0.5).then_inc(consts, 1)
            pool.wait_ge(consts, 2)
            pool.affine_select(out=meta_row[:, :], in_=meta_row[:, :], compare_op=ALU.is_ge,
                               fill=0.0, base=-NS, pattern=[[0, 1]], channel_multiplier=1).then_inc(consts, 1)
            def sample_state(i, out):
                u, b = divmod(i, NS)
                view = (state_sample if out else state)[0, b, HPG * u:HPG * u + HPG].rearrange(
                    "(t two) p n -> (two p) t n", two=2)
                if out:
                    pool.wait_ge(ss_new, i + 1)
                    pool.dma_start(view, ss[:, i % 2, :, :]).then_inc(ss_out[i % 2], 16)
                else:
                    if i >= 2:
                        pool.wait_ge(ss_out[i % 2], 16 * (i // 2))
                    if i and i % NS < 1:
                        pool.wait_ge(s_saved, 16 * u)
                    pool.dma_start(ss[:, i % 2, :, :], view).then_inc(ss_in[i % 2], 16)

            sample_state(0, False)
            sample_state(1, False)
            for task in order:
                if task[0] == "sample":
                    i = NS * task[1] + task[2]
                    sample_state(i, True)
                    if task[2] + 2 < NS:
                        sample_state(i + 2, False)
                elif task[0] == "norm":
                    e, n = ev(*task[1:]), step_cols(task[2])[1]
                    pool.wait_ge(squared, e + 1)
                    pool.tensor_scalar(ymean[0:n, :], ysum[0:n, :], 1.0 / 512, 4 * EPS, ALU.mult,
                                       ALU.add).then_inc(meant, 1)
                    pool.wait_ge(meant, e + 1)
                    if e:
                        pool.wait_ge(y_normed, e)
                    pool.tensor_tensor(yrstd[0:n, :], ymean[0:n, :], power[0:n, :],
                                       ALU.pow).then_inc(rooted, 1)
                elif task[0] == "keep":
                    u = task[1]
                    pool.wait_ge(s_kept, u + 1)
                    pool.dma_start(state_prompt[0, 0, HPG * u:HPG * u + HPG].rearrange(
                        "(t two) p n -> (two p) t n", two=2), ss[:, 0, :, :]).then_inc(s_saved, 16)
                    if u + 1 < U:
                        sample_state(NS * (u + 1) + 1, False)
                        sample_state(NS * (u + 1), False)
            pool.wait_ge(s_saved, 16 * U)
            for i in range(2):
                pool.wait_ge(ss_out[i], 16 * U * NS // 2)

        @block.scalar
        def _(act):
            def evac(i):
                t, g = pieces[i]
                j = t % NT
                act.wait_ge(piece_done, i + 1)
                bank = PR[i % 2]
                if g == 3:
                    q = tile_index(t)
                    if q:
                        act.wait_ge(cv_stored, 32 * q)
                    act.activation(cvo[:, :], bank[0:11, 0:P], ACT.Copy).then_inc(bank_free[i % 2], 1)
                elif j in convs:
                    c, n = CGS[g]
                    ci, q = conv_index[(t, g)], tile_index(t)
                    if ci >= 2:
                        act.wait_ge(convolved, ci - 1)
                    if ci >= 1 and g == 0:
                        act.wait_ge(cv_packed, q)
                    if g == 0:
                        if q >= 2:
                            act.wait_ge(piece_done, where[(prev_tile[prev_tile[t]], 3)] + 1)
                        act.activation(cvp[:, q % 2, 3:11], bank[:, 0:NS], ACT.Copy)
                        act.activation(pre[:, ci % 2, 3:3 + n - NS], bank[:, NS:n],
                                       ACT.Copy).then_inc(bank_free[i % 2], 1)
                    else:
                        if g == 2:
                            act.wait_ge(convolved, ci)
                        act.activation(pre[:, ci % 2, 3:3 + n], bank[:, 0:n],
                                       ACT.Copy).then_inc(bank_free[i % 2], 1)
                else:
                    n = CGS[g][1]
                    act.wait_ge(stored[i % 2], 16 * rows_before[i % 2][i])
                    act.activation(th[:, i % 2, 0:n], bank[:, 0:n], ACT.Tanh, scale=0.5).then_inc(tanhed, 1)

            prev_tile, last = {}, None
            for t in range(U * NT):
                if t % NT in convs:
                    prev_tile[t] = last
                    last = t

            def finish(i):
                t, g = pieces[i]
                if t % NT not in convs or g == 3:
                    return
                n = CGS[g][1]
                act.wait_ge(convolved, conv_index[(t, g)] + 1)
                act.wait_ge(stored[i % 2], 16 * rows_before[i % 2][i])
                act.activation(th[:, i % 2, 0:n], cu[:, i % 2, 0:n], ACT.Tanh).then_inc(tanhed, 1)

            def decay_of(u, s):
                e, n = ev(u, s), step_cols(s)[1]
                L = decay(u, s)
                act.wait_ge(acb_in[e % 2], 16 * (e // 2 + 1))
                if e:
                    act.wait_ge(s_new, e)
                    act.wait_ge(y_summed, e)
                act.activation(ea[0:n, :], tab["ac"][0:n, s, HPG * u:HPG * u + HPG], ACT.Exp)
                act.activation(el[:, :].unsqueeze(2), L[:, :, n - 1:n], ACT.Exp).then_inc(el_done, 1)
                act.wait_ge(el_done, e + 1)
                for r in range(HPG):
                    h = HPG * u + r
                    last = act.activation(L[0:n, r, :], L[0:n, r, :], ACT.Relu, scale=-1.0,
                                          bias=tab["ac"][0:n, s, h:h + 1])
                last.then_inc(gaps, 1)
                act.wait_ge(gaps, e + 1)
                act.activation(L[0:n], L[0:n], ACT.Exp, scale=-1.0).then_inc(decays, 1)

            def inputs(u, s):
                e, n = ev(u, s), step_cols(s)[1]
                act.wait_ge(turned, e + 1)
                if e:
                    act.wait_ge(s_prod, e)
                act.activation(bt[0:n, :], M[0:n, 0:P], ACT.Copy).then_inc(b_turned, 1)

            def sample(u, i):
                if i == 0 and u:
                    act.wait_ge(y_turned, ev(u, 0))
                act.wait_ge(ss_turned, NS * u + i + 1)
                if i:
                    act.wait_ge(ss_inter, NS * u + i - u)
                act.activation(y[:, :], SU[:, :], ACT.Copy).then_inc(ss_copied, 1)

            def norm(u, s):
                e, n = ev(u, s), step_cols(s)[1]
                act.wait_ge(gated, e + 1)
                if e:
                    act.wait_ge(rooted, e)
                act.wait_ge(intra, e + 1)
                act.activation(xdt[0:n, :], y[0:n, :], ACT.Square, accum_out=ysum[0:n, :]).then_inc(squared, 1)
                act.wait_ge(rooted, e + 1)
                act.activation(y[0:n, :], y[0:n, :], ACT.Copy, scale=yrstd[0:n, :]).then_inc(y_normed, 1)

            def turn(u, s):
                e, n = ev(u, s), step_cols(s)[1]
                act.wait_ge(y_turned, e + 1)
                if e:
                    act.wait_ge(out_done, 2 * e)
                act.activation(ythi[:, :, 0:n], X[:, 0:4 * n].rearrange("p (a c) -> p a c", a=4),
                               ACT.Copy).then_inc(yt_hi, 1)

            def keep(u):
                act.wait_ge(s_turned, u + 1)
                act.wait_ge(ss_out[0], 16 * (u + 1) * NS // 2)
                act.activation(ss[:, 0, :, :], Z[:, :].rearrange("p (a n) -> p a n", a=4),
                               ACT.Copy).then_inc(s_kept, 1)

            act.wait_ge(zeros, 3)
            stages = {"evac": evac, "finish": finish, "decay": decay_of, "inputs": inputs, "sample": sample,
                      "norm": norm, "turn": turn, "keep": keep}
            for task in order:
                if task[0] == "split":
                    W.high(act, m, task[1], raw_in, w_hi, piece_done, out_done)
                elif task[0] in stages:
                    stages[task[0]](*task[1:])

        @block.vector
        def _(dve):
            links = [0]

            def link(ins):
                links[0] += 1
                ins.then_inc(chain, 1)
                dve.wait_ge(chain, links[0])

            dve.memset(ythi[:, :, :].bitcast(F32), 0.0).then_inc(zeros, 1)
            dve.memset(ytlo[:, :, :].bitcast(F32), 0.0).then_inc(zeros, 1)
            dve.memset(cm[:, :], 0.0).then_inc(zeros, 1)
            dve.wait_ge(zeros, 3)
            dve.wait_ge(consts, 3)
            cw = m["cw"]

            def evac(i):
                t, g = pieces[i]
                j, n = t % NT, CGS[min(g, 2)][1]
                if g == 3:
                    return
                if j not in convs:
                    dve.wait_ge(tanhed, tanh_count(i))
                    dve.scalar_tensor_tensor(out=th[:, i % 2, 0:n], in0=th[:, i % 2, 0:n], scalar=1.0,
                                             in1=PR[i % 2][:, 0:n], op0=ALU.add,
                                             op1=ALU.mult).then_inc(bank_free[i % 2], 1)
                    return
                ci, q, a = conv_index[(t, g)], tile_index(t), channel(t)
                p, u = pre[:, ci % 2, :], cu[:, i % 2, :]
                dve.wait_ge(bank_free[i % 2], i // 2 + 1)
                if ci >= 1:
                    dve.wait_ge(silued, done_before(i))
                off = NS if g == 0 else 0
                if g == 0:
                    link(dve.memset(p[:, 0:3], 0.0))
                else:
                    w = CGS[g - 1][1] - (NS if g == 1 else 0)
                    link(dve.tensor_copy(p[:, 0:3], pre[:, (ci + 1) % 2, w:w + 3]))
                if g == 2:
                    dve.tensor_copy(cvp[:, q % 2, 0:3], p[:, n:n + 3]).then_inc(cv_packed, 1)
                if g == 0:
                    old, new = tab["sc"][:, a, :, :], cvp[:, q % 2, 3:11]
                    taps = [old[:, 0, :], old[:, 1, :], old[:, 2, :], new]
                    link(dve.tensor_scalar(u[:, 0:NS], taps[0], cw[:, 0, a:a + 1], cw[:, 4, a:a + 1],
                                           ALU.mult, ALU.add))
                    for k in range(1, 4):
                        link(dve.scalar_tensor_tensor(out=u[:, 0:NS], in0=taps[k], scalar=cw[:, k, a:a + 1],
                                                      in1=u[:, 0:NS], op0=ALU.mult, op1=ALU.add))
                w = n - off
                link(dve.tensor_scalar(u[:, off:n], p[:, 0:w], cw[:, 0, a:a + 1], cw[:, 4, a:a + 1],
                                       ALU.mult, ALU.add))
                for k in range(1, 4):
                    ins = dve.scalar_tensor_tensor(out=u[:, off:n], in0=p[:, k:k + w],
                                                   scalar=cw[:, k, a:a + 1], in1=u[:, off:n],
                                                   op0=ALU.mult, op1=ALU.add)
                    if k < 3:
                        link(ins)
                    else:
                        ins.then_inc(convolved, 1)

            silu_order = []

            def done_before(i):
                return len([x for x in silu_order if x <= i - 2])

            def finish(i):
                t, g = pieces[i]
                if t % NT not in convs or g == 3:
                    return
                n = CGS[g][1]
                silu_order.append(i)
                dve.wait_ge(tanhed, tanh_count(i))
                dve.scalar_tensor_tensor(out=th[:, i % 2, 0:n], in0=th[:, i % 2, 0:n], scalar=1.0,
                                         in1=cu[:, i % 2, 0:n], op0=ALU.add, op1=ALU.mult).then_inc(silued, 1)

            def heads(x, n, w=HD):
                return x.unsqueeze(2).to_broadcast([n, HPG, w])

            def split_heads(x):
                return x.rearrange("p (r c) -> p r c", r=HPG)

            def inputs(u, s):
                e, n = ev(u, s), step_cols(s)[1]
                L, x = decay(u, s), tokens(u, s)
                hs = slice(HPG * u, HPG * u + HPG)
                dve.wait_ge(b_turned, e + 1)
                tri = m["tri0"] if s == 0 else m["tri"]
                dve.tensor_tensor(cbm[0:n, 0:n], M[0:n, P:P + n], tri[:, :], ALU.mult).then_inc(cb_masked, 1)
                if e:
                    dve.wait_ge(intra, e)
                    dve.wait_ge(s_prod, e)
                    if s == 1:
                        dve.wait_ge(ss_prod, NS * (u + 1))
                    dve.wait_ge(squared, e)
                dve.tensor_tensor(split_heads(xdt[0:n, :]), split_heads(X[0:n, :]),
                                  heads(tab["dt"][0:n, s, hs], n), ALU.mult).then_inc(xdt_ready, 1)
                dve.wait_ge(decays, e + 1)
                dve.wait_ge(acb_in[e % 2], 16 * (e // 2 + 1))
                last = L[0:n, :, n - 1:n].rearrange("p r o -> p (r o)")
                if s:
                    link(dve.tensor_copy(wl[0:n, :], last))
                else:
                    link(dve.tensor_scalar(wl[0:n, :], last, meta_row[:, :], None, ALU.mult))
                dve.wait_ge(xdt_ready, e + 1)
                dve.tensor_tensor(split_heads(xw[0:n, :]), split_heads(xdt[0:n, :]), heads(wl[0:n, :], n),
                                  ALU.mult).then_inc(xw_ready, 1)
                dve.wait_ge(cb_masked, e + 1)
                dve.tensor_tensor(L[0:n], L[0:n], cbm[0:n, 0:n].unsqueeze(1).to_broadcast([n, HPG, n]),
                                  ALU.mult).then_inc(attn, 1)
                if s == 0:
                    dve.wait_ge(ck_in[e % 2], 16 * (e // 2 + 1))
                    dve.tensor_copy(cm[:, 0:(NS - 1) * (C0 + 1) + 1:C0 + 1], x[:, 5, 0:NS]).then_inc(cm_ready, 1)
                    mask_b(NS * u)

            def mask_b(i):
                if i:
                    dve.wait_ge(ss_prod, i)
                dve.tensor_scalar(bm[:, :], bt[0:C0, :], ident[0:C0, i % NS:i % NS + 1], None,
                                  ALU.mult).then_inc(bm_ready, 1)

            def sample(u, b):
                i = NS * u + b
                st = ss[:, i % 2, :, :]
                dve.wait_ge(ss_turned, i + 1)
                dve.wait_ge(ss_in[i % 2], 16 * (i // 2 + 1))
                link(dve.tensor_tensor(st, st, tab["ecol"][:, 4 * u:4 * u + 4, b:b + 1].to_broadcast(
                    [P, 4, P]), ALU.mult))
                dve.wait_ge(ss_prod, i + 1)
                dve.tensor_tensor(st, st, Z[:, :].rearrange("p (a n) -> p a n", a=4),
                                  ALU.add).then_inc(ss_new, 1)
                if b + 1 < NS:
                    mask_b(i + 1)

            def scan(u, s):
                e, n = ev(u, s), step_cols(s)[1]
                hs = slice(HPG * u, HPG * u + HPG)
                if s == 0:
                    if u:
                        dve.wait_ge(s_turned, u)
                    dve.wait_ge(s_prod, e + 1)
                    dve.tensor_copy(S[:, :], SU[:, :]).then_inc(s_new, 1)
                else:
                    dve.wait_ge(s_prod, e + 1)
                    dve.wait_ge(el_done, e + 1)
                    link(dve.tensor_tensor(split_heads(S[:, :]), split_heads(S[:, :]), heads(el[:, :], P),
                                           ALU.mult))
                    dve.tensor_tensor(S[:, :], S[:, :], SU[:, :], ALU.add).then_inc(s_new, 1)
                dve.wait_ge(inter, e + 1)
                dve.wait_ge(el_done, e + 1)
                if e:
                    dve.wait_ge(y_turned, e)
                link(dve.tensor_tensor(split_heads(y[0:n, :]), split_heads(Y2[0:n, :]),
                                       heads(ea[0:n, :], n), ALU.mult))
                dve.wait_ge(intra, e + 1)
                link(dve.tensor_tensor(y[0:n, :], y[0:n, :], Y1[0:n, :], ALU.add))
                link(dve.tensor_tensor(split_heads(xw[0:n, :]), split_heads(X[0:n, :]),
                                       heads(tab["dskip"][0:n, hs], n), ALU.mult))
                dve.tensor_tensor(y[0:n, :], y[0:n, :], xw[0:n, :], ALU.add).then_inc(y_summed, 1)

            def norm(u, s):
                e, n = ev(u, s), step_cols(s)[1]
                dve.wait_ge(z_turned, e + 1)
                dve.wait_ge(y_summed, e + 1)
                dve.tensor_tensor(y[0:n, :], y[0:n, :], Z[0:n, :], ALU.mult).then_inc(gated, 1)

            def turn(u, s):
                e, n = ev(u, s), step_cols(s)[1]
                dve.wait_ge(yt_hi, e + 1)
                dve.tensor_tensor(ytlo[:, :, 0:n], X[:, 0:4 * n].rearrange("p (a c) -> p a c", a=4),
                                  ythi[:, :, 0:n].bitcast(F32), ALU.subtract).then_inc(yt_lo, 1)

            def products(u, s):
                e, n = ev(u, s), step_cols(s)[1]
                for half in range(2):
                    dve.wait_ge(out_done, 2 * e + half + 1)
                    dst = y_acc[0:n, s, 512 * half:512 * half + 512]
                    if u == 0:
                        dve.tensor_copy(dst, Y[half][0:n, :]).then_inc(added, 1)
                    else:
                        dve.tensor_tensor(dst, dst, Y[half][0:n, :], ALU.add).then_inc(added, 1)

            stages = {"evac": evac, "finish": finish, "inputs": inputs, "sample": sample, "scan": scan,
                      "norm": norm, "turn": turn, "products": products}
            for task in order:
                if task[0] == "split":
                    W.low(dve, m, task[1], w_hi, w_lo)
                elif task[0] in stages:
                    stages[task[0]](*task[1:])

        @block.tensor
        def _(pe):
            def piece(i, p):
                t, g = pieces[i]
                if g == 0 and p == 0:
                    pe.wait_ge(w_lo, W.index[("in", t)] + 1)
                if i >= 2 and p == 0:
                    pe.wait_ge(bank_free[i % 2], i // 2)
                if g == 3:
                    q = tile_index(t)
                    pe.wait_ge(cv_packed, q + 1)
                    pe.transpose(PR[i % 2][0:11, 0:P], cvp[:, q % 2, :], ident[:, :]).then_inc(piece_done, 1)
                else:
                    last = project_part(pe, m, t, g, p, PR[i % 2])
                    if p == PARTS - 1:
                        last.then_inc(piece_done, 1)

            def inputs(u, s):
                e, n = ev(u, s), step_cols(s)[1]
                x = tokens(u, s)
                pe.wait_ge(ck_in[e % 2], 16 * (e // 2 + 1))
                if e:
                    pe.wait_ge(yt_lo, e)
                    pe.wait_ge(cb_masked, e)
                for j in range(4):
                    pe.transpose(X[0:n, j * P:(j + 1) * P], x[:, j, :], ident[:, :])
                pe.transpose(M[0:n, 0:P], x[:, 4, :], ident[:, :])
                pe.matmul(M[0:n, P:P + n], x[:, 4, :], x[:, 5, :], start=True, stop=True).then_inc(turned, 1)

            def banks_free(e):
                if e >= 2:
                    pe.wait_ge(added, 2 * (e - 1))
                if e:
                    pe.wait_ge(y_summed, e)
                    pe.wait_ge(s_new, e)

            def sample(u, b):
                n, i = C0, NS * u + b
                if b == 0:
                    banks_free(ev(u, 0))
                    pe.wait_ge(cm_ready, u + 1)
                    pe.wait_ge(xdt_ready, ev(u, 0) + 1)
                    if u:
                        pe.wait_ge(s_kept, u)
                pe.wait_ge(ss_in[i % 2], 16 * (i // 2 + 1))
                if b:
                    pe.wait_ge(ss_copied, i)
                for j in range(4):
                    last = pe.transpose(SU[:, j * P:(j + 1) * P], ss[:, i % 2, j, :], ident[:, :])
                last.then_inc(ss_turned, 1)
                pe.wait_ge(bm_ready, i + 1)
                if b:
                    pe.wait_ge(ss_new, i)
                for j in range(4):
                    last = pe.matmul(Z[:, j * P:(j + 1) * P], xdt[0:n, j * P:(j + 1) * P],
                                     bm[:, :], start=True, stop=True)
                last.then_inc(ss_prod, 1)
                pe.wait_ge(ss_copied, i + 1)
                pe.matmul(Y2[0:n, :], cm[:, b * C0:(b + 1) * C0], y[:, :], start=(b == 0),
                          stop=(b == NS - 1)).then_inc(inter if b == NS - 1 else ss_inter, 1)

            def scan(u, s):
                e, n = ev(u, s), step_cols(s)[1]
                x, G = tokens(u, s), decay(u, s)
                if s:
                    banks_free(e)
                    pe.matmul(Y2[0:n, :], x[:, 5, :], S[:, :], start=True, stop=True).then_inc(inter, 1)
                pe.wait_ge(xw_ready, e + 1)
                pe.wait_ge(b_turned, e + 1)
                pe.matmul(SU[:, :], bt[0:n, :], xw[0:n, :], start=True, stop=True).then_inc(s_prod, 1)
                pe.wait_ge(attn, e + 1)
                for r in range(HPG):
                    last = pe.matmul(Y1[0:n, r * HD:(r + 1) * HD], G[0:n, r, :],
                                     xdt[0:n, r * HD:(r + 1) * HD], start=True, stop=True)
                last.then_inc(intra, 1)

            def gates(u, s):
                e, n = ev(u, s), step_cols(s)[1]
                pe.wait_ge(z_in, 16 * (e + 1))
                if e:
                    pe.wait_ge(gated, e)
                if s == 0:
                    pe.wait_ge(ss_new, NS * (u + 1))
                for j in range(4):
                    last = pe.transpose(Z[0:n, j * P:(j + 1) * P], zc[:, j, 0:n], ident[:, :])
                last.then_inc(z_turned, 1)

            def turn(u, s):
                e, n = ev(u, s), step_cols(s)[1]
                pe.wait_ge(y_normed, e + 1)
                for j in range(4):
                    last = pe.transpose(X[:, j * n:(j + 1) * n], y[0:n, j * P:(j + 1) * P], ident[0:n, 0:n])
                last.then_inc(y_turned, 1)

            def products(u, s):
                e = ev(u, s)
                pe.wait_ge(yt_lo, e + 1)
                pe.wait_ge(y_summed, min(e + 2, U * STEPS))
                pe.wait_ge(w_lo, W.index[("out", u * WT + WT - 1)] + 1)
                for half in range(2):
                    out_products(pe, m, (ythi, ytlo), WT, half, Y[half]).then_inc(out_done, 1)

            def keep(u):
                pe.wait_ge(s_new, STEPS * (u + 1))
                pe.wait_ge(gated, STEPS * (u + 1))
                for j in range(4):
                    last = pe.transpose(Z[:, j * P:(j + 1) * P], S[:, j * P:(j + 1) * P], ident[:, :])
                last.then_inc(s_turned, 1)

            stages = {"piece": piece, "inputs": inputs, "sample": sample, "scan": scan, "gates": gates,
                      "turn": turn, "products": products, "keep": keep}
            for task in order:
                if task[0] in stages:
                    stages[task[0]](*task[1:])


_INS = ["x_prompt", "x_sample", "state_gla", "state_ssm", "state_conv", "meta_tokens", "pre_norm",
        "post_norm", "gla_w_in", "gla_w_gate_up", "gla_b_gate", "gla_w_norm", "gla_w_out", "ssd_w_in",
        "ssd_conv_w", "ssd_conv_b", "ssd_dt_bias", "ssd_a_log", "ssd_d_skip", "ssd_w_norm", "ssd_w_out"]
_OUTS = [(1, SEQ, D), (NS, 1, D), (1, 1, U, HK, HV), (1, 1, SH, HD, P), (1, 1, 3, CONV),
         (1, NS, U, HK, HV), (1, NS, SH, HD, P), (1, NS, 3, CONV)]


def kernel(**inputs):
    import numpy as _np
    import concourse.bacc as _bacc
    from concourse import mybir as _mybir
    from concourse.bass_utils import run_bass_kernel_spmd as _run

    nc = _bacc.Bacc("TRN2", target_bir_lowering=False, num_devices=1)
    arrays, args = {}, []
    for name in _INS:
        a = _np.ascontiguousarray(inputs[name])
        arrays[f"in_{name}_dram"] = a
        args.append(nc.dram_tensor(f"in_{name}_dram", a.shape, _mybir.dt.from_np(a.dtype), kind="ExternalInput").ap())
    for i, shape in enumerate(_OUTS):
        args.append(nc.dram_tensor(f"out_{i}_dram", shape, _mybir.dt.float32, kind="ExternalOutput").ap())
    hybrid_kernel(nc, *args)
    r = _run(nc, [arrays], core_ids=[0])
    return tuple(r.results[0][f"out_{i}_dram"] for i in range(len(_OUTS)))
```

```python
from contextlib import ExitStack

import concourse.bass as bass
from concourse import mybir

F32 = mybir.dt.float32
F32R = mybir.dt.float32r
I32 = mybir.dt.int32
ALU = mybir.AluOpType
ACT = mybir.ActivationFunctionType

P = 128
D = 1024
KT = D // P
NS = 8
NM = 16
SEQ = 1024
C0 = NS + NM
T = C0 + SEQ
STEPS = 1 + SEQ // P
EPS = 1e-6
U = 4
HK = 128
HV = 256
TAU = 16.0
GR = 16
SH = 32
HPG = 8
HD = 64
DI = 2048
CONV = 3072
CGS = [(0, 350), (350, 350), (700, 348)]
GLA_COLS = {"q": 0, "k": 512, "v": 1024, "r": 2048, "g": 3072}
SSD_COLS = {"z": 0, "x": 2048, "B": 4096, "C": 4608, "dt": 5120}


def step_cols(s):
    return (0, C0) if s == 0 else (C0 + P * (s - 1), P)


def gla_levels(s):
    return ([8, 4, 2, 1], NS) if s == 0 else ([64, 32, 16, 8, 4, 2, 1], 0)


PARTS = 4


def interleave(tiles, convs, wo_tiles, lead, first, later, between, after_last, early):
    pieces, late = [], None
    for t in range(U * tiles):
        for c in range(3):
            pieces.append((t, c))
            if c == 0 and late is not None:
                pieces.append((late, 3))
                late = None
        if t % tiles in convs:
            late = t
    if late is not None:
        pieces.append((late, 3))
    last = [max(i for i, (t, _) in enumerate(pieces) if t // tiles == u) for u in range(U)]
    order, weights = [], []
    at = 0

    def weight(w):
        weights.append(w)
        order.append(("split", len(weights) - 1))

    def part():
        nonlocal at
        i, p = divmod(at, PARTS)
        t, c = pieces[i]
        at += 1
        if p == 0:
            order.extend(early.get(i, []))
        order.append(("piece", i, p))
        if i and p == (1 if c < 3 else 0):
            order.append(("drain", i - 1))
        if p:
            return
        if c == 0 and t + 1 < U * tiles:
            weight(("in", t + 1))
        for lag, name in enumerate(("evac", "finish", "store"), 1):
            if i >= lag:
                order.append((name, i - lag))
        if c == 3:
            at += PARTS - 1
        if i + 1 == len(pieces):
            for p in range(p + 1, PARTS if c < 3 else 1):
                order.append(("piece", i, p))
                if p == 1:
                    order.append(("drain", i - 1))
            at = PARTS * len(pieces)
            order.extend([("evac", i), ("drain", i), ("finish", i - 1), ("store", i - 2), ("finish", i),
                          ("store", i - 1), ("store", i)])

    def pieces_to(goal):
        while at < min(goal, PARTS * len(pieces)):
            part()

    weight(("in", 0))
    start = PARTS * min(last[0] + 1 + lead, len(pieces))
    pieces_to(start)
    shares = sum(n for name, n in first if name == "fill")
    shares += (STEPS - 1) * sum(n for name, n in later if name == "fill")
    per = PARTS * len(pieces) / U / shares
    filled = 0.0

    def stage(name, e):
        if 0 <= e < U * STEPS:
            u, s = divmod(e, STEPS)
            if name == "load" and s == 0:
                pieces_to(PARTS * (last[u] + 4))
            if u == U - 1 or not name.startswith("residual"):
                order.append((name, u, s))

    for name, shift in later:
        if name not in ("fill", "sample", "weights"):
            for e in range(shift):
                stage(name, e)
    for e in range(U * STEPS):
        u, s = divmod(e, STEPS)
        for name, n in (later if s else first):
            if name == "fill":
                filled += n
                pieces_to(start + filled * per)
            elif name == "sample":
                order.append(("sample", u, n))
            elif name == "weights":
                for k in range(wo_tiles):
                    weight(("out", u * wo_tiles + k))
            else:
                stage(name, e + n)
        if s == STEPS - 1:
            for name in between:
                order.append((name, u))
    for name, shift in after_last:
        stage(name, U * STEPS - 1 + shift)
    return order, pieces, weights, last


def hybrid_kernel(nc, x_prompt, x_sample, state_gla, state_ssm, state_conv, meta_tokens, pre_norm,
                  post_norm, gla_w_in, gla_w_gate_up, gla_b_gate, gla_w_norm, gla_w_out, ssd_w_in,
                  ssd_conv_w, ssd_conv_b, ssd_dt_bias, ssd_a_log, ssd_d_skip, ssd_w_norm, ssd_w_out,
                  y_prompt, y_sample, gla_prompt, ssm_prompt, conv_prompt, gla_sample, ssm_sample,
                  conv_sample):
    gq = nc.dram_tensor("gla_rows", [U, 7 * P, T], F32, kind="Internal").ap()
    sq = nc.dram_tensor("ssd_rows", [U, 10 * P, T], F32, kind="Internal").ap()
    acd = nc.dram_tensor("ssd_decay_rows", [SH, T], F32, kind="Internal").ap()
    x1d = nc.dram_tensor("x_after_gla", [T, D], F32, kind="Internal").ap()

    with ExitStack() as top:
        def sb(name, shape, dt=F32):
            return top.enter_context(nc.sbuf_tensor(name, shape, dt))

        def ps(name):
            return top.enter_context(nc.psum_tensor(name, [P, 512], F32))

        m = {}
        m["h"] = sb("h", [P, 2, KT, T], F32R)
        m["y"] = sb("y_acc", [P, STEPS, D])
        m["w"] = sb("w", [P, 2, 2, KT, P], F32R)
        m["raw"] = sb("w_raw", [P, 2, D])
        m["wo"] = sb("w_out", [P, 4, 2, D], F32R)
        m["ident"] = sb("ident", [P, P])
        m["tri"] = sb("tri", [P, P])
        m["tri0"] = sb("tri0", [C0, C0])
        m["wn"] = sb("wn", [P, 24])
        m["bg"] = sb("bg", [P, U])
        m["cw"] = sb("cw", [P, 5, 24])
        m["banks"] = [ps(f"bank{i}") for i in range(8)]
        io = dict(xp=x_prompt, xs=x_sample, meta=meta_tokens, x1=x1d, pre=pre_norm, post=post_norm,
                  yp=y_prompt, ys=y_sample)
        for name in ("rows_out0", "rows_out1", "gla_state_out", "gla_sample_out0",
                     "gla_sample_out1", "conv_old_out", "conv_out", "ssm_state_out", "ssm_sample_out0",
                     "ssm_sample_out1"):
            m[name] = nc.alloc_semaphore(name)
        with nc.cleanup_on_exit():
            constants(nc, m, gla_w_norm, ssd_w_norm, gla_b_gate, ssd_conv_w, ssd_conv_b)
        with nc.cleanup_on_exit():
            norm_phase(nc, m, io)
        with nc.cleanup_on_exit():
            gla_layer(nc, m, io, gq, gla_w_in, gla_w_gate_up, gla_w_out, state_gla, gla_prompt, gla_sample)
        with ExitStack() as ssd:
            t = {}
            for name, shape in (("dt", [P, STEPS, SH]), ("ac", [P, STEPS, SH]), ("ecol", [P, 16, NS]),
                                ("dskip", [P, SH]), ("sc", [P, 24, 3, NS])):
                t[name] = ssd.enter_context(nc.sbuf_tensor(name, shape, F32))
            with nc.cleanup_on_exit():
                ssd_layer(nc, m, io, t, sq, acd, ssd_w_in, ssd_dt_bias, ssd_a_log, ssd_d_skip, ssd_w_out,
                          state_ssm, state_conv, ssm_prompt, ssm_sample, conv_prompt, conv_sample)


def constants(nc, m, gla_w_norm, ssd_w_norm, gla_b_gate, conv_w, conv_b):
    ident, tri, tri0 = m["ident"], m["tri"], m["tri0"]
    bank = m["banks"][0]
    with ExitStack() as ctx:
        rows = ctx.enter_context(nc.sbuf_tensor("rows", [24, 8, P], F32))
        loaded = nc.alloc_semaphore("c_loaded")
        made = nc.alloc_semaphore("c_made")
        turned = nc.alloc_semaphore("c_turned")
        kept = nc.alloc_semaphore("c_kept")
        block = ctx.enter_context(nc.Block())
        parts = [(conv_w[0, i].rearrange("(a p) -> a p", p=P), 24) for i in range(4)]
        parts.append((conv_b[0].rearrange("(a p) -> a p", p=P), 24))
        parts.append((ssd_w_norm[0].rearrange("(a p) -> a p", p=P), 16))
        parts.append((gla_w_norm[0].rearrange("(a p) -> a p", p=P), 8))
        parts.append((gla_b_gate[0].rearrange("(a p) -> a p", p=P), 4))

        @block.sync
        def _(sp):
            for i, (src, n) in enumerate(parts):
                sp.dma_start(rows[0:n, i, :], src).then_inc(loaded, 16)

        @block.gpsimd
        def _(pool):
            pool.memset(ident[:, :], 0.0).then_inc(made, 1)
            pool.memset(tri[:, :], 1.0).then_inc(made, 1)
            pool.wait_ge(made, 2)
            pool.affine_select(out=ident[:, :], in_=ident[:, :], compare_op=ALU.not_equal, fill=1.0,
                               base=0, pattern=[[-1, P]], channel_multiplier=1).then_inc(made, 1)
            pool.affine_select(out=tri[:, :], in_=tri[:, :], compare_op=ALU.is_ge, fill=0.0,
                               base=0, pattern=[[1, P]], channel_multiplier=-1).then_inc(made, 1)
            pool.wait_ge(made, 4)
            pool.tensor_copy(tri0[:, :], tri[0:C0, 0:C0]).then_inc(made, 1)
            pool.wait_ge(made, 5)
            pool.tensor_copy(tri0[0:NS, :], ident[0:NS, 0:C0]).then_inc(made, 1)

        @block.tensor
        def _(pe):
            pe.wait_ge(made, 6)
            pe.wait_ge(loaded, 16 * len(parts))
            for i, (_, n) in enumerate(parts):
                last = pe.transpose(bank[:, 24 * i:24 * i + n], rows[0:n, i, :], ident[0:n, 0:n])
            last.then_inc(turned, 1)

        @block.scalar
        def _(act):
            act.wait_ge(turned, 1)
            act.activation(m["cw"][:, :, :], bank[:, 0:120].rearrange("p (i a) -> p i a", i=5),
                           ACT.Copy, scale=0.5).then_inc(kept, 1)
            act.activation(m["wn"][:, 0:16], bank[:, 120:136], ACT.Copy).then_inc(kept, 1)
            act.activation(m["wn"][:, 16:24], bank[:, 144:152], ACT.Copy, scale=0.5).then_inc(kept, 1)
            act.activation(m["bg"][:, :], bank[:, 168:172], ACT.Copy).then_inc(kept, 1)
            act.wait_ge(kept, 4)


class Residual:

    def __init__(self, m, io, k, sem, order, tiles, stats, power, added_to, event):
        self.m, self.io, self.k, self.power, self.added_to, self.event = m, io, k, power, added_to, event
        self.post, self.pre, self.junk, self.xt = tiles[0], tiles[1], tiles[2], tiles[3:]
        self.ssum, self.mean, self.rstd = (stats[:, i * 2 * STEPS:(i + 1) * 2 * STEPS] for i in range(3))
        self.w_in, self.x_in = sem("rw_in"), [sem(f"x_in{i}") for i in range(2)]
        self.stored = [m[f"rows_out{i}"] if k == 2 else sem(f"x_stored{i}") for i in range(2)]
        (self.squared, self.meant, self.rooted, self.scaled, self.added, self.normed, self.turned, self.high,
         self.low) = (sem("r_" + x) for x in ("squared", "meant", "rooted", "scaled", "added", "normed",
                                              "turned", "high", "low"))
        squares = []
        for task in order:
            if task[0] == "residual_square":
                squares.append((0, task[2]))
            elif task[0] == "residual_add" and k == 1:
                squares.append((1, task[2]))
        self.squares = {q: i for i, q in enumerate(squares)}

    def arrived(self, s):
        return 16 * (s // 2 + 1 + (1 if self.k == 1 and s % 2 == 0 else 0))

    def load_weights(self, sp):
        k = self.k
        sp.dma_start(self.post, self.io["post"][k - 1:k, :].to_broadcast([P, D])).then_inc(self.w_in, 16)
        if k == 1:
            sp.dma_start(self.pre, self.io["pre"][1:2, :].to_broadcast([P, D])).then_inc(self.w_in, 16)

    def load(self, sp, s):
        io, (c, n) = self.io, step_cols(s)
        if s == 0:
            self.load_weights(sp)
        if s >= 2:
            sp.wait_ge(self.stored[s % 2], 16 * (s // 2))
            if self.k == 1:
                sp.wait_ge(self.normed, s - 1)
        if self.k == 2:
            copies = [(0, io["x1"][c:c + n, :])]
        elif s == 0:
            copies = [(0, io["xs"][:, 0, :]), (NS, io["meta"])]
        else:
            copies = [(0, io["xp"][0, P * (s - 1):P * s, :])]
        for p0, src in copies:
            sp.dma_start(self.xt[s % 2][p0:p0 + src.shape[0], :], src).then_inc(self.x_in[s % 2], 16)

    def store(self, sp, s):
        io, (c, n) = self.io, step_cols(s)
        sp.wait_ge(self.added, s + 1)
        if self.k == 1:
            n, dst = n, io["x1"][c:c + n, :]
        elif s == 0:
            n, dst = NS, io["ys"][:, 0, :]
        else:
            dst = io["yp"][0, P * (s - 1):P * s, :]
        sp.dma_start(dst, self.xt[s % 2][0:n, :]).then_inc(self.stored[s % 2], 16)

    def all_stored(self, sp):
        for i in range(2):
            sp.wait_ge(self.stored[i], 16 * ((STEPS + 1 - i) // 2))

    def column(self, t, which, s, n):
        return t[0:n, which * STEPS + s:which * STEPS + s + 1]

    def root(self, pool, which, s):
        n, i = step_cols(s)[1], self.squares[(which, s)]
        mean, rstd = self.column(self.mean, which, s, n), self.column(self.rstd, which, s, n)
        pool.wait_ge(self.squared, i + 1)
        pool.tensor_scalar(mean, self.column(self.ssum, which, s, n), 1.0 / D, EPS, ALU.mult,
                           ALU.add).then_inc(self.meant, 1)
        pool.wait_ge(self.meant, i + 1)
        pool.tensor_tensor(rstd, mean, self.power[0:n, :], ALU.pow).then_inc(self.rooted, 1)

    def square(self, act, which, s):
        n, i = step_cols(s)[1], self.squares[(which, s)]
        if i:
            act.wait_ge(self.squared, i)
        if which == 0:
            act.wait_ge(self.added_to, 2 * (self.event(U - 1, s) + 1))
        else:
            act.wait_ge(self.added, s + 1)
        src = self.m["y"][0:n, s, :] if which == 0 else self.xt[s % 2][0:n, :]
        act.activation(self.junk[0:n, :], src, ACT.Square,
                       accum_out=self.column(self.ssum, which, s, n)).then_inc(self.squared, 1)

    def add(self, dve, s):
        n, y, xt = step_cols(s)[1], self.m["y"], self.xt[s % 2]
        if s == 0:
            dve.wait_ge(self.w_in, 32 if self.k == 1 else 16)
        dve.wait_ge(self.rooted, self.squares[(0, s)] + 1)
        dve.scalar_tensor_tensor(out=y[0:n, s, :], in0=y[0:n, s, :], scalar=self.column(self.rstd, 0, s, n),
                                 in1=self.post[0:n, :], op0=ALU.mult, op1=ALU.mult).then_inc(self.scaled, 1)
        dve.wait_ge(self.scaled, s + 1)
        dve.wait_ge(self.x_in[s % 2], self.arrived(s))
        dve.tensor_tensor(xt[0:n, :], xt[0:n, :], y[0:n, s, :], ALU.add).then_inc(self.added, 1)

    def norm(self, dve, s):
        n = step_cols(s)[1]
        dve.wait_ge(self.rooted, self.squares[(1, s)] + 1)
        dve.wait_ge(self.added, s + 1)
        dve.scalar_tensor_tensor(out=self.m["y"][0:n, s, :], in0=self.xt[s % 2][0:n, :],
                                 scalar=self.column(self.rstd, 1, s, n), in1=self.pre[0:n, :],
                                 op0=ALU.mult, op1=ALU.mult).then_inc(self.normed, 1)

    def turn(self, pe, s, banks):
        n = step_cols(s)[1]
        pe.wait_ge(self.normed, s + 1)
        if s:
            pe.wait_ge(self.low, 2 * s)
        for j in range(2):
            for a in range(4):
                f = (4 * j + a) * P
                last = pe.transpose(banks[j][:, a * n:a * n + n], self.m["y"][0:n, s, f:f + P],
                                    self.m["ident"][0:n, 0:n])
            last.then_inc(self.turned, 1)

    def split(self, engine, s, banks, low):
        c, n = step_cols(s)
        h = self.m["h"]
        for j in range(2):
            src = banks[j][:, 0:4 * n].rearrange("p (a c) -> p a c", a=4)
            a = slice(4 * j, 4 * j + 4)
            if low:
                engine.wait_ge(self.high, 2 * s + j + 1)
                engine.tensor_tensor(h[:, 1, a, c:c + n], src, h[:, 0, a, c:c + n].bitcast(F32),
                                     ALU.subtract).then_inc(self.low, 1)
            else:
                engine.wait_ge(self.turned, 2 * s + j + 1)
                engine.activation(h[:, 0, a, c:c + n], src, ACT.Copy).then_inc(self.high, 1)


def norm_phase(nc, m, io):
    y, h, ident = m["y"], m["h"], m["ident"]
    banks = m["banks"]
    with ExitStack() as ctx:
        def sb(name, shape):
            return ctx.enter_context(nc.sbuf_tensor("n_" + name, shape, F32))

        def sem(name):
            return nc.alloc_semaphore("n_" + name)

        pre, xt, junk = sb("pre", [P, D]), sb("xt", [P, STEPS // 2 + 1, D]), sb("junk", [P, D])
        SLOTS = STEPS // 2 + 1
        ssum, mean, rstd = sb("ssum", [P, STEPS]), sb("mean", [P, STEPS]), sb("rstd", [P, STEPS])
        power = sb("power", [P, 1])
        w_in, x_in = sem("w_in"), [sem(f"x_in{i}") for i in range(SLOTS)]
        (ready, squared, meant, rooted, normed, turned, high, low) = (
            sem(x) for x in ("ready", "squared", "meant", "rooted", "normed", "turned", "high", "low"))
        block = ctx.enter_context(nc.Block())

        def pair(s):
            return banks[2 * (s % 4):2 * (s % 4) + 2]

        @block.sync
        def _(sp):
            for s in range(STEPS):
                if s >= SLOTS:
                    sp.wait_ge(normed, s - SLOTS + 1)
                copies = [(0, io["xs"][:, 0, :]), (NS, io["meta"])] if s == 0 else \
                         [(0, io["xp"][0, P * (s - 1):P * s, :])]
                for p0, src in copies:
                    sp.dma_start(xt[p0:p0 + src.shape[0], s % SLOTS, :], src).then_inc(x_in[s % SLOTS], 16)
                if s == 0:
                    sp.dma_start(pre[:, :], io["pre"][0:1, :].to_broadcast([P, D])).then_inc(w_in, 16)

        @block.gpsimd
        def _(pool):
            pool.memset(power[:, :], -0.5).then_inc(ready, 1)
            pool.wait_ge(ready, 1)
            for s in range(STEPS):
                n = step_cols(s)[1]
                pool.wait_ge(squared, s + 1)
                pool.tensor_scalar(mean[0:n, s:s + 1], ssum[0:n, s:s + 1], 1.0 / D, EPS,
                                   ALU.mult, ALU.add).then_inc(meant, 1)
                pool.wait_ge(meant, s + 1)
                pool.tensor_tensor(rstd[0:n, s:s + 1], mean[0:n, s:s + 1], power[0:n, :],
                                   ALU.pow).then_inc(rooted, 1)

        @block.scalar
        def _(act):
            for s in range(STEPS + 2):
                if s < STEPS:
                    n = step_cols(s)[1]
                    act.wait_ge(x_in[s % SLOTS], 16 * (s // SLOTS + 1 + (1 if s % SLOTS == 0 else 0)))
                    if s:
                        act.wait_ge(squared, s)
                    act.activation(junk[0:n, :], xt[0:n, s % SLOTS, :], ACT.Square,
                                   accum_out=ssum[0:n, s:s + 1]).then_inc(squared, 1)
                q = s - 2
                if q < 0:
                    continue
                c, n = step_cols(q)
                for j in range(2):
                    act.wait_ge(turned, 2 * q + j + 1)
                    act.activation(h[:, 0, 4 * j:4 * j + 4, c:c + n],
                                   pair(q)[j][:, 0:4 * n].rearrange("p (a c) -> p a c", a=4),
                                   ACT.Copy).then_inc(high, 1)

        @block.vector
        def _(dve):
            dve.wait_ge(w_in, 16)
            for s in range(STEPS + 2):
                if s < STEPS:
                    n = step_cols(s)[1]
                    dve.wait_ge(rooted, s + 1)
                    dve.scalar_tensor_tensor(out=y[0:n, s, :], in0=xt[0:n, s % SLOTS, :],
                                             scalar=rstd[0:n, s:s + 1], in1=pre[0:n, :],
                                             op0=ALU.mult, op1=ALU.mult).then_inc(normed, 1)
                q = s - 2
                if q < 0:
                    continue
                c, n = step_cols(q)
                for j in range(2):
                    dve.wait_ge(high, 2 * q + j + 1)
                    dve.tensor_tensor(h[:, 1, 4 * j:4 * j + 4, c:c + n],
                                      pair(q)[j][:, 0:4 * n].rearrange("p (a c) -> p a c", a=4),
                                      h[:, 0, 4 * j:4 * j + 4, c:c + n].bitcast(F32),
                                      ALU.subtract).then_inc(low, 1)

        @block.tensor
        def _(pe):
            for s in range(STEPS):
                n = step_cols(s)[1]
                pe.wait_ge(normed, s + 1)
                if s >= 4:
                    pe.wait_ge(low, 2 * (s - 3))
                for j in range(2):
                    for a in range(4):
                        f = (4 * j + a) * P
                        last = pe.transpose(pair(s)[j][:, a * n:a * n + n], y[0:n, s, f:f + P],
                                            ident[0:n, 0:n])
                    last.then_inc(turned, 1)


def reset_mask(pool, mask, made, at):
    pool.memset(mask, 1.0).then_inc(made, 1)
    pool.wait_ge(made, at + 1)
    n = mask.shape[0]
    pool.memset(mask[:, 0:NS + 1], 0.0).then_inc(made, 1)
    for s in range(1, STEPS):
        c = step_cols(s)[0]
        pool.memset(mask[:, c:c + 1], 0.0).then_inc(made, 1)
    return at + 1 + STEPS


class Narrow:

    def __init__(self, m, sem, source, width, raw, banks):
        self.m, self.source, self.width, self.banks = m, source, width, banks
        self.raw = raw.rearrange("p (k f) -> p k f", k=KT)
        self.parts = [m["wo"][:, 0, i, :].rearrange("p (k f) -> p k f", k=KT) for i in range(2)]
        self.raw_in, self.zeroed, self.w_hi, self.w_lo, self.projected = (
            sem("n_" + x) for x in ("raw_in", "zeroed", "w_hi", "w_lo", "projected"))

    def load(self, sp):
        sp.dma_start(self.raw, self.source.rearrange("(k p) f -> p k f", p=P)).then_inc(self.raw_in, 16)

    def clear(self, pool):
        for part in self.parts:
            pool.memset(part.bitcast(F32), 0.0).then_inc(self.zeroed, 1)

    def high(self, act):
        act.wait_ge(self.zeroed, 2)
        act.wait_ge(self.raw_in, 16)
        act.activation(self.parts[0][:, :, 0:self.width], self.raw, ACT.Copy).then_inc(self.w_hi, 1)

    def low(self, dve):
        dve.wait_ge(self.w_hi, 1)
        dve.tensor_tensor(self.parts[1][:, :, 0:self.width], self.raw,
                          self.parts[0][:, :, 0:self.width].bitcast(F32), ALU.subtract).then_inc(self.w_lo, 1)

    def project(self, pe):
        h = self.m["h"]
        pe.wait_ge(self.w_lo, 1)
        for g, (c, n) in enumerate(CGS):
            i = 0
            for k in range(KT):
                for a, b in ((0, 0), (0, 1), (1, 0)):
                    last = pe.matmul(self.banks[g][:, 0:n], self.parts[a][:, k, :], h[:, b, k, c:c + n],
                                     start=(i == 0), stop=(i == 3 * KT - 1))
                    i += 1
            last.then_inc(self.projected, 1)


class Gates:

    def __init__(self, m, sem, w_in, w_up, gq):
        c0 = GLA_COLS["g"]
        self.bg, self.gq, self.w_up = m["bg"], gq, w_up
        room = m["y"][:, :, :].rearrange("p s d -> p (s d)")
        self.mask = room[:, 0:T]
        self.t1 = room[:, T:3 * T].rearrange("p (b t) -> p b t", b=2)
        self.t2 = room[:, 3 * T:5 * T].rearrange("p (b t) -> p b t", b=2)
        self.low = room[0:GR, 5 * T:6 * T]
        self.up = room[0:GR, 6 * T:6 * T + U * HK]
        self.banks = m["banks"][2:8]
        self.narrow = Narrow(m, sem, w_in[:, c0:c0 + GR], GR,
                             room[:, 6 * T + U * HK:6 * T + U * HK + KT * GR], self.banks)
        (self.up_in, self.made, self.lows, self.gated, self.absd, self.capped, self.exped, self.logged,
         self.summed, self.scanned) = (sem("n_" + x) for x in (
             "up_in", "made", "lows", "gated", "absd", "capped", "exped", "logged", "summed", "scanned"))
        self.stored = [sem(f"n_stored{i}") for i in range(2)]

    def load(self, sp):
        self.narrow.load(sp)
        sp.dma_start(self.up, self.w_up).then_inc(self.up_in, 16)

    def store(self, sp, u):
        sp.wait_ge(self.scanned, u + 1)
        sp.dma_start(self.gq[u, 2 * P:3 * P, :], self.t2[:, u % 2, :]).then_inc(self.stored[u % 2], 16)

    def prepare(self, pool):
        self.narrow.clear(pool)
        reset_mask(pool, self.mask, self.made, 0)

    def act_low(self, act):
        for g, (c, n) in enumerate(CGS):
            act.wait_ge(self.narrow.projected, g + 1)
            act.activation(self.low[:, c:c + n], self.banks[g][0:GR, 0:n], ACT.Copy).then_inc(self.lows, 1)

    def act_head(self, act, u):
        if u >= 2:
            act.wait_ge(self.scanned, u - 1)
        t1 = self.t1[:, u % 2, :]
        for g, (c, n) in enumerate(CGS):
            i = 3 * u + g
            act.wait_ge(self.gated, i + 1)
            act.activation(t1[:, c:c + n], self.banks[i % 6][:, 0:n], ACT.Abs,
                           bias=self.bg[:, u:u + 1]).then_inc(self.absd, 1)
        act.wait_ge(self.absd, 3 * u + 3)
        act.activation(t1, t1, ACT.Exp, scale=-1.0).then_inc(self.exped, 1)
        act.wait_ge(self.exped, u + 1)
        act.activation(t1, t1, ACT.Ln, bias=1.0).then_inc(self.logged, 1)

    def dve_head(self, dve, u):
        t1, t2 = self.t1[:, u % 2, :], self.t2[:, u % 2, :]
        if u == 0:
            dve.wait_ge(self.made, 1 + STEPS)
        if u >= 2:
            dve.wait_ge(self.stored[u % 2], 16 * (u // 2))
        for g, (c, n) in enumerate(CGS):
            i = 3 * u + g
            dve.wait_ge(self.absd, i + 1)
            dve.tensor_scalar(t2[:, c:c + n], self.banks[i % 6][:, 0:n], self.bg[:, u:u + 1], 0.0,
                              ALU.add, ALU.min).then_inc(self.capped, 1)

    def dve_sum(self, dve, u):
        t1, t2 = self.t1[:, u % 2, :], self.t2[:, u % 2, :]
        dve.wait_ge(self.logged, u + 1)
        dve.wait_ge(self.capped, 3 * u + 3)
        dve.tensor_tensor(t1, t2, t1, ALU.subtract).then_inc(self.summed, 1)
        dve.wait_ge(self.summed, u + 1)
        dve.tensor_tensor_scan(t2, self.mask, t1, 0.0, ALU.mult, ALU.add).then_inc(self.scanned, 1)

    def pe_head(self, pe, u):
        if u == 0:
            pe.wait_ge(self.up_in, 16)
            pe.wait_ge(self.lows, 3)
        for g, (c, n) in enumerate(CGS):
            i = 3 * u + g
            if i >= 6:
                pe.wait_ge(self.capped, i - 5)
            pe.matmul(self.banks[i % 6][:, 0:n], self.up[:, u * HK:(u + 1) * HK], self.low[:, c:c + n],
                      start=True, stop=True).then_inc(self.gated, 1)


class Weights:

    def __init__(self, weights, pieces, w_in, w_out, columns, tiles, wo_tiles, wn0):
        self.ends = {t: i + 1 for i, (t, g) in enumerate(pieces) if g == 2}
        self.weights, self.w_in, self.w_out, self.columns = weights, w_in, w_out, columns
        self.tiles, self.wo_tiles, self.wn0 = tiles, wo_tiles, wn0
        self.index = {w: i for i, w in enumerate(weights)}

    def source(self, i):
        kind, t = self.weights[i]
        if kind == "in":
            c = self.columns(t)
            return self.w_in[:, c:c + P].rearrange("(k p) f -> p k f", p=P)
        return self.w_out[t * P:(t + 1) * P, :]

    def raw(self, m, i):
        r = m["raw"][:, i % 2, :]
        return r.rearrange("p (k f) -> p k f", k=KT) if self.weights[i][0] == "in" else r

    def part(self, m, i, part):
        kind, t = self.weights[i]
        return m["w"][:, t % 2, part, :, :] if kind == "in" else m["wo"][:, t % self.wo_tiles, part, :]

    def load(self, sp, m, i, raw_in, w_lo):
        if i >= 2:
            sp.wait_ge(w_lo, i - 1)
        sp.dma_start(self.raw(m, i), self.source(i)).then_inc(raw_in[i % 2], 16)

    def high(self, act, m, i, raw_in, w_hi, piece_done, out_used):
        kind, t = self.weights[i]
        act.wait_ge(raw_in[i % 2], 16 * (i // 2 + 1))
        if kind == "in":
            if t >= 2:
                act.wait_ge(piece_done, self.ends[t - 2])
            act.activation(self.part(m, i, 0), self.raw(m, i), ACT.Copy).then_inc(w_hi, 1)
        else:
            u = t // self.wo_tiles
            if u:
                act.wait_ge(out_used, 2 * STEPS * u)
            act.activation(self.part(m, i, 0), self.raw(m, i), ACT.Copy,
                           scale=m["wn"][:, self.wn0 + t:self.wn0 + t + 1]).then_inc(w_hi, 1)

    def low(self, dve, m, i, w_hi, w_lo):
        kind, t = self.weights[i]
        dve.wait_ge(w_hi, i + 1)
        hi = self.part(m, i, 0).bitcast(F32)
        if kind == "in":
            dve.tensor_tensor(self.part(m, i, 1), self.raw(m, i), hi, ALU.subtract).then_inc(w_lo, 1)
        else:
            dve.scalar_tensor_tensor(out=self.part(m, i, 1), in0=self.raw(m, i),
                                     scalar=m["wn"][:, self.wn0 + t:self.wn0 + t + 1], in1=hi,
                                     op0=ALU.mult, op1=ALU.subtract).then_inc(w_lo, 1)


def project_part(pe, m, t, g, p, bank):
    c, n = CGS[g]
    for k in range(p * KT // PARTS, (p + 1) * KT // PARTS):
        for i, (a, b) in enumerate(((0, 0), (0, 1), (1, 0))):
            last = pe.matmul(bank[:, 0:n], m["w"][:, t % 2, a, k, :], m["h"][:, b, k, c:c + n],
                             start=(k == 0 and i == 0), stop=(k == KT - 1 and i == 2))
    return last


def out_products(pe, m, yt, wo_tiles, half, bank):
    i = 0
    for k in range(wo_tiles):
        for a, b in ((0, 0), (0, 1), (1, 0)):
            last = pe.matmul(bank[:, :], yt[a][:, k, :], m["wo"][:, k, b, 512 * half:512 * half + 512],
                             start=(i == 0), stop=(i == 3 * wo_tiles - 1))
            i += 1
    return last


def gla_layer(nc, m, io, gq, w_in, w_up, w_out, state, state_prompt, state_sample):
    NT, WT = 6, 2
    step = [("load", 1), ("keys", 0), ("levels", 0), ("turn", -1), ("residual_turn", -4), ("fill", 1), ("state", 0),
            ("distance", 1), ("fill", 0.2), ("attend", 0), ("norm", 0), ("decay", 1), ("products", -1),
            ("gate", 0), ("fill", 1), ("residual_square", -1), ("scale", 1),
            ("residual_low", -4), ("residual_norm", -3), ("residual_add", -2), ("residual_in", -1),
            ("values", 1), ("fill", 0.75)]
    first = step[:6]
    for i in range(4):
        first += [("sample", i), ("fill", 0.5)]
    first += step[6:13] + [("weights", 0)] + step[13:]
    early = {1: [("gate_low",)]}
    for u in range(U):
        early[3 + 4 * u] = [("gate_head", u)]
        early[4 + 4 * u] = [("gate_sum", u)]
        early[6 + 4 * u] = [("gate_store", u)]
    rest = [("turn", 0), ("residual_turn", -3), ("products", 0), ("residual_square", 0), ("residual_low", -3),
            ("residual_add", -1), ("residual_norm", -2), ("residual_in", 0), ("residual_turn", -2),
            ("residual_add", 0), ("residual_norm", -1), ("residual_low", -2), ("residual_turn", -1),
            ("residual_norm", 0), ("residual_low", -1), ("residual_turn", 0), ("residual_low", 0)]
    order, pieces, weights, last_piece = interleave(NT, set(), WT, 3, first, step, [], rest, early)
    kinds = ["q", "k", "v", "v", "r", "r"]
    rows = [0, 1, 3, 4, 5, 6]

    def column(t):
        u, j = divmod(t, NT)
        kind = kinds[j]
        width = HK if kind in "qk" else HV
        return GLA_COLS[kind] + u * width + (P if j in (3, 5) else 0)

    W = Weights(weights, pieces, w_in[0], w_out[0], column, NT, WT, 16)
    PA, PB, TA, TB, L0, L1, O, X = m["banks"]
    PR, L, ident, y = (PA, PB), (L0, L1), m["ident"], m["y"]
    with ExitStack() as ctx:
        def sb(name, shape, dt=F32):
            return ctx.enter_context(nc.sbuf_tensor("g_" + name, shape, dt))

        def sem(name):
            return nc.alloc_semaphore("g_" + name)

        mask = sb("lmask", [P, 7, P])
        mask0 = sb("lmask0", [C0, 4, C0])
        rowsel = sb("rowsel", [C0, NS + 1])
        st = sb("stage", [P, 2, 350])
        th = sb("th", [P, 350])
        ck = sb("chunk", [P, 2, 7, P])
        E = sb("decays", [P, 8, P])
        Eq = sb("q_decayed", [P, 7, P])
        eb = sb("ebcum", [P, P])
        qe = sb("q_inter", [P, P])
        kd0 = sb("k_first", [P, C0])
        kt = sb("k_turned", [P, P])
        km = sb("k_masked", [C0, NS + 1, P])
        vt = sb("v_turned", [P, HV])
        G, G0 = sb("attn", [P, P]), sb("attn0", [C0, C0])
        on, og = sb("o_normed", [P, HV]), sb("o_gated", [P, HV])
        othi, otlo = sb("ot_hi", [P, 2, P], F32R), sb("ot_lo", [P, 2, P], F32R)
        S = sb("state", [P, HV])
        qm = sb("q_masked", [P, NS * C0])
        ss = sb("sample_state", [P, 2, 2, HV])
        osum, omean, orstd, power = (sb(x, [P, 1]) for x in ("osum", "omean", "orstd", "power"))

        raw_in = [sem(f"raw_in{i}") for i in range(2)]
        w_hi, w_lo = sem("w_hi"), sem("w_lo")
        piece_done = sem("piece_done")
        tanhed = sem("tanhed")
        staged = [sem(f"staged{i}") for i in range(2)]
        stored = [sem(f"stored{i}") for i in range(2)]
        ck_in = [sem(f"ck_in{i}") for i in range(2)]
        consts, zeros, dsub, dabs, decays, eb_done = (sem(x) for x in
                                                      ("consts", "zeros", "dsub", "dabs", "decays", "eb_done"))
        k_ready, q_ready, qi_ready, ta_done, tb_done = (sem(x) for x in
                                                        ("k_ready", "q_ready", "qi_ready", "ta_done", "tb_done"))
        v_turned, k_turned, levels, attn_part, attn = (sem(x) for x in
                                                       ("v_turned", "k_turned", "levels", "attn_part", "attn"))
        s_prod, s_new, o_done, squared = (sem(x) for x in ("s_prod", "s_new", "o_done", "squared"))
        meant, rooted, o_scaled, o_gated, o_turned = (sem(x) for x in
                                                      ("meant", "rooted", "o_scaled", "o_gated", "o_turned"))
        ot_hi, ot_lo, out_done, added = (sem(x) for x in ("ot_hi", "ot_lo", "out_done", "added"))
        s_saved = m["gla_state_out"]
        ss_in = [sem(f"ss_in{i}") for i in range(2)]
        ss_out = [m[f"gla_sample_out{i}"] for i in range(2)]
        qm_ready, km_ready, ss_prod, ss_new = (sem(x) for x in ("qm_ready", "km_ready", "ss_prod", "ss_new"))
        k_ready0 = sem("k_ready0")
        gates = Gates(m, sem, w_in[0], w_up[0], gq)
        CONSTS = 10 + 3 * 11 + 2
        more = sb("more", [P, 2, D])
        junk = m["w"][:, 0, 0].rearrange("p k f -> p (k f)")
        res = Residual(m, io, 1, sem, order, [m["raw"][:, 0, :], m["raw"][:, 1, :], junk, more[:, 0, :],
                                              more[:, 1, :]],
                       sb("stats", [P, 6 * STEPS]), power, added, lambda u, s: u * STEPS + s)
        block = ctx.enter_context(nc.Block())

        def ev(u, s):
            return u * STEPS + s

        def tokens(u, s):
            return ck[:, ev(u, s) % 2, :, 0:step_cols(s)[1]]

        @block.sync
        def _(sp):
            def store(i):
                t, g = pieces[i]
                u, j = divmod(t, NT)
                c, n = CGS[g]
                sp.wait_ge(staged[i % 2], i // 2 + 1)
                sp.dma_start(gq[u, rows[j] * P:(rows[j] + 1) * P, c:c + n],
                             st[:, i % 2, 0:n]).then_inc(stored[i % 2], 16)

            def load(u, s):
                e = ev(u, s)
                c, n = step_cols(s)
                if s == 0:
                    for i in range(2):
                        sp.wait_ge(stored[i], 16 * ((last_piece[u] - i) // 2 + 1))
                    sp.wait_ge(gates.stored[u % 2], 16 * (u // 2 + 1))
                if e >= 2:
                    sp.wait_ge(ta_done, e - 1)
                    sp.wait_ge(levels, 2 * (e - 1))
                    sp.wait_ge(qi_ready, e - 1)
                    sp.wait_ge(eb_done, e - 1)
                sp.dma_start(tokens(u, s), gq[u, :, c:c + n].rearrange("(t p) c -> p t c", p=P)).then_inc(
                    ck_in[e % 2], 16)

            gates.load(sp)
            W.load(sp, m, 0, raw_in, w_lo)
            W.load(sp, m, 1, raw_in, w_lo)
            for task in order:
                if task[0] == "split" and task[1] + 2 < len(weights):
                    W.load(sp, m, task[1] + 2, raw_in, w_lo)
                elif task[0] == "store":
                    store(task[1])
                elif task[0] == "gate_store":
                    gates.store(sp, task[1])
                elif task[0] == "load":
                    load(*task[1:])
                elif task[0] == "residual_in":
                    if task[2] == 0:
                        sp.wait_ge(w_lo, len(weights))
                    res.load(sp, task[2])
                elif task[0] == "residual_add":
                    res.store(sp, task[2])
                elif task[0] == "norm" and task[2] == STEPS - 1:
                    u = task[1]
                    sp.wait_ge(s_new, STEPS * (u + 1))
                    sp.dma_start(state_prompt[0, 0, u], S[:, :]).then_inc(s_saved, 16)
            sp.wait_ge(s_saved, 16 * U)
            for i in range(2):
                sp.wait_ge(stored[i], 16 * ((len(pieces) - 1 - i) // 2 + 1))
            res.all_stored(sp)

        @block.gpsimd
        def _(pool):
            gates.prepare(pool)
            for li, h in enumerate(gla_levels(1)[0]):
                pool.memset(mask[:, li, :], 0.0).then_inc(consts, 1)
            pool.memset(mask0[:, :, :], 0.0).then_inc(consts, 1)
            pool.memset(rowsel[:, :], 1.0).then_inc(consts, 1)
            pool.memset(power[:, :], -0.5).then_inc(consts, 1)
            n = 10
            pool.wait_ge(consts, n)
            sets = [(mask[:, li, :], h, 0) for li, h in enumerate(gla_levels(1)[0])]
            sets += [(mask0[:, li, NS:C0], h, NS) for li, h in enumerate(gla_levels(0)[0])]
            views = [(v.rearrange("p (b w) -> p b w", w=2 * h)[:, :, h:2 * h], h, off) for v, h, off in sets]
            for v, h, off in views:
                pool.memset(v, 1.0).then_inc(consts, 1)
            n += len(views)
            pool.wait_ge(consts, n)
            for v, h, off in views:
                pool.affine_select(out=v, in_=v, compare_op=ALU.is_ge, fill=0.0, base=-off,
                                   pattern=[[-2 * h, v.shape[1]], [0, h]],
                                   channel_multiplier=1).then_inc(consts, 1)
            n += len(views)
            pool.wait_ge(consts, n)
            for v, h, off in views:
                pool.affine_select(out=v, in_=v, compare_op=ALU.is_ge, fill=0.0, base=off + h - 1,
                                   pattern=[[2 * h, v.shape[1]], [0, h]],
                                   channel_multiplier=-1).then_inc(consts, 1)
            n += len(views)
            pool.affine_select(out=rowsel[:, NS:NS + 1], in_=rowsel[:, NS:NS + 1], compare_op=ALU.is_ge,
                               fill=0.0, base=-NS, pattern=[[0, 1]], channel_multiplier=1).then_inc(consts, 1)
            pool.tensor_copy(rowsel[:, 0:NS], ident[0:C0, 0:NS]).then_inc(consts, 1)
            assert n + 2 == CONSTS
            def sample_state(i, out):
                u, b = divmod(i, 4)
                if out:
                    pool.wait_ge(ss_new, 2 * (i + 1))
                    pool.dma_start(state_sample[0, 2 * b:2 * b + 2, u].rearrange("b k v -> k b v"),
                                 ss[:, i % 2, :, :]).then_inc(ss_out[i % 2], 16)
                else:
                    if i >= 2:
                        pool.wait_ge(ss_out[i % 2], 16 * (i // 2))
                    pool.dma_start(ss[:, i % 2, :, :],
                                 state[0, 2 * b:2 * b + 2, u].rearrange("b k v -> k b v")).then_inc(
                                     ss_in[i % 2], 16)

            sample_state(0, False)
            sample_state(1, False)
            for task in order:
                if task[0] == "sample":
                    i = 4 * task[1] + task[2]
                    sample_state(i, True)
                    if i + 2 < 4 * U:
                        sample_state(i + 2, False)
                elif task[0] == "residual_square":
                    res.root(pool, 0, task[2])
                elif task[0] == "residual_add":
                    res.root(pool, 1, task[2])
                elif task[0] == "norm":
                    e, n = ev(*task[1:]), step_cols(task[2])[1]
                    pool.wait_ge(squared, e + 1)
                    pool.tensor_scalar(omean[0:n, :], osum[0:n, :], 1.0 / HV, EPS, ALU.mult,
                                       ALU.add).then_inc(meant, 1)
                    pool.wait_ge(meant, e + 1)
                    if e:
                        pool.wait_ge(o_scaled, e)
                    pool.tensor_tensor(orstd[0:n, :], omean[0:n, :], power[0:n, :],
                                       ALU.pow).then_inc(rooted, 1)
            for i in range(2):
                pool.wait_ge(ss_out[i], 16 * 2 * U)

        @block.scalar
        def _(act):
            def evac(i):
                t, g = pieces[i]
                j, n = t % NT, CGS[g][1]
                act.wait_ge(piece_done, i + 1)
                if j >= 4:
                    q = (t // NT) * 6 + (j - 4) * 3 + g
                    if q:
                        act.wait_ge(staged[(prev_gate[i]) % 2], prev_gate[i] // 2 + 1)
                    act.activation(th[:, 0:n], PR[i % 2][:, 0:n], ACT.Tanh, scale=0.5).then_inc(tanhed, 1)
                    return
                if i >= 2:
                    act.wait_ge(stored[i % 2], 16 * (i // 2))
                act.activation(st[:, i % 2, 0:n], PR[i % 2][:, 0:n], ACT.Copy,
                               scale=HK ** -0.5 if j == 0 else 1.0).then_inc(staged[i % 2], 1)

            def decay(u, s):
                e, n = ev(u, s), step_cols(s)[1]
                x = tokens(u, s)
                act.wait_ge(ck_in[e % 2], 16 * (e // 2 + 1))
                if e:
                    act.wait_ge(qi_ready, e)
                    act.wait_ge(s_new, e)
                    if s == 1:
                        act.wait_ge(ss_new, 2 * 4 * (u + 1))
                act.activation(eb[:, 0:n], x[:, 2, :], ACT.Exp, scale=1.0 / TAU).then_inc(eb_done, 1)
                act.wait_ge(dsub, e + 1)
                act.activation(E[:, :, 0:n], E[:, :, 0:n], ACT.Abs).then_inc(dabs, 1)
                act.wait_ge(dabs, e + 1)
                act.activation(E[:, :, 0:n], E[:, :, 0:n], ACT.Exp, scale=-1.0 / TAU).then_inc(decays, 1)

            def values(u, s):
                e, n = ev(u, s), step_cols(s)[1]
                act.wait_ge(ta_done, e + 1)
                if e:
                    act.wait_ge(o_done, e)
                    act.wait_ge(s_prod, e)
                    if s == 1:
                        act.wait_ge(ss_prod, 4 * (u + 1))
                act.activation(vt[0:n, :], TA[0:n, 0:HV], ACT.Copy).then_inc(v_turned, 1)

            def keys(u, s):
                e = ev(u, s)
                if s:
                    act.wait_ge(tb_done, e + 1)
                    act.activation(kt[:, :], TB[:, 0:P], ACT.Copy).then_inc(k_turned, 1)

            def norm(u, s):
                e, n = ev(u, s), step_cols(s)[1]
                act.wait_ge(o_done, e + 1)
                if e:
                    act.wait_ge(rooted, e)
                    act.wait_ge(o_gated, e)
                act.activation(on[0:n, :], O[0:n, 0:HV], ACT.Square, accum_out=osum[0:n, :]).then_inc(squared, 1)
                act.wait_ge(rooted, e + 1)
                act.activation(on[0:n, :], O[0:n, 0:HV], ACT.Copy, scale=orstd[0:n, :]).then_inc(o_scaled, 1)

            def turn(u, s):
                e, n = ev(u, s), step_cols(s)[1]
                act.wait_ge(o_turned, e + 1)
                if e:
                    act.wait_ge(out_done, 2 * e)
                act.activation(othi[:, :, 0:n], X[:, 0:2 * n].rearrange("p (a c) -> p a c", a=2),
                               ACT.Copy).then_inc(ot_hi, 1)

            prev_gate, seen = {}, None
            for i, (t, g) in enumerate(pieces):
                if t % NT >= 4:
                    prev_gate[i] = seen
                    seen = i
            gates.narrow.high(act)
            for task in order:
                if task[0] == "gate_low":
                    gates.act_low(act)
                elif task[0] == "gate_head":
                    gates.act_head(act, task[1])
                elif task[0] == "split":
                    W.high(act, m, task[1], raw_in, w_hi, piece_done, out_done)
                elif task[0] == "evac":
                    evac(task[1])
                elif task[0] in ("decay", "values", "keys", "norm", "turn"):
                    {"decay": decay, "values": values, "keys": keys, "norm": norm,
                     "turn": turn}[task[0]](*task[1:])
                elif task[0] == "residual_square":
                    if task[2] == 0:
                        act.wait_ge(piece_done, len(pieces))
                    res.square(act, 0, task[2])
                elif task[0] == "residual_add":
                    res.square(act, 1, task[2])
                elif task[0] == "residual_turn":
                    res.split(act, task[2], PR, False)

        @block.vector
        def _(dve):
            gates.narrow.low(dve)
            dve.memset(E[:, :, :], 0.0).then_inc(zeros, 1)
            dve.memset(G[:, :], 0.0).then_inc(zeros, 1)
            dve.memset(G0[:, :], 0.0).then_inc(zeros, 1)
            dve.memset(othi[:, :, :].bitcast(F32), 0.0).then_inc(zeros, 1)
            dve.memset(otlo[:, :, :].bitcast(F32), 0.0).then_inc(zeros, 1)
            dve.memset(qm[:, :], 0.0).then_inc(zeros, 1)

            def evac(i):
                t, g = pieces[i]
                n = CGS[g][1]
                if t % NT < 4:
                    return
                q = (t // NT) * 6 + (t % NT - 4) * 3 + g
                dve.wait_ge(tanhed, q + 1)
                if i >= 2:
                    dve.wait_ge(stored[i % 2], 16 * (i // 2))
                dve.scalar_tensor_tensor(out=st[:, i % 2, 0:n], in0=th[:, 0:n], scalar=1.0,
                                         in1=PR[i % 2][:, 0:n], op0=ALU.add,
                                         op1=ALU.mult).then_inc(staged[i % 2], 1)

            def decay(u, s):
                e, n = ev(u, s), step_cols(s)[1]
                if e == 0:
                    dve.wait_ge(zeros, 6)
                    dve.wait_ge(consts, CONSTS)
                x = tokens(u, s)
                sizes, off = gla_levels(s)
                dve.wait_ge(ck_in[e % 2], 16 * (e // 2 + 1))
                if e:
                    dve.wait_ge(levels, 2 * e)
                    dve.wait_ge(tb_done, e)
                b = x[:, 2, off:n]
                if s == 0:
                    dve.memset(E[:, :, 0:NS], 0.0).then_inc(zeros, 1)
                for li, h in enumerate(sizes):
                    v = b.rearrange("p (b w) -> p b w", w=2 * h)
                    nb = v.shape[1]
                    dve.tensor_tensor(E[:, li, off:n].rearrange("p (b w) -> p b w", w=2 * h), v,
                                      v[:, :, h - 1:h].to_broadcast([P, nb, 2 * h]), ALU.subtract)
                dve.tensor_tensor(E[:, 7, off:n], b, x[:, 2, n - 1:n].to_broadcast([P, n - off]),
                                  ALU.subtract).then_inc(dsub, 1)

            def scale(u, s):
                e, n = ev(u, s), step_cols(s)[1]
                x = tokens(u, s)
                sizes = gla_levels(s)[0]
                dve.wait_ge(decays, e + 1)
                nl = len(sizes)
                dve.tensor_tensor(Eq[:, 0:nl, 0:n], E[:, 0:nl, 0:n],
                                  x[:, 0:1, :].to_broadcast([P, nl, n]), ALU.mult).then_inc(q_ready, 1)
                dve.wait_ge(q_ready, e + 1)
                dve.tensor_tensor(E[:, :, 0:n], E[:, :, 0:n],
                                  x[:, 1:2, :].to_broadcast([P, 8, n]), ALU.mult).then_inc(k_ready, 1)
                dve.wait_ge(eb_done, e + 1)
                if e:
                    dve.wait_ge(o_done, e)
                dve.tensor_tensor(qe[:, 0:n], x[:, 0, :], eb[:, 0:n], ALU.mult).then_inc(qi_ready, 1)
                if s == 0:
                    dve.wait_ge(k_ready, e + 1)
                    dve.tensor_copy(kd0[:, 0:NS], x[:, 1, 0:NS]).then_inc(k_ready0, 1)
                    dve.tensor_copy(kd0[:, NS:C0], E[:, 7, NS:C0]).then_inc(k_ready0, 1)
                    dve.wait_ge(qi_ready, e + 1)
                    dve.tensor_copy(qm[:, 0:(NS - 1) * (C0 + 1) + 1:C0 + 1], qe[:, 0:NS]).then_inc(qm_ready, 1)

            def keys(u, s):
                e = ev(u, s)
                if s == 0:
                    dve.wait_ge(tb_done, e + 1)
                    dve.tensor_tensor(km[:, :, :], TB[0:C0, 0:P].unsqueeze(1).to_broadcast([C0, NS + 1, P]),
                                      rowsel[:, :].unsqueeze(2).to_broadcast([C0, NS + 1, P]),
                                      ALU.mult).then_inc(km_ready, 1)

            def levels_of(u, s):
                e, n = ev(u, s), step_cols(s)[1]
                sizes, off = gla_levels(s)
                nl = len(sizes)
                g, mk = (G0, mask0) if s == 0 else (G, mask)
                if e:
                    dve.wait_ge(o_done, e)
                part = 60 * u + (7 * s - 3 if s else 0)
                for li in range(nl):
                    if li % 4 == 0:
                        dve.wait_ge(levels, 2 * e + li // 4 + 1)
                    if li:
                        dve.wait_ge(attn_part, part + li)
                    dve.copy_predicated(g[:, :], mk[:, li, :].bitcast(I32),
                                        L[li // 4][0:n, (li % 4) * P:(li % 4) * P + n]).then_inc(attn_part, 1)
                dve.wait_ge(attn_part, part + nl)
                dve.wait_ge(levels, 2 * e + 2)
                dve.copy_predicated(g[:, :], ident[0:n, 0:n].bitcast(I32),
                                    L1[0:n, 3 * P:3 * P + n]).then_inc(attn, 1)

            def sample(u, i):
                i += 4 * u
                dve.wait_ge(ss_prod, i + 1)
                for b in range(2):
                    c = 2 * (i % 4) + b
                    dve.scalar_tensor_tensor(out=ss[:, i % 2, b, :], in0=ss[:, i % 2, b, :],
                                             scalar=eb[:, c:c + 1], in1=X[:, b * HV:(b + 1) * HV],
                                             op0=ALU.mult, op1=ALU.add).then_inc(ss_new, 1)

            def state_of(u, s):
                e, n = ev(u, s), step_cols(s)[1]
                if s == 0:
                    if e:
                        dve.wait_ge(s_saved, 16 * u)
                    dve.wait_ge(s_prod, e + 1)
                    dve.tensor_copy(S[:, :], TB[:, P:P + HV]).then_inc(s_new, 1)
                else:
                    dve.wait_ge(s_prod, e + 1)
                    dve.scalar_tensor_tensor(out=S[:, :], in0=S[:, :], scalar=eb[:, n - 1:n],
                                             in1=TB[:, P:P + HV], op0=ALU.mult, op1=ALU.add).then_inc(s_new, 1)

            def gate(u, s):
                e, n = ev(u, s), step_cols(s)[1]
                dve.wait_ge(o_scaled, e + 1)
                if e:
                    dve.wait_ge(o_turned, e)
                dve.tensor_tensor(og[0:n, :], on[0:n, :], TA[0:n, HV:2 * HV], ALU.mult).then_inc(o_gated, 1)

            def turn(u, s):
                e, n = ev(u, s), step_cols(s)[1]
                dve.wait_ge(ot_hi, e + 1)
                if e:
                    dve.wait_ge(out_done, 2 * e)
                dve.tensor_tensor(otlo[:, :, 0:n], X[:, 0:2 * n].rearrange("p (a c) -> p a c", a=2),
                                  othi[:, :, 0:n].bitcast(F32), ALU.subtract).then_inc(ot_lo, 1)

            def products(u, s):
                e, n = ev(u, s), step_cols(s)[1]
                if e == 0:
                    for i in range(2):
                        dve.wait_ge(gates.stored[i], 16 * (U // 2))
                for half in range(2):
                    dve.wait_ge(out_done, 2 * e + half + 1)
                    dst = y[0:n, s, 512 * half:512 * half + 512]
                    if u == 0:
                        dve.tensor_copy(dst, L[half][0:n, :]).then_inc(added, 1)
                    else:
                        dve.tensor_tensor(dst, dst, L[half][0:n, :], ALU.add).then_inc(added, 1)

            stages = {"distance": decay, "scale": scale, "keys": keys, "levels": levels_of, "sample": sample,
                      "state": state_of, "gate": gate, "turn": turn, "products": products}
            for task in order:
                if task[0] == "gate_head":
                    gates.dve_head(dve, task[1])
                elif task[0] == "gate_sum":
                    gates.dve_sum(dve, task[1])
                elif task[0] == "split":
                    W.low(dve, m, task[1], w_hi, w_lo)
                elif task[0] == "drain":
                    evac(task[1])
                elif task[0] in stages:
                    stages[task[0]](*task[1:])
                elif task[0] == "residual_add":
                    res.add(dve, task[2])
                elif task[0] == "residual_norm":
                    res.norm(dve, task[2])
                elif task[0] == "residual_low":
                    res.split(dve, task[2], PR, True)

        @block.tensor
        def _(pe):
            def piece(i, p):
                t, g = pieces[i]
                if g == 0 and p == 0:
                    pe.wait_ge(w_lo, W.index[("in", t)] + 1)
                if i >= 2 and p == 0:
                    pe.wait_ge(staged[i % 2], i // 2)
                last = project_part(pe, m, t, g, p, PR[i % 2])
                if p == PARTS - 1:
                    last.then_inc(piece_done, 1)

            def values(u, s):
                e, n = ev(u, s), step_cols(s)[1]
                x = tokens(u, s)
                pe.wait_ge(ck_in[e % 2], 16 * (e // 2 + 1))
                if e:
                    pe.wait_ge(o_gated, e)
                for j in range(4):
                    last = pe.transpose(TA[0:n, j * P:(j + 1) * P], x[:, 3 + j, :], ident[:, :])
                last.then_inc(ta_done, 1)

            def keys(u, s):
                e, n = ev(u, s), step_cols(s)[1]
                if e:
                    pe.wait_ge(s_new, e)
                if s == 0:
                    pe.wait_ge(k_ready0, 2 * (u + 1))
                    pe.transpose(TB[0:n, 0:P], kd0[:, :], ident[:, :]).then_inc(tb_done, 1)
                else:
                    pe.wait_ge(k_ready, e + 1)
                    pe.transpose(TB[0:n, 0:P], E[:, 7, :], ident[:, :]).then_inc(tb_done, 1)

            def levels_of(u, s):
                e, n = ev(u, s), step_cols(s)[1]
                x = tokens(u, s)
                nl = len(gla_levels(s)[0])
                pe.wait_ge(q_ready, e + 1)
                pe.wait_ge(k_ready, e + 1)
                if e >= 2:
                    pe.wait_ge(added, 2 * (e - 1))
                for half in range(2):
                    for li in range(4 * half, min(4 * half + 4, nl)):
                        last = pe.matmul(L[half][0:n, (li % 4) * P:(li % 4) * P + n], E[:, li, 0:n],
                                         Eq[:, li, 0:n], start=True, stop=True)
                    if half:
                        last = pe.matmul(L1[0:n, 3 * P:3 * P + n], x[:, 1, :], x[:, 0, :],
                                         start=True, stop=True)
                    last.then_inc(levels, 1)

            def output_free(e):
                pe.wait_ge(qi_ready, e + 1)
                pe.wait_ge(v_turned, e + 1)

            def sample(u, i):
                n = C0
                if i == 0:
                    output_free(ev(u, 0))
                    pe.wait_ge(qm_ready, u + 1)
                    pe.wait_ge(km_ready, u + 1)
                i += 4 * u
                pe.wait_ge(ss_in[i % 2], 16 * (i // 2 + 1))
                for b in range(2):
                    c = 2 * (i % 4) + b
                    pe.matmul(O[0:n, 0:HV], qm[:, c * C0:(c + 1) * C0], ss[:, i % 2, b, :],
                              start=(c == 0), stop=False)
                if i:
                    pe.wait_ge(ss_new, 2 * i)
                    if i % 4 == 0:
                        pe.wait_ge(ot_lo, ev(u, 0))
                for b in range(2):
                    c = 2 * (i % 4) + b
                    last = pe.matmul(X[:, b * HV:(b + 1) * HV], km[:, c, :], vt[0:n, :],
                                     start=True, stop=True)
                last.then_inc(ss_prod, 1)

            def state_of(u, s):
                e, n = ev(u, s), step_cols(s)[1]
                if s == 0:
                    pe.matmul(TB[:, P:P + HV], km[:, NS, :], vt[0:n, :], start=True, stop=True).then_inc(s_prod, 1)
                else:
                    output_free(e)
                    pe.wait_ge(k_turned, e - u)
                    pe.wait_ge(s_new, e)
                    pe.matmul(O[0:n, 0:HV], qe[:, :], S[:, :], start=True, stop=False)
                    pe.matmul(TB[:, P:P + HV], kt[:, :], vt[:, :], start=True, stop=True).then_inc(s_prod, 1)

            def attend(u, s):
                e, n = ev(u, s), step_cols(s)[1]
                pe.wait_ge(attn, e + 1)
                g = G0 if s == 0 else G
                pe.matmul(O[0:n, 0:HV], g[:, :], vt[0:n, :], start=False, stop=True).then_inc(o_done, 1)

            def turn(u, s):
                e, n = ev(u, s), step_cols(s)[1]
                pe.wait_ge(o_gated, e + 1)
                if e:
                    pe.wait_ge(ot_lo, e)
                for j in range(2):
                    last = pe.transpose(X[:, j * n:(j + 1) * n], og[0:n, j * P:(j + 1) * P], ident[0:n, 0:n])
                last.then_inc(o_turned, 1)

            def products(u, s):
                e = ev(u, s)
                pe.wait_ge(ot_lo, e + 1)
                pe.wait_ge(w_lo, W.index[("out", u * WT + WT - 1)] + 1)
                for half in range(2):
                    out_products(pe, m, (othi, otlo), WT, half, L[half]).then_inc(out_done, 1)

            stages = {"piece": piece, "gate_head": lambda u: gates.pe_head(pe, u), "values": values, "keys": keys, "levels": levels_of, "sample": sample,
                      "state": state_of, "attend": attend, "turn": turn, "products": products}
            gates.narrow.project(pe)
            for task in order:
                if task[0] in stages:
                    stages[task[0]](*task[1:])
                elif task[0] == "residual_turn":
                    if task[2] == 0:
                        for i in range(2):
                            pe.wait_ge(staged[i], (len(pieces) + 1 - i) // 2)
                    res.turn(pe, task[2], PR)


class StepSizes:

    def __init__(self, m, t, sem, w_in, dt_bias, a_log, d_skip, state_conv, acd, conv_sample, sel):
        c0 = SSD_COLS["dt"]
        self.m, self.t, self.ident, self.sel = m, t, m["ident"], sel
        self.dt_bias, self.a_log, self.d_skip, self.acd = dt_bias, a_log, d_skip, acd
        self.state_conv, self.conv_sample, self.moved = state_conv, conv_sample, m["conv_old_out"]
        room = m["y"][:, :, :].rearrange("p s d -> p (s d)")
        self.mask, self.t1, self.t2, self.ac = (room[0:SH, i * T:(i + 1) * T] for i in range(4))
        at = 4 * T
        self.cs = room[0:3 * NS, at:at + CONV]
        at += CONV
        raw, at = room[:, at:at + KT * SH], at + KT * SH
        self.bias, self.alog, self.aexp = (room[0:SH, at + i:at + i + 1] for i in range(3))
        self.ea = room[0:SH, at + 8:at + 8 + NS]
        (self.DTB, self.ACB, _), self.C, self.EB = m["banks"][2:5], m["banks"][5:7], m["banks"][7]
        self.narrow = Narrow(m, sem, w_in[:, c0:c0 + SH], SH, raw, m["banks"][2:5])
        (self.small_in, self.made, self.aexped, self.absd, self.capped, self.exped, self.logged, self.dt_done,
         self.a_done, self.scanned, self.ea_done, self.turned, self.kept, self.conv_in, self.d_in,
         self.stored) = (sem("n_" + x) for x in (
             "small_in", "made", "aexped", "absd", "capped", "exped", "logged", "dt_done", "a_done",
             "scanned", "ea_done", "turned", "kept", "conv_in", "d_in", "stored"))

    def load(self, sp):
        self.narrow.load(sp)
        for i in range(3):
            sp.dma_start(self.cs[NS * i:NS * i + NS, :], self.state_conv[0, :, i, :]).then_inc(self.conv_in, 16)
        sp.dma_start(self.bias, self.dt_bias.rearrange("a h -> h a")).then_inc(self.small_in, 16)
        sp.dma_start(self.alog, self.a_log.rearrange("a h -> h a")).then_inc(self.small_in, 16)

    def load_rest(self, sp):
        sp.dma_start(self.t["dskip"][:, :], self.d_skip.to_broadcast([P, SH])).then_inc(self.d_in, 16)
        sp.dma_start(self.conv_sample[0, :, 0:2, :], self.state_conv[0, :, 1:3, :]).then_inc(self.moved, 16)

    def store(self, sp):
        sp.wait_ge(self.scanned, 1)
        sp.dma_start(self.acd, self.ac).then_inc(self.stored, 16)

    def prepare(self, pool):
        self.narrow.clear(pool)
        made, sel = self.made, self.sel
        n = reset_mask(pool, self.mask, made, 0)
        pool.memset(sel, 1.0).then_inc(made, 1)
        pool.wait_ge(made, n + 1)
        pool.affine_select(out=sel, in_=sel, compare_op=ALU.is_ge, fill=0.0, base=0,
                           pattern=[[1, DI]], channel_multiplier=-HD).then_inc(made, 1)
        pool.wait_ge(made, n + 2)
        pool.affine_select(out=sel, in_=sel, compare_op=ALU.is_ge, fill=0.0, base=HD - 1,
                           pattern=[[-1, DI]], channel_multiplier=HD).then_inc(made, 1)

    def turn_conv(self, pe):
        pe.wait_ge(self.conv_in, 48)
        for a in range(24):
            last = pe.transpose(self.C[a // 12][:, (a % 12) * 24:(a % 12) * 24 + 24],
                                self.cs[:, a * P:(a + 1) * P], self.ident[0:24, 0:24])
        last.then_inc(self.turned, 1)

    def keep_conv(self, act):
        act.wait_ge(self.turned, 1)
        for c, bank in enumerate(self.C):
            act.activation(self.t["sc"][:, 12 * c:12 * c + 12, :, :],
                           bank[:, 0:12 * 24].rearrange("p (a i b) -> p a i b", a=12, i=3),
                           ACT.Copy).then_inc(self.kept, 1)

    def act_sizes(self, act):
        act.wait_ge(self.small_in, 32)
        act.activation(self.aexp, self.alog, ACT.Exp).then_inc(self.aexped, 1)
        for g, (c, n) in enumerate(CGS):
            act.wait_ge(self.narrow.projected, g + 1)
            act.activation(self.t1[:, c:c + n], self.narrow.banks[g][0:SH, 0:n], ACT.Abs,
                           bias=self.bias).then_inc(self.absd, 1)
        act.wait_ge(self.absd, 3)
        act.activation(self.t1, self.t1, ACT.Exp, scale=-1.0).then_inc(self.exped, 1)
        act.wait_ge(self.exped, 1)
        act.activation(self.t1, self.t1, ACT.Ln, bias=1.0).then_inc(self.logged, 1)

    def dve_sizes(self, dve):
        dve.wait_ge(self.small_in, 32)
        for g, (c, n) in enumerate(CGS):
            dve.wait_ge(self.absd, g + 1)
            dve.tensor_scalar(self.t2[:, c:c + n], self.narrow.banks[g][0:SH, 0:n], self.bias, 0.0, ALU.add,
                              ALU.max).then_inc(self.capped, 1)
        dve.wait_ge(self.capped, 3)
        dve.wait_ge(self.logged, 1)
        dve.tensor_tensor(self.t2, self.t2, self.t1, ALU.add).then_inc(self.dt_done, 1)
        dve.wait_ge(self.dt_done, 1)
        dve.wait_ge(self.aexped, 1)
        dve.tensor_scalar(self.t1, self.t2, self.aexp, -1.0, ALU.mult, ALU.mult).then_inc(self.a_done, 1)
        dve.wait_ge(self.a_done, 1)
        dve.wait_ge(self.made, 1 + STEPS)
        dve.tensor_tensor_scan(self.ac, self.mask, self.t1, 0.0, ALU.mult, ALU.add).then_inc(self.scanned, 1)

    def act_samples(self, act):
        act.wait_ge(self.scanned, 1)
        act.activation(self.ea, self.ac[:, 0:NS], ACT.Exp).then_inc(self.ea_done, 1)

    def turn_sizes(self, pe):
        pe.wait_ge(self.dt_done, 1)
        pe.wait_ge(self.scanned, 1)
        pe.wait_ge(self.ea_done, 1)
        pe.wait_ge(self.made, 1 + STEPS + 3)
        for s in range(STEPS):
            c, n = step_cols(s)
            pe.transpose(self.DTB[0:n, s * SH:(s + 1) * SH], self.t2[:, c:c + n], self.ident[0:SH, 0:SH])
            pe.transpose(self.ACB[0:n, s * SH:(s + 1) * SH], self.ac[:, c:c + n], self.ident[0:SH, 0:SH])
        for a in range(16):
            last = pe.matmul(self.EB[:, a * NS:(a + 1) * NS], self.sel[:, a * P:(a + 1) * P], self.ea,
                             start=True, stop=True)
        last.then_inc(self.turned, 1)

    def keep_sizes(self, act):
        act.wait_ge(self.turned, 2)
        for q, n in ((slice(0, 1), C0), (slice(1, STEPS), P)):
            for name, bank in (("dt", self.DTB), ("ac", self.ACB)):
                view = bank[0:n, 0:STEPS * SH].rearrange("p (s h) -> p s h", h=SH)[:, q, :]
                act.activation(self.t[name][0:n, q, :], view, ACT.Copy).then_inc(self.kept, 1)
        act.activation(self.t["ecol"][:, :, :], self.EB[:, 0:P].rearrange("p (a b) -> p a b", a=16),
                       ACT.Copy).then_inc(self.kept, 1)


def ssd_layer(nc, m, io, tab, sq, acd, w_in, dt_bias, a_log, d_skip, w_out, state, state_conv,
              state_prompt, state_sample, conv_prompt, conv_sample):
    NT, WT = 10, 4
    convs = set(range(6))
    step = [("load", 1), ("turn", -1), ("inputs", 0), ("fill", 1.4), ("scan", 0), ("gates", 0), ("fill", 1),
            ("norm", 0), ("products", -1), ("fill", 0.5), ("decay", 1), ("fill", 0.5), ("decay_exp", 1),
            ("residual_square", -1), ("residual_add", -2), ("residual_in", -1), ("fill", 0.7)]
    first = step[:4]
    for i in range(NS):
        first += [("sample", i), ("fill", 0.45)]
    first += step[4:10] + [("weights", 0)] + step[10:]
    early = {3: [("sizes",)], 6: [("size_samples",)], 8: [("size_turn",)]}
    rest = [("turn", 0), ("products", 0), ("residual_square", 0), ("residual_add", -1), ("residual_in", 0),
            ("residual_add", 0)]
    order, pieces, weights, last_piece = interleave(NT, convs, WT, 7, first, step, ["keep"], rest, early)

    def column(t):
        g, j = divmod(t, NT)
        if j < 4:
            return SSD_COLS["x"] + g * 512 + j * P
        if j < 6:
            return SSD_COLS["B" if j == 4 else "C"] + g * P
        return SSD_COLS["z"] + g * 512 + (j - 6) * P

    def channel(t):
        g, j = divmod(t, NT)
        return 4 * g + j if j < 4 else 16 + 4 * (j - 4) + g

    W = Weights(weights, pieces, w_in[0], w_out[0], column, NT, WT, 0)
    PA, PB, X, Z, M, Y1, Y2, SU = m["banks"]
    PR, Y, ident, y_acc = (PA, PB), (Y1, Y2), m["ident"], m["y"]
    conv_index = {p: i for i, p in enumerate(p for p in pieces if p[0] % NT in convs and p[1] < 3)}
    where = {p: i for i, p in enumerate(pieces)}
    rows_before = [[], []]
    for i, (t, g) in enumerate(pieces):
        for par in range(2):
            rows_before[par].append((rows_before[par][-1] if i else 0) +
                                    (1 if i and (i - 1) % 2 == par and pieces[i - 1][1] < 3 else 0))

    def rows_to(i):
        return sum(1 for p in pieces[:i + 1] if p[1] < 3)

    def tile_index(t):
        return 6 * (t // NT) + t % NT

    with ExitStack() as ctx:
        def sb(name, shape, dt=F32):
            return ctx.enter_context(nc.sbuf_tensor("s_" + name, shape, dt))

        def sem(name):
            return nc.alloc_semaphore("s_" + name)

        room = sb("room", [P, 2 * (353 + 350 + 350)])
        pre, cu, th = (room[:, a:a + 2 * n].rearrange("p (b c) -> p b c", b=2)
                       for a, n in ((0, 353), (706, 350), (1406, 350)))
        cvp, cvo = sb("cv_cols", [P, 2, 11]), sb("cv_rows", [11, P])
        ck = sb("chunk", [P, 2, 6, P])
        zc = sb("z", [P, 4, P])
        acb = sb("decay", [P, 2, HPG, P])
        el, wl, ea = sb("e_last", [P, HPG]), sb("w_last", [P, HPG]), sb("e_sum", [P, HPG])
        bt, cbm = sb("b_turned", [P, P]), sb("cb", [P, P])
        xdt, xw, y = sb("xdt", [P, 512]), sb("xw", [P, 512]), sb("ys", [P, 512])
        ythi, ytlo = sb("yt_hi", [P, 4, P], F32R), sb("yt_lo", [P, 4, P], F32R)
        S = sb("state", [P, 512])
        cm = sb("c_masked", [P, NS * C0])
        bm = sb("b_masked", [C0, P])
        meta_row = sb("meta_row", [C0, 1])
        ss = sb("sample_state", [P, 2, 4, P])
        ysum, ymean, yrstd, power = (sb(x, [P, 1]) for x in ("ysum", "ymean", "yrstd", "power"))

        raw_in = [sem(f"raw_in{i}") for i in range(2)]
        bank_free = [sem(f"bank_free{i}") for i in range(2)]
        stored = [sem(f"stored{i}") for i in range(2)]
        cv_stored, s_saved = m["conv_out"], m["ssm_state_out"]
        ck_in = [sem(f"ck_in{i}") for i in range(2)]
        acb_in = [sem(f"acb_in{i}") for i in range(2)]
        ss_in = [sem(f"ss_in{i}") for i in range(2)]
        ss_out = [m[f"ssm_sample_out{i}"] for i in range(2)]
        (w_hi, w_lo, piece_done, z_in, convolved, tanhed, silued, cv_packed, consts, zeros, chain) = (
            sem(x) for x in ("w_hi", "w_lo", "piece_done", "z_in", "convolved", "tanhed", "silued",
                             "cv_packed", "consts", "zeros", "chain"))
        gaps = sem("gaps")
        (turned, b_turned, el_done, decays, cb_masked, xdt_ready, xw_ready, attn, intra, inter, s_prod,
         s_new, y_summed, z_turned, gated, squared, meant, rooted, y_normed, y_turned, yt_hi, yt_lo,
         out_done, added) = (sem(x) for x in (
             "turned", "b_turned", "el_done", "decays", "cb_masked", "xdt_ready", "xw_ready", "attn",
             "intra", "inter", "s_prod", "s_new", "y_summed", "z_turned", "gated", "squared", "meant",
             "rooted", "y_normed", "y_turned", "yt_hi", "yt_lo", "out_done", "added"))
        (cm_ready, bm_ready, ss_turned, ss_copied, ss_inter, ss_prod, ss_new, s_turned, s_kept) = (
            sem(x) for x in ("cm_ready", "bm_ready", "ss_turned", "ss_copied", "ss_inter", "ss_prod",
                             "ss_new", "s_turned", "s_kept"))
        junk = m["h"][:, :, :, :].rearrange("p a k t -> p (a k t)")[:, 0:D]
        res = Residual(m, io, 2, sem, order, [m["raw"][:, 0, :], None, junk, room[:, 0:D], room[:, D:2 * D]],
                       m["raw"][:, 1, 0:6 * STEPS], power, added,
                       lambda u, s: u * STEPS + s)
        sizes = StepSizes(m, tab, sem, w_in[0], dt_bias, a_log, d_skip, state_conv, acd, conv_sample,
                          acb[0:SH, :, :, :].rearrange("p a r c -> p (a r c)"))
        block = ctx.enter_context(nc.Block())

        def ev(u, s):
            return u * STEPS + s

        def tokens(u, s):
            return ck[:, ev(u, s) % 2, :, 0:step_cols(s)[1]]

        def decay(u, s):
            return acb[:, ev(u, s) % 2, :, 0:step_cols(s)[1]]

        def tanh_count(i):
            return tanh_order[i] + 1

        tanh_order = {}
        for task in order:
            if task[0] in ("evac", "finish"):
                j, g = pieces[task[1]][0] % NT, pieces[task[1]][1]
                if g < 3 and (j in convs) == (task[0] == "finish"):
                    tanh_order[task[1]] = len(tanh_order)

        @block.sync
        def _(sp):
            def store(i):
                t, g = pieces[i]
                u, j = divmod(t, NT)
                if g == 3:
                    q, a = tile_index(t), channel(t)
                    sp.wait_ge(bank_free[i % 2], i // 2 + 1)
                    sp.dma_start(conv_prompt[0, 0, :, a * P:(a + 1) * P],
                                 cvo[0:3, :]).then_inc(cv_stored, 16)
                    sp.dma_start(conv_sample[0, :, 2, a * P:(a + 1) * P],
                                 cvo[3:11, :]).then_inc(cv_stored, 16)
                    return
                c, n = CGS[g]
                sp.wait_ge(silued, rows_to(i))
                sp.dma_start(sq[u, j * P:(j + 1) * P, c:c + n], th[:, i % 2, 0:n]).then_inc(stored[i % 2], 16)

            def load(u, s):
                e = ev(u, s)
                c, n = step_cols(s)
                if s == 0:
                    for par in range(2):
                        n_rows = rows_before[par][last_piece[u]] + (1 if last_piece[u] % 2 == par and
                                                                    pieces[last_piece[u]][1] < 3 else 0)
                        sp.wait_ge(stored[par], 16 * n_rows)
                if e == 0:
                    sp.wait_ge(sizes.stored, 16)
                    sp.wait_ge(sizes.turned, 2)
                if e >= 2:
                    sp.wait_ge(intra, e - 1)
                    sp.wait_ge(s_prod, e - 1)
                    if s in (1, 2):
                        sp.wait_ge(cm_ready, u + 1 if s == 2 else max(u, 0))
                sp.dma_start(tokens(u, s), sq[u, 0:6 * P, c:c + n].rearrange("(t p) c -> p t c", p=P)).then_inc(
                    ck_in[e % 2], 16)
                sp.dma_start(decay(u, s), acd[HPG * u:HPG * u + HPG, c:c + n].unsqueeze(0).to_broadcast(
                    [P, HPG, n])).then_inc(acb_in[e % 2], 16)

            def load_z(u, s):
                e = ev(u, s)
                c, n = step_cols(s)
                if e:
                    sp.wait_ge(z_turned, e)
                sp.dma_start(zc[:, :, 0:n], sq[u, 6 * P:10 * P, c:c + n].rearrange("(t p) c -> p t c", p=P)).then_inc(
                    z_in, 16)

            sizes.load(sp)
            W.load(sp, m, 0, raw_in, w_lo)
            W.load(sp, m, 1, raw_in, w_lo)
            sizes.load_rest(sp)
            for task in order:
                if task[0] == "split" and task[1] + 2 < len(weights):
                    W.load(sp, m, task[1] + 2, raw_in, w_lo)
                elif task[0] == "store":
                    store(task[1])
                elif task[0] == "size_turn":
                    sizes.store(sp)
                elif task[0] == "load":
                    load(*task[1:])
                elif task[0] == "residual_in":
                    if task[2] == 0:
                        sp.wait_ge(w_lo, len(weights))
                        sp.wait_ge(silued, rows_to(len(pieces) - 1))
                        for i in range(2):
                            sp.wait_ge(stored[i], 16 * (rows_before[i][-1] + (
                                1 if (len(pieces) - 1) % 2 == i and pieces[-1][1] < 3 else 0)))
                    res.load(sp, task[2])
                elif task[0] == "residual_add":
                    res.store(sp, task[2])
                elif task[0] == "inputs":
                    load_z(*task[1:])
            sp.wait_ge(cv_stored, 32 * 6 * U)
            for i in range(2):
                sp.wait_ge(stored[i], 16 * (rows_before[i][-1] + (1 if (len(pieces) - 1) % 2 == i and
                                                                  pieces[-1][1] < 3 else 0)))
            res.all_stored(sp)
            sp.wait_ge(sizes.moved, 16)
            sp.wait_ge(sizes.d_in, 16)

        @block.gpsimd
        def _(pool):
            sizes.prepare(pool)
            pool.memset(meta_row[:, :], 1.0).then_inc(consts, 1)
            pool.memset(power[:, :], -0.5).then_inc(consts, 1)
            pool.wait_ge(consts, 2)
            pool.affine_select(out=meta_row[:, :], in_=meta_row[:, :], compare_op=ALU.is_ge,
                               fill=0.0, base=-NS, pattern=[[0, 1]], channel_multiplier=1).then_inc(consts, 1)
            def sample_state(i, out):
                u, b = divmod(i, NS)
                view = (state_sample if out else state)[0, b, HPG * u:HPG * u + HPG].rearrange(
                    "(t two) p n -> (two p) t n", two=2)
                if out:
                    pool.wait_ge(ss_new, i + 1)
                    pool.dma_start(view, ss[:, i % 2, :, :]).then_inc(ss_out[i % 2], 16)
                else:
                    if i >= 2:
                        pool.wait_ge(ss_out[i % 2], 16 * (i // 2))
                    if i and i % NS < 1:
                        pool.wait_ge(s_saved, 16 * u)
                    pool.dma_start(ss[:, i % 2, :, :], view).then_inc(ss_in[i % 2], 16)

            sample_state(0, False)
            sample_state(1, False)
            for task in order:
                if task[0] == "sample":
                    i = NS * task[1] + task[2]
                    sample_state(i, True)
                    if task[2] + 2 < NS:
                        sample_state(i + 2, False)
                elif task[0] == "residual_square":
                    res.root(pool, 0, task[2])
                elif task[0] == "norm":
                    e, n = ev(*task[1:]), step_cols(task[2])[1]
                    pool.wait_ge(squared, e + 1)
                    pool.tensor_scalar(ymean[0:n, :], ysum[0:n, :], 1.0 / 512, 4 * EPS, ALU.mult,
                                       ALU.add).then_inc(meant, 1)
                    pool.wait_ge(meant, e + 1)
                    if e:
                        pool.wait_ge(y_normed, e)
                    pool.tensor_tensor(yrstd[0:n, :], ymean[0:n, :], power[0:n, :],
                                       ALU.pow).then_inc(rooted, 1)
                elif task[0] == "keep":
                    u = task[1]
                    pool.wait_ge(s_kept, u + 1)
                    pool.dma_start(state_prompt[0, 0, HPG * u:HPG * u + HPG].rearrange(
                        "(t two) p n -> (two p) t n", two=2), ss[:, 0, :, :]).then_inc(s_saved, 16)
                    if u + 1 < U:
                        sample_state(NS * (u + 1) + 1, False)
                        sample_state(NS * (u + 1), False)
            pool.wait_ge(s_saved, 16 * U)
            for i in range(2):
                pool.wait_ge(ss_out[i], 16 * U * NS // 2)

        @block.scalar
        def _(act):
            def evac(i):
                t, g = pieces[i]
                j = t % NT
                act.wait_ge(piece_done, i + 1)
                bank = PR[i % 2]
                if g == 3:
                    q = tile_index(t)
                    if q:
                        act.wait_ge(cv_stored, 32 * q)
                    act.activation(cvo[:, :], bank[0:11, 0:P], ACT.Copy).then_inc(bank_free[i % 2], 1)
                elif j in convs:
                    c, n = CGS[g]
                    ci, q = conv_index[(t, g)], tile_index(t)
                    if ci >= 2:
                        act.wait_ge(convolved, ci - 1)
                    if ci >= 1 and g == 0:
                        act.wait_ge(cv_packed, q)
                    if g == 0:
                        if q >= 2:
                            act.wait_ge(piece_done, where[(prev_tile[prev_tile[t]], 3)] + 1)
                        act.activation(cvp[:, q % 2, 3:11], bank[:, 0:NS], ACT.Copy)
                        act.activation(pre[:, ci % 2, 3:3 + n - NS], bank[:, NS:n],
                                       ACT.Copy).then_inc(bank_free[i % 2], 1)
                    else:
                        if g == 2:
                            act.wait_ge(convolved, ci)
                        act.activation(pre[:, ci % 2, 3:3 + n], bank[:, 0:n],
                                       ACT.Copy).then_inc(bank_free[i % 2], 1)
                else:
                    n = CGS[g][1]
                    act.wait_ge(silued, rows_to(i - 2))
                    act.wait_ge(stored[i % 2], 16 * rows_before[i % 2][i])
                    act.activation(th[:, i % 2, 0:n], bank[:, 0:n], ACT.Tanh, scale=0.5).then_inc(tanhed, 1)
                    act.activation(cu[:, i % 2, 0:n], bank[:, 0:n], ACT.Copy).then_inc(bank_free[i % 2], 1)

            prev_tile, last = {}, None
            for t in range(U * NT):
                if t % NT in convs:
                    prev_tile[t] = last
                    last = t

            def finish(i):
                t, g = pieces[i]
                if t % NT not in convs or g == 3:
                    return
                n = CGS[g][1]
                act.wait_ge(convolved, conv_index[(t, g)] + 1)
                act.wait_ge(stored[i % 2], 16 * rows_before[i % 2][i])
                act.activation(th[:, i % 2, 0:n], cu[:, i % 2, 0:n], ACT.Tanh).then_inc(tanhed, 1)

            def decay_of(u, s):
                e, n = ev(u, s), step_cols(s)[1]
                L = decay(u, s)
                act.wait_ge(acb_in[e % 2], 16 * (e // 2 + 1))
                act.wait_ge(sizes.kept, 7)
                if e:
                    act.wait_ge(s_new, e)
                    act.wait_ge(y_summed, e)
                act.activation(ea[0:n, :], tab["ac"][0:n, s, HPG * u:HPG * u + HPG], ACT.Exp)
                act.activation(el[:, :].unsqueeze(2), L[:, :, n - 1:n], ACT.Exp).then_inc(el_done, 1)
                act.wait_ge(el_done, e + 1)
                for r in range(HPG):
                    h = HPG * u + r
                    last = act.activation(L[0:n, r, :], L[0:n, r, :], ACT.Relu, scale=-1.0,
                                          bias=tab["ac"][0:n, s, h:h + 1])
                last.then_inc(gaps, 1)

            def decay_exp(u, s):
                e, n = ev(u, s), step_cols(s)[1]
                L = decay(u, s)
                act.wait_ge(gaps, e + 1)
                act.activation(L[0:n], L[0:n], ACT.Exp, scale=-1.0).then_inc(decays, 1)

            def inputs(u, s):
                e, n = ev(u, s), step_cols(s)[1]
                act.wait_ge(turned, e + 1)
                if e:
                    act.wait_ge(s_prod, e)
                act.activation(bt[0:n, :], M[0:n, 0:P], ACT.Copy).then_inc(b_turned, 1)

            def sample(u, i):
                if i == 0 and u:
                    act.wait_ge(y_turned, ev(u, 0))
                act.wait_ge(ss_turned, NS * u + i + 1)
                if i:
                    act.wait_ge(ss_inter, NS * u + i - u)
                act.activation(y[:, :], SU[:, :], ACT.Copy).then_inc(ss_copied, 1)

            def norm(u, s):
                e, n = ev(u, s), step_cols(s)[1]
                act.wait_ge(gated, e + 1)
                if e:
                    act.wait_ge(rooted, e)
                act.wait_ge(intra, e + 1)
                act.activation(xdt[0:n, :], y[0:n, :], ACT.Square, accum_out=ysum[0:n, :]).then_inc(squared, 1)
                act.wait_ge(rooted, e + 1)
                act.activation(y[0:n, :], y[0:n, :], ACT.Copy, scale=yrstd[0:n, :]).then_inc(y_normed, 1)

            def turn(u, s):
                e, n = ev(u, s), step_cols(s)[1]
                act.wait_ge(y_turned, e + 1)
                if e:
                    act.wait_ge(out_done, 2 * e)
                act.activation(ythi[:, :, 0:n], SU[:, 0:4 * n].rearrange("p (a c) -> p a c", a=4),
                               ACT.Copy).then_inc(yt_hi, 1)

            def keep(u):
                act.wait_ge(s_turned, u + 1)
                act.wait_ge(ss_out[0], 16 * (u + 1) * NS // 2)
                act.activation(ss[:, 0, :, :], Z[:, :].rearrange("p (a n) -> p a n", a=4),
                               ACT.Copy).then_inc(s_kept, 1)

            sizes.narrow.high(act)
            sizes.keep_conv(act)
            stages = {"evac": evac, "finish": finish, "decay": decay_of, "decay_exp": decay_exp, "inputs": inputs, "sample": sample,
                      "norm": norm, "turn": turn, "keep": keep}
            for task in order:
                if task[0] == "sizes":
                    sizes.act_sizes(act)
                elif task[0] == "size_samples":
                    sizes.act_samples(act)
                elif task[0] == "size_turn":
                    sizes.keep_sizes(act)
                elif task[0] == "split":
                    W.high(act, m, task[1], raw_in, w_hi, piece_done, out_done)
                elif task[0] in stages:
                    stages[task[0]](*task[1:])
                elif task[0] == "residual_square":
                    if task[2] == 0:
                        act.wait_ge(piece_done, len(pieces))
                    res.square(act, 0, task[2])

        @block.vector
        def _(dve):
            links = [0]

            def mark(ins):
                links[0] += 1
                ins.then_inc(chain, 1)
                return links[0]

            def link(ins):
                dve.wait_ge(chain, mark(ins))

            sizes.narrow.low(dve)
            dve.memset(ythi[:, :, :].bitcast(F32), 0.0).then_inc(zeros, 1)
            dve.memset(ytlo[:, :, :].bitcast(F32), 0.0).then_inc(zeros, 1)
            dve.memset(cm[:, :], 0.0).then_inc(zeros, 1)
            dve.wait_ge(zeros, 3)
            dve.wait_ge(consts, 3)
            dve.wait_ge(sizes.kept, 2)
            cw = m["cw"]

            def evac(i):
                t, g = pieces[i]
                j, n = t % NT, CGS[min(g, 2)][1]
                if g == 3:
                    return
                if j not in convs:
                    return
                ci, q, a = conv_index[(t, g)], tile_index(t), channel(t)
                p, u = pre[:, ci % 2, :], cu[:, i % 2, :]
                dve.wait_ge(bank_free[i % 2], i // 2 + 1)
                if i >= 2:
                    dve.wait_ge(silued, rows_to(i - 2))
                off = NS if g == 0 else 0
                if g == 0:
                    link(dve.memset(p[:, 0:3], 0.0))
                else:
                    w = CGS[g - 1][1] - (NS if g == 1 else 0)
                    link(dve.tensor_copy(p[:, 0:3], pre[:, (ci + 1) % 2, w:w + 3]))
                if g == 2:
                    dve.tensor_copy(cvp[:, q % 2, 0:3], p[:, n:n + 3]).then_inc(cv_packed, 1)
                if g == 0:
                    old, new = tab["sc"][:, a, :, :], cvp[:, q % 2, 3:11]
                    taps = [old[:, 0, :], old[:, 1, :], old[:, 2, :], new]
                    link(dve.tensor_scalar(u[:, 0:NS], taps[0], cw[:, 0, a:a + 1], cw[:, 4, a:a + 1],
                                           ALU.mult, ALU.add))
                    for k in range(1, 4):
                        link(dve.scalar_tensor_tensor(out=u[:, 0:NS], in0=taps[k], scalar=cw[:, k, a:a + 1],
                                                      in1=u[:, 0:NS], op0=ALU.mult, op1=ALU.add))
                w = n - off
                link(dve.tensor_scalar(u[:, off:n], p[:, 0:w], cw[:, 0, a:a + 1], cw[:, 4, a:a + 1],
                                       ALU.mult, ALU.add))
                for k in range(1, 4):
                    ins = dve.scalar_tensor_tensor(out=u[:, off:n], in0=p[:, k:k + w],
                                                   scalar=cw[:, k, a:a + 1], in1=u[:, off:n],
                                                   op0=ALU.mult, op1=ALU.add)
                    if k < 3:
                        link(ins)
                    else:
                        ins.then_inc(convolved, 1)

            def finish(i):
                t, g = pieces[i]
                if g == 3:
                    return
                n = CGS[g][1]
                dve.wait_ge(tanhed, tanh_count(i))
                if t % NT not in convs:
                    dve.wait_ge(bank_free[i % 2], i // 2 + 1)
                dve.scalar_tensor_tensor(out=th[:, i % 2, 0:n], in0=th[:, i % 2, 0:n], scalar=1.0,
                                         in1=cu[:, i % 2, 0:n], op0=ALU.add, op1=ALU.mult).then_inc(silued, 1)

            def heads(x, n, w=HD):
                return x.unsqueeze(2).to_broadcast([n, HPG, w])

            def split_heads(x):
                return x.rearrange("p (r c) -> p r c", r=HPG)

            def inputs(u, s):
                e, n = ev(u, s), step_cols(s)[1]
                L, x = decay(u, s), tokens(u, s)
                hs = slice(HPG * u, HPG * u + HPG)
                dve.wait_ge(b_turned, e + 1)
                dve.wait_ge(sizes.kept, 7)
                dve.wait_ge(sizes.d_in, 16)
                tri = m["tri0"] if s == 0 else m["tri"]
                dve.tensor_tensor(cbm[0:n, 0:n], M[0:n, P:P + n], tri[:, :], ALU.mult).then_inc(cb_masked, 1)
                if e:
                    dve.wait_ge(intra, e)
                    dve.wait_ge(s_prod, e)
                    if s == 1:
                        dve.wait_ge(ss_prod, NS * (u + 1))
                    dve.wait_ge(squared, e)
                dve.tensor_tensor(split_heads(xdt[0:n, :]), split_heads(X[0:n, :]),
                                  heads(tab["dt"][0:n, s, hs], n), ALU.mult).then_inc(xdt_ready, 1)
                dve.wait_ge(decays, e + 1)
                dve.wait_ge(acb_in[e % 2], 16 * (e // 2 + 1))
                last = L[0:n, :, n - 1:n].rearrange("p r o -> p (r o)")
                if s:
                    link(dve.tensor_copy(wl[0:n, :], last))
                else:
                    link(dve.tensor_scalar(wl[0:n, :], last, meta_row[:, :], None, ALU.mult))
                dve.wait_ge(xdt_ready, e + 1)
                dve.tensor_tensor(split_heads(xw[0:n, :]), split_heads(xdt[0:n, :]), heads(wl[0:n, :], n),
                                  ALU.mult).then_inc(xw_ready, 1)
                dve.wait_ge(cb_masked, e + 1)
                dve.tensor_tensor(L[0:n], L[0:n], cbm[0:n, 0:n].unsqueeze(1).to_broadcast([n, HPG, n]),
                                  ALU.mult).then_inc(attn, 1)
                if s == 0:
                    dve.wait_ge(ck_in[e % 2], 16 * (e // 2 + 1))
                    dve.tensor_copy(cm[:, 0:(NS - 1) * (C0 + 1) + 1:C0 + 1], x[:, 5, 0:NS]).then_inc(cm_ready, 1)
                    mask_b(NS * u)

            def mask_b(i):
                if i:
                    dve.wait_ge(ss_prod, i)
                dve.tensor_scalar(bm[:, :], bt[0:C0, :], ident[0:C0, i % NS:i % NS + 1], None,
                                  ALU.mult).then_inc(bm_ready, 1)

            def sample(u, b):
                i = NS * u + b
                st = ss[:, i % 2, :, :]
                dve.wait_ge(ss_turned, i + 1)
                dve.wait_ge(ss_in[i % 2], 16 * (i // 2 + 1))
                link(dve.tensor_tensor(st, st, tab["ecol"][:, 4 * u:4 * u + 4, b:b + 1].to_broadcast(
                    [P, 4, P]), ALU.mult))
                dve.wait_ge(ss_prod, i + 1)
                dve.tensor_tensor(st, st, Z[:, :].rearrange("p (a n) -> p a n", a=4),
                                  ALU.add).then_inc(ss_new, 1)
                if b + 1 < NS:
                    mask_b(i + 1)

            def scan(u, s):
                e, n = ev(u, s), step_cols(s)[1]
                hs = slice(HPG * u, HPG * u + HPG)
                if s == 0:
                    if u:
                        dve.wait_ge(s_turned, u)
                    dve.wait_ge(s_prod, e + 1)
                    dve.tensor_copy(S[:, :], SU[:, :]).then_inc(s_new, 1)
                else:
                    dve.wait_ge(inter, e + 1)
                    dve.wait_ge(el_done, e + 1)
                    kept_part = mark(dve.tensor_tensor(split_heads(S[:, :]), split_heads(S[:, :]),
                                                       heads(el[:, :], P), ALU.mult))
                dve.wait_ge(inter, e + 1)
                dve.wait_ge(el_done, e + 1)
                if e:
                    dve.wait_ge(y_turned, e)
                from_state = mark(dve.tensor_tensor(split_heads(y[0:n, :]), split_heads(Y2[0:n, :]),
                                                    heads(ea[0:n, :], n), ALU.mult))
                dve.wait_ge(s_prod, e + 1)
                if s:
                    dve.wait_ge(chain, kept_part)
                    dve.tensor_tensor(S[:, :], S[:, :], SU[:, :], ALU.add).then_inc(s_new, 1)
                skipped = mark(dve.tensor_tensor(split_heads(xw[0:n, :]), split_heads(X[0:n, :]),
                                                 heads(tab["dskip"][0:n, hs], n), ALU.mult))
                dve.wait_ge(intra, e + 1)
                dve.wait_ge(chain, from_state)
                link(dve.tensor_tensor(y[0:n, :], y[0:n, :], Y1[0:n, :], ALU.add))
                dve.wait_ge(chain, skipped)
                dve.tensor_tensor(y[0:n, :], y[0:n, :], xw[0:n, :], ALU.add).then_inc(y_summed, 1)

            def norm(u, s):
                e, n = ev(u, s), step_cols(s)[1]
                dve.wait_ge(z_turned, e + 1)
                dve.wait_ge(y_summed, e + 1)
                dve.tensor_tensor(y[0:n, :], y[0:n, :], Z[0:n, :], ALU.mult).then_inc(gated, 1)

            def turn(u, s):
                e, n = ev(u, s), step_cols(s)[1]
                dve.wait_ge(yt_hi, e + 1)
                dve.tensor_tensor(ytlo[:, :, 0:n], SU[:, 0:4 * n].rearrange("p (a c) -> p a c", a=4),
                                  ythi[:, :, 0:n].bitcast(F32), ALU.subtract).then_inc(yt_lo, 1)

            def products(u, s):
                e, n = ev(u, s), step_cols(s)[1]
                if e == 0:
                    dve.wait_ge(sizes.stored, 16)
                    dve.wait_ge(sizes.turned, 2)
                for half in range(2):
                    dve.wait_ge(out_done, 2 * e + half + 1)
                    dst = y_acc[0:n, s, 512 * half:512 * half + 512]
                    if u == 0:
                        dve.tensor_copy(dst, Y[half][0:n, :]).then_inc(added, 1)
                    else:
                        dve.tensor_tensor(dst, dst, Y[half][0:n, :], ALU.add).then_inc(added, 1)

            stages = {"drain": evac, "finish": finish, "inputs": inputs, "sample": sample, "scan": scan,
                      "norm": norm, "turn": turn, "products": products}
            for task in order:
                if task[0] == "sizes":
                    sizes.dve_sizes(dve)
                elif task[0] == "split":
                    W.low(dve, m, task[1], w_hi, w_lo)
                elif task[0] in stages:
                    stages[task[0]](*task[1:])
                elif task[0] == "residual_add":
                    res.add(dve, task[2])

        @block.tensor
        def _(pe):
            def piece(i, p):
                t, g = pieces[i]
                if g == 0 and p == 0:
                    pe.wait_ge(w_lo, W.index[("in", t)] + 1)
                if i >= 2 and p == 0:
                    pe.wait_ge(bank_free[i % 2], i // 2)
                if g == 3:
                    q = tile_index(t)
                    pe.wait_ge(cv_packed, q + 1)
                    pe.transpose(PR[i % 2][0:11, 0:P], cvp[:, q % 2, :], ident[:, :]).then_inc(piece_done, 1)
                else:
                    last = project_part(pe, m, t, g, p, PR[i % 2])
                    if p == PARTS - 1:
                        last.then_inc(piece_done, 1)

            def inputs(u, s):
                e, n = ev(u, s), step_cols(s)[1]
                x = tokens(u, s)
                pe.wait_ge(ck_in[e % 2], 16 * (e // 2 + 1))
                if e:
                    pe.wait_ge(y_summed, e)
                    pe.wait_ge(cb_masked, e)
                for j in range(4):
                    pe.transpose(X[0:n, j * P:(j + 1) * P], x[:, j, :], ident[:, :])
                pe.transpose(M[0:n, 0:P], x[:, 4, :], ident[:, :])
                pe.matmul(M[0:n, P:P + n], x[:, 4, :], x[:, 5, :], start=True, stop=True).then_inc(turned, 1)

            def banks_free(e):
                if e >= 2:
                    pe.wait_ge(added, 2 * (e - 1))
                if e:
                    pe.wait_ge(y_summed, e)
                    pe.wait_ge(s_new, e)
                    pe.wait_ge(yt_lo, e)

            def sample(u, b):
                n, i = C0, NS * u + b
                if b == 0:
                    banks_free(ev(u, 0))
                    pe.wait_ge(cm_ready, u + 1)
                    pe.wait_ge(xdt_ready, ev(u, 0) + 1)
                    if u:
                        pe.wait_ge(s_kept, u)
                pe.wait_ge(ss_in[i % 2], 16 * (i // 2 + 1))
                if b:
                    pe.wait_ge(ss_copied, i)
                for j in range(4):
                    last = pe.transpose(SU[:, j * P:(j + 1) * P], ss[:, i % 2, j, :], ident[:, :])
                last.then_inc(ss_turned, 1)
                pe.wait_ge(bm_ready, i + 1)
                if b:
                    pe.wait_ge(ss_new, i)
                for j in range(4):
                    last = pe.matmul(Z[:, j * P:(j + 1) * P], xdt[0:n, j * P:(j + 1) * P],
                                     bm[:, :], start=True, stop=True)
                last.then_inc(ss_prod, 1)
                pe.wait_ge(ss_copied, i + 1)
                pe.matmul(Y2[0:n, :], cm[:, b * C0:(b + 1) * C0], y[:, :], start=(b == 0),
                          stop=(b == NS - 1)).then_inc(inter if b == NS - 1 else ss_inter, 1)

            def scan(u, s):
                e, n = ev(u, s), step_cols(s)[1]
                x, G = tokens(u, s), decay(u, s)
                if s:
                    banks_free(e)
                    pe.matmul(Y2[0:n, :], x[:, 5, :], S[:, :], start=True, stop=True).then_inc(inter, 1)
                pe.wait_ge(xw_ready, e + 1)
                pe.wait_ge(b_turned, e + 1)
                pe.matmul(SU[:, :], bt[0:n, :], xw[0:n, :], start=True, stop=True).then_inc(s_prod, 1)
                pe.wait_ge(attn, e + 1)
                for r in range(HPG):
                    last = pe.matmul(Y1[0:n, r * HD:(r + 1) * HD], G[0:n, r, :],
                                     xdt[0:n, r * HD:(r + 1) * HD], start=True, stop=True)
                last.then_inc(intra, 1)

            def gates(u, s):
                e, n = ev(u, s), step_cols(s)[1]
                pe.wait_ge(z_in, 16 * (e + 1))
                if e:
                    pe.wait_ge(gated, e)
                if s == 0:
                    pe.wait_ge(ss_new, NS * (u + 1))
                for j in range(4):
                    last = pe.transpose(Z[0:n, j * P:(j + 1) * P], zc[:, j, 0:n], ident[:, :])
                last.then_inc(z_turned, 1)

            def turn(u, s):
                e, n = ev(u, s), step_cols(s)[1]
                pe.wait_ge(y_normed, e + 1)
                pe.wait_ge(s_new, e + 1)
                for j in range(4):
                    last = pe.transpose(SU[:, j * n:(j + 1) * n], y[0:n, j * P:(j + 1) * P], ident[0:n, 0:n])
                last.then_inc(y_turned, 1)

            def products(u, s):
                e = ev(u, s)
                pe.wait_ge(yt_lo, e + 1)
                pe.wait_ge(y_summed, min(e + 2, U * STEPS))
                pe.wait_ge(w_lo, W.index[("out", u * WT + WT - 1)] + 1)
                for half in range(2):
                    out_products(pe, m, (ythi, ytlo), WT, half, Y[half]).then_inc(out_done, 1)

            def keep(u):
                pe.wait_ge(s_new, STEPS * (u + 1))
                pe.wait_ge(gated, STEPS * (u + 1))
                for j in range(4):
                    last = pe.transpose(Z[:, j * P:(j + 1) * P], S[:, j * P:(j + 1) * P], ident[:, :])
                last.then_inc(s_turned, 1)

            stages = {"piece": piece, "size_turn": lambda: sizes.turn_sizes(pe), "inputs": inputs, "sample": sample, "scan": scan, "gates": gates,
                      "turn": turn, "products": products, "keep": keep}
            sizes.narrow.project(pe)
            sizes.turn_conv(pe)
            for task in order:
                if task[0] in stages:
                    stages[task[0]](*task[1:])


_INS = ["x_prompt", "x_sample", "state_gla", "state_ssm", "state_conv", "meta_tokens", "pre_norm",
        "post_norm", "gla_w_in", "gla_w_gate_up", "gla_b_gate", "gla_w_norm", "gla_w_out", "ssd_w_in",
        "ssd_conv_w", "ssd_conv_b", "ssd_dt_bias", "ssd_a_log", "ssd_d_skip", "ssd_w_norm", "ssd_w_out"]
_OUTS = [(1, SEQ, D), (NS, 1, D), (1, 1, U, HK, HV), (1, 1, SH, HD, P), (1, 1, 3, CONV),
         (1, NS, U, HK, HV), (1, NS, SH, HD, P), (1, NS, 3, CONV)]


def kernel(**inputs):
    import numpy as _np
    import concourse.bacc as _bacc
    from concourse import mybir as _mybir
    from concourse.bass_utils import run_bass_kernel_spmd as _run

    nc = _bacc.Bacc("TRN2", target_bir_lowering=False, num_devices=1)
    arrays, args = {}, []
    for name in _INS:
        a = _np.ascontiguousarray(inputs[name])
        arrays[f"in_{name}_dram"] = a
        args.append(nc.dram_tensor(f"in_{name}_dram", a.shape, _mybir.dt.from_np(a.dtype), kind="ExternalInput").ap())
    for i, shape in enumerate(_OUTS):
        args.append(nc.dram_tensor(f"out_{i}_dram", shape, _mybir.dt.float32, kind="ExternalOutput").ap())
    hybrid_kernel(nc, *args)
    r = _run(nc, [arrays], core_ids=[0])
    return tuple(r.results[0][f"out_{i}_dram"] for i in range(len(_OUTS)))
```
